# Optimizing a Trainium2 kernel written in Bass

```python
import jax, jax.numpy as jnp
from jax import lax
import numpy as np

D_MODEL = 1024
BATCH = 1
SEQ = 1024
DEPTH = 2

BRANCH_WIDTH = 512
N_BRANCHES = 3
NORM_EPS = 1e-6
RWKV_HEADS = 8
RWKV_HEAD_DIM = 64
RWKV_WIDTH = RWKV_HEADS * RWKV_HEAD_DIM
RWKV_DECAY_LORA = 64
RWKV_AAA_LORA = 64
RWKV_VRES_LORA = 32
RWKV_GN_EPS = 64e-5
RWKV_SHIFT_SIZES = (RWKV_WIDTH, RWKV_WIDTH, RWKV_WIDTH, RWKV_DECAY_LORA, RWKV_AAA_LORA)
RWKV_SHIFT_COLS = 3 * RWKV_WIDTH + RWKV_DECAY_LORA + RWKV_AAA_LORA
GMLP_WIDTH = 512
GMLP_GROUPS = 8
GMLP_GROUP_DIM = GMLP_WIDTH // GMLP_GROUPS
GMLP_CHUNK = 128
GMLP_LN_EPS = 1e-5
MLA_HEADS = 8
MLA_Q_LORA = 384
MLA_KV_LORA = 256
MLA_NOPE = 64
MLA_ROPE = 32
MLA_V = 64
MLA_WIDTH = MLA_HEADS * MLA_V
ROPE_THETA = 10000.0
ATTN_BLOCK = 128
IN_SEG_SIZES = (RWKV_SHIFT_COLS, RWKV_WIDTH,
                GMLP_WIDTH, GMLP_WIDTH, GMLP_WIDTH,
                MLA_Q_LORA, MLA_KV_LORA, MLA_ROPE, MLA_WIDTH,
                N_BRANCHES * D_MODEL)
IN_COLS = sum(IN_SEG_SIZES)

kernel_name = 'hybrid_rwkv7_gmlp_mla_gated_block'

def _offsets(sizes):
    return [int(o) for o in np.cumsum(sizes)[:-1]]

def _rmsnorm(x, gain):
    x32 = x.astype(jnp.float32)
    y = x32 * lax.rsqrt(jnp.mean(x32 * x32, axis=-1, keepdims=True) + NORM_EPS)
    return (y * gain.astype(jnp.float32)).astype(x.dtype)

def _layernorm(x, w, b, eps):
    x32 = x.astype(jnp.float32)
    mu = jnp.mean(x32, axis=-1, keepdims=True)
    xc = x32 - mu
    var = jnp.mean(xc * xc, axis=-1, keepdims=True)
    return (xc * lax.rsqrt(var + eps) * w.astype(jnp.float32) + b.astype(jnp.float32)).astype(x.dtype)

def _wkv7_step(state, inp):
    r, w, k, v, a, b = inp
    sa = jnp.einsum('bhij,bhj->bhi', state, a)
    state = state * w[:, :, None, :] + sa[..., None] * b[:, :, None, :] + v[..., None] * k[:, :, None, :]
    y = jnp.einsum('bhij,bhj->bhi', state, r)
    return state, y

def _rwkv7_mix(p, v_first, vres_gate, mu, w0, w_up, a0, a_up, k_k, k_a, r_k, ln_w, ln_b):
    B, T, _ = p.shape
    dt = p.dtype
    f32 = jnp.float32
    prev = jnp.pad(p, ((0, 0), (1, 0), (0, 0)))[:, :-1]
    p = p + (prev - p) * mu
    r, k, v, w_dn, a_dn = jnp.split(p, _offsets(RWKV_SHIFT_SIZES), axis=-1)
    w_log = -jax.nn.softplus(-(w0 + jnp.tanh(w_dn) @ w_up).astype(f32)) - 0.5
    decay = jnp.exp(-jnp.exp(w_log))
    a = jax.nn.sigmoid((a0 + a_dn @ a_up).astype(f32))
    if vres_gate is not None:
        v = v + (v_first - v) * vres_gate
    v_out = v.astype(dt)
    hs = (B, T, RWKV_HEADS, RWKV_HEAD_DIM)
    kk = (k * k_k).astype(f32).reshape(hs)
    kk = kk / jnp.maximum(jnp.sqrt(jnp.sum(kk * kk, axis=-1, keepdims=True)), 1e-12)
    k = (k.astype(f32) * (1.0 + (a - 1.0) * k_a.astype(f32))).reshape(hs)
    r = r.astype(f32).reshape(hs)
    v = v.astype(f32).reshape(hs)
    decay = decay.reshape(hs)
    a = a.reshape(hs)
    tm = lambda t: jnp.swapaxes(t, 0, 1)
    state0 = jnp.zeros((B, RWKV_HEADS, RWKV_HEAD_DIM, RWKV_HEAD_DIM), f32)
    _, y = lax.scan(_wkv7_step, state0, (tm(r), tm(decay), tm(k), tm(v), tm(-kk), tm(kk * a)))
    y = tm(y)
    y = _layernorm(y, ln_w.reshape(RWKV_HEADS, RWKV_HEAD_DIM), ln_b.reshape(RWKV_HEADS, RWKV_HEAD_DIM), RWKV_GN_EPS)
    y = y + jnp.sum(r * k * r_k.astype(f32), axis=-1, keepdims=True) * v
    return y.reshape(B, T, RWKV_WIDTH).astype(dt), v_out

def _gmlp_mix(u, v, ln_w, ln_b, w_s, b_s):
    B, T, _ = u.shape
    u = jax.nn.gelu(u, approximate=False)
    v = _layernorm(jax.nn.gelu(v, approximate=False), ln_w, ln_b, GMLP_LN_EPS)
    vc = v.reshape(B, T // GMLP_CHUNK, GMLP_CHUNK, GMLP_GROUPS, GMLP_GROUP_DIM)
    causal = jnp.tril(jnp.ones((GMLP_CHUNK, GMLP_CHUNK), dtype=bool))
    w = jnp.where(causal[None], w_s, jnp.zeros((), w_s.dtype))
    vm = jnp.einsum('gts,bnsgc->bntgc', w, vc) + b_s.T[:, :, None]
    return u * vm.reshape(B, T, GMLP_WIDTH)

def _apply_rope(x, cos, sin):
    half = x.shape[-1] // 2
    x1 = x[..., :half].astype(jnp.float32)
    x2 = x[..., half:].astype(jnp.float32)
    return jnp.concatenate([x1 * cos - x2 * sin, x2 * cos + x1 * sin], axis=-1).astype(x.dtype)

def _mla_mix(c_q, c_kv, k_rope, positions, q_norm, w_uq, kv_norm, w_ukv):
    B, T, _ = c_q.shape
    q = (_rmsnorm(c_q, q_norm) @ w_uq).reshape(B, T, MLA_HEADS, MLA_NOPE + MLA_ROPE)
    kv = (_rmsnorm(c_kv, kv_norm) @ w_ukv).reshape(B, T, MLA_HEADS, MLA_NOPE + MLA_V)
    q_nope, q_rope = q[..., :MLA_NOPE], q[..., MLA_NOPE:]
    k_nope, v = kv[..., :MLA_NOPE], kv[..., MLA_NOPE:]
    inv_freq = 1.0 / (ROPE_THETA ** (jnp.arange(0, MLA_ROPE, 2, dtype=jnp.float32) / MLA_ROPE))
    ang = positions.astype(jnp.float32)[..., None] * inv_freq
    cos, sin = jnp.cos(ang), jnp.sin(ang)
    q_rope = _apply_rope(q_rope, cos[:, :, None, :], sin[:, :, None, :])
    k_rope = _apply_rope(k_rope, cos, sin)
    q = jnp.concatenate([q_nope, q_rope], axis=-1)
    k = jnp.concatenate([k_nope, jnp.broadcast_to(k_rope[:, :, None, :], (B, T, MLA_HEADS, MLA_ROPE))], axis=-1)
    scale = (MLA_NOPE + MLA_ROPE) ** -0.5
    outs = []
    for i in range(T // ATTN_BLOCK):
        q0, q1 = i * ATTN_BLOCK, (i + 1) * ATTN_BLOCK
        s = jnp.einsum('bqhd,bkhd->bhqk', q[:, q0:q1], k[:, :q1]).astype(jnp.float32) * scale
        causal = jnp.arange(q1)[None, :] <= jnp.arange(q0, q1)[:, None]
        s = jnp.where(causal, s, -jnp.inf)
        pr = jax.nn.softmax(s, axis=-1).astype(v.dtype)
        outs.append(jnp.einsum('bhqk,bkhd->bqhd', pr, v[:, :q1]))
    return jnp.concatenate(outs, axis=1).reshape(B, T, MLA_WIDTH)

def setup_inputs(seed: int = 0) -> dict:
    key = jax.random.key(seed)
    ks = jax.random.split(key, 28)
    nrm = lambda k, shape, s: jax.random.normal(k, shape, jnp.float32) * s
    L, Lv = DEPTH, max(DEPTH - 1, 0)
    offs = jax.random.randint(ks[1], (BATCH, 1), 0, 4096)
    return {
        'x': nrm(ks[0], (BATCH, SEQ, D_MODEL), 1.0),
        'positions': (offs + jnp.arange(SEQ)[None, :]).astype(jnp.int32),
        'w_in': nrm(ks[2], (L, D_MODEL, IN_COLS), D_MODEL ** -0.5),
        'pre_norm': 1.0 + nrm(ks[3], (L, D_MODEL), 0.1),
        'post_norm': 1.0 + nrm(ks[4], (L, D_MODEL), 0.1),
        'rwkv_mu': jax.random.uniform(ks[5], (L, RWKV_SHIFT_COLS), jnp.float32),
        'rwkv_w0': -2.0 + nrm(ks[6], (L, RWKV_WIDTH), 0.5),
        'rwkv_w_up': nrm(ks[7], (L, RWKV_DECAY_LORA, RWKV_WIDTH), RWKV_DECAY_LORA ** -0.5),
        'rwkv_a0': nrm(ks[8], (L, RWKV_WIDTH), 0.5),
        'rwkv_a_up': nrm(ks[9], (L, RWKV_AAA_LORA, RWKV_WIDTH), RWKV_AAA_LORA ** -0.5),
        'rwkv_k_k': 0.85 + nrm(ks[10], (L, RWKV_WIDTH), 0.1),
        'rwkv_k_a': 1.0 + nrm(ks[11], (L, RWKV_WIDTH), 0.1),
        'rwkv_r_k': nrm(ks[12], (L, RWKV_HEADS, RWKV_HEAD_DIM), 0.1),
        'rwkv_ln_w': 1.0 + nrm(ks[13], (L, RWKV_WIDTH), 0.1),
        'rwkv_ln_b': nrm(ks[14], (L, RWKV_WIDTH), 0.02),
        'rwkv_v0': nrm(ks[15], (Lv, RWKV_WIDTH), 0.5),
        'rwkv_v_down': nrm(ks[16], (Lv, D_MODEL, RWKV_VRES_LORA), D_MODEL ** -0.5),
        'rwkv_v_up': nrm(ks[17], (Lv, RWKV_VRES_LORA, RWKV_WIDTH), RWKV_VRES_LORA ** -0.5),
        'gmlp_ln_w': 1.0 + nrm(ks[18], (L, GMLP_WIDTH), 0.1),
        'gmlp_ln_b': nrm(ks[19], (L, GMLP_WIDTH), 0.02),
        'gmlp_w_s': nrm(ks[20], (L, GMLP_GROUPS, GMLP_CHUNK, GMLP_CHUNK), GMLP_CHUNK ** -0.5),
        'gmlp_b_s': 1.0 + nrm(ks[21], (L, GMLP_GROUPS, GMLP_CHUNK), 0.1),
        'mla_q_norm': 1.0 + nrm(ks[22], (L, MLA_Q_LORA), 0.1),
        'mla_w_uq': nrm(ks[23], (L, MLA_Q_LORA, MLA_HEADS * (MLA_NOPE + MLA_ROPE)), MLA_Q_LORA ** -0.5),
        'mla_kv_norm': 1.0 + nrm(ks[24], (L, MLA_KV_LORA), 0.1),
        'mla_w_ukv': nrm(ks[25], (L, MLA_KV_LORA, MLA_HEADS * (MLA_NOPE + MLA_V)), MLA_KV_LORA ** -0.5),
        'w_branch': nrm(ks[26], (L, N_BRANCHES, BRANCH_WIDTH, D_MODEL), BRANCH_WIDTH ** -0.5),
        'w_out': nrm(ks[27], (L, D_MODEL, D_MODEL), D_MODEL ** -0.5),
    }

def reference(x, positions, w_in, pre_norm, post_norm, rwkv_mu, rwkv_w0, rwkv_w_up, rwkv_a0, rwkv_a_up,
              rwkv_k_k, rwkv_k_a, rwkv_r_k, rwkv_ln_w, rwkv_ln_b, rwkv_v0, rwkv_v_down, rwkv_v_up,
              gmlp_ln_w, gmlp_ln_b, gmlp_w_s, gmlp_b_s, mla_q_norm, mla_w_uq, mla_kv_norm, mla_w_ukv,
              w_branch, w_out):
    B, T, D = x.shape
    v_first = None
    for l in range(DEPTH):
        h = _rmsnorm(x, pre_norm[l])
        p = h @ w_in[l]
        (rw_in, rw_gate, g_u, g_v, g_gate, c_q, c_kv, k_rope, mla_gate, merge) = jnp.split(
            p, _offsets(IN_SEG_SIZES), axis=-1)
        vres_gate = None
        if l > 0:
            vres_gate = jax.nn.sigmoid((rwkv_v0[l - 1] + (h @ rwkv_v_down[l - 1]) @ rwkv_v_up[l - 1]).astype(jnp.float32))
        y_a, v_l = _rwkv7_mix(rw_in, v_first, vres_gate, rwkv_mu[l], rwkv_w0[l], rwkv_w_up[l], rwkv_a0[l],
                              rwkv_a_up[l], rwkv_k_k[l], rwkv_k_a[l], rwkv_r_k[l], rwkv_ln_w[l], rwkv_ln_b[l])
        if l == 0:
            v_first = v_l
        y_b = _gmlp_mix(g_u, g_v, gmlp_ln_w[l], gmlp_ln_b[l], gmlp_w_s[l], gmlp_b_s[l])
        y_c = _mla_mix(c_q, c_kv, k_rope, positions, mla_q_norm[l], mla_w_uq[l], mla_kv_norm[l], mla_w_ukv[l])
        branches = jnp.stack([y_a * jax.nn.silu(rw_gate),
                              y_b * jax.nn.silu(g_gate),
                              y_c * jax.nn.silu(mla_gate)], axis=2)
        proj = jnp.einsum('btnk,nkd->btnd', branches, w_branch[l])
        gates = jax.nn.sigmoid(merge.reshape(B, T, N_BRANCHES, D))
        mixed = jnp.sum(gates * proj, axis=2) @ w_out[l]
        x = x + _rmsnorm(mixed, post_norm[l])
    return x


_drawn_inputs = setup_inputs


def setup_inputs(seed=0):
    import zlib

    import numpy as np

    out = dict(_drawn_inputs(seed))
    spreads = {}
    factors = {'rwkv_ln_b': 3.26, 'gmlp_ln_b': 7.436, 'mla_q_norm': 5.311, 'mla_kv_norm': 3.143}
    for name, (base, spread) in spreads.items():
        noise = np.random.default_rng([zlib.crc32(name.encode()), seed]).standard_normal(out[name].shape)
        drawn = base * np.exp(spread * noise) if base else spread * noise
        out[name] = __import__('jax').numpy.asarray(drawn.astype(out[name].dtype))
    for name, factor in factors.items():
        out[name] = (out[name] * factor).astype(out[name].dtype)
    return out
```

```python
import math
from contextlib import ExitStack

import numpy as np

import concourse.bass as bass
from concourse import mybir

F32 = mybir.dt.float32
I32 = mybir.dt.int32
ACT = mybir.ActivationFunctionType
ALU = mybir.AluOpType
AX = mybir.AxisListType

P = 128
D = 1024
KD = D // P
T = 1024
HALF = 512
L = 2
BW = 512
NBR = 3
CH = 128
NC = T // CH
HD = 64
NH = 8
NP = NH // 2
W_LORA, A_LORA, V_LORA = 64, 64, 32
NOPE, ROPE = 64, 32
QK = NOPE + ROPE
Q_LORA, KV_LORA = 384, 256
NORM_EPS, GN_EPS, LN_EPS = 1e-6, 64e-5, 1e-5
DECAY = math.exp(-0.5)
KK_SHIFT = 16
SCALE = QK ** -0.5
MASKED = -1e30

SIZES = (3 * BW + W_LORA + A_LORA, BW, BW, BW, BW, Q_LORA, KV_LORA, ROPE, BW, NBR * D)
OFF = [0] + [int(o) for o in np.cumsum(SIZES)]
(O_RW, O_RWG, O_GU, O_GV, O_GG, O_CQ, O_CKV, O_KR, O_MG, O_MERGE) = OFF[:10]

N_RW = 14
T_GU = N_RW
T_LAT = T_GU + 4
N_LAT = 6
T_GATE = T_LAT + N_LAT
N_GATE = 12
N_WT = T_GATE + N_GATE

PAR = {}
_at = 0
for _name, _n in (("pre", 8), ("post", 8), ("mu", N_RW), ("w0", 4), ("a0", 4), ("k_k", 4), ("k_a", 4),
                  ("r_k", 4), ("ln_w", 4), ("ln_b", 4), ("v0", 4), ("q_norm", 3), ("kv_norm", 2), ("flag", 1)):
    PAR[_name] = _at
    _at += _n
N_PAR = _at

CON = {}
_at = 0
for _name, _n in (("ident", P), ("blocks", P), ("amask", 4 * P), ("unit", P), ("level", 6 * HD),
                  ("causal", P), ("restart", NC * (CH + 1)), ("freq", 1)):
    CON[_name] = (_at, _n)
    _at += _n
N_CON = _at


class Core:
    pass


def bc(ap, *shape):
    return ap.to_broadcast(list(shape))


def norm_phase(nc, g, l):
    with ExitStack() as ctx:
        x = ctx.enter_context(nc.sbuf_tensor("x_in", [P, KD, T], F32))
        sq = ctx.enter_context(nc.sbuf_tensor("x_sq", [P, 2, T], F32))
        acc = ctx.enter_context(nc.sbuf_tensor("x_acc", [P, T], F32))
        rstd = ctx.enter_context(nc.sbuf_tensor("x_rstd", [P, T], F32))
        lg = ctx.enter_context(nc.sbuf_tensor("x_lg", [P, T], F32))
        ps = g.ps
        par_loaded, squared, added, summed, rooted, lg_done = g.sems("par_loaded squared added summed rooted lg_done")
        x_loaded = [g.sem(f"x_loaded{q}") for q in range(4)]
        g.start()
        block = ctx.enter_context(nc.Block())

        @block.sync
        def _(sp):
            sp.dma_start(g.par[:, :], g.d_par[bass.ds(l, 1)].rearrange("o p n -> p (o n)")).then_inc(par_loaded, 16)
            for q in range(4):
                sp.dma_start(x[:, 2 * q:2 * q + 2, :], g.d_out[:, 2 * q:2 * q + 2, :]).then_inc(x_loaded[q], 16)

        @block.scalar
        def _(act):
            for k in range(KD):
                act.wait_ge(x_loaded[k // 2], 16)
                if k >= 2:
                    act.wait_ge(added, k - 1)
                nc.scalar.activation(sq[:, k % 2, :], x[:, k, :], ACT.Square).then_inc(squared, 1)
            act.wait_ge(summed, 1)
            for b in range(2):
                cols = slice(b * HALF, (b + 1) * HALF)
                nc.scalar.activation(lg[:, cols], ps[:, b, :], ACT.Ln, scale=1.0 / D, bias=g.eps(NORM_EPS)).then_inc(lg_done, 1)
            act.wait_ge(lg_done, 2)
            nc.scalar.activation(rstd[:, :], lg[:, :], ACT.Exp, scale=-0.5).then_inc(rooted, 1)

        @block.vector
        def _(dve):
            dve.wait_ge(squared, 1)
            nc.vector.tensor_copy(acc[:, :], sq[:, 0, :]).then_inc(added, 1)
            for k in range(1, KD):
                dve.wait_ge(squared, k + 1)
                dve.wait_ge(added, k)
                nc.vector.tensor_tensor(acc[:, :], acc[:, :], sq[:, k % 2, :], ALU.add).then_inc(added, 1)
            dve.wait_ge(par_loaded, 16)
            dve.wait_ge(rooted, 1)
            for k in range(KD):
                nc.vector.scalar_tensor_tensor(g.h[:, k, :], x[:, k, :], g.pcol("pre", k), rstd[:, :], ALU.mult, ALU.mult)

        @block.tensor
        def _(pe):
            pe.wait_ge(added, KD)
            for b in range(2):
                mm = nc.tensor.matmul(ps[:, b, :], g.ones[:, :], acc[:, b * HALF:(b + 1) * HALF], start=True, stop=True)
            mm.then_inc(summed, 1)


def load_tiles(sp, g, l, first, n, slots, w_loaded, done):
    def load(i, u):
        sp.dma_start(slots[:, u], g.d_wt[bass.ds(l * N_WT + first + 2 * i + u, 1)].rearrange("o p k m -> p (o k) m"))\
            .then_inc(w_loaded[u], 16)

    load(0, 0)
    load(0, 1)
    with sp.Fori(1, n // 2) as i:
        for u in range(2):
            sp.wait_ge(done[u], i)
            load(i, u)


def project(nc, g, pe, slots, rhs, banks, w_loaded, free, done, n):
    with pe.Fori(0, n // 2) as i:
        for u in range(2):
            pe.wait_ge(w_loaded[u], i * 16 + 16)
            pe.wait_ge(free[u], i + 1)
            for k in range(KD):
                for b in range(2):
                    mm = nc.tensor.matmul(g.ps[:, banks[u] + b, :], slots[:, u, k, :],
                                          rhs[:, k, b * HALF:(b + 1) * HALF], start=k == 0, stop=k == KD - 1)
            mm.then_inc(done[u], 1)


def rwkv_project_phase(nc, g, l, mix):
    with ExitStack() as ctx:
        slots = ctx.enter_context(nc.sbuf_tensor("w_slots", [P, 2, KD, P], F32))
        raw = ctx.enter_context(nc.sbuf_tensor("raw", [P, 2, T + 1], F32))
        diff = ctx.enter_context(nc.sbuf_tensor("diff", [P, 2, T], F32))
        w_loaded, free, done, raw_ready, raw_free, diffed = (
            [g.sem(f"rp_{name}{u}") for u in range(2)] for name in ("w_loaded", "free", "done", "raw", "raw_free", "diff"))
        zeroed = g.sem("rp_zeroed")
        g.start()
        block = ctx.enter_context(nc.Block())

        @block.sync
        def _(sp):
            load_tiles(sp, g, l, 0, N_RW, slots, w_loaded, done)

        @block.tensor
        def _(pe):
            project(nc, g, pe, slots, g.h, (0, 2), w_loaded, free, done, N_RW)

        @block.scalar
        def _(act):
            for u in range(2):
                act.sem_inc(free[u], 1)
            with act.Fori(0, N_RW // 2) as i:
                for u in range(2):
                    act.wait_ge(done[u], i + 1)
                    act.wait_ge(raw_free[u], i + 1)
                    nc.scalar.activation(raw[:, u, 1:T + 1], g.ps[:, 2 * u:2 * u + 2, :].rearrange("p b n -> p (b n)"),
                                         ACT.Copy).then_inc(free[u], 1)

        @block.vector
        def _(dve):
            nc.vector.memset(raw[:, :, 0:1], 0.0).then_inc(zeroed, 1)
            dve.wait_ge(zeroed, 1)
            for u in range(2):
                dve.sem_inc(raw_free[u], 1)
            with dve.Fori(0, N_RW // 2) as i:
                for u in range(2):
                    dve.wait_ge(free[u], i + 2)
                    nc.vector.tensor_tensor(diff[:, u, :], raw[:, u, 0:T], raw[:, u, 1:T + 1], ALU.subtract).then_inc(diffed[u], 1)
                    dve.wait_ge(diffed[u], i + 1)
                    nc.vector.scalar_tensor_tensor(mix[:, bass.ds(i * 2 + u, 1), :].rearrange("p o t -> p (o t)"),
                                                   diff[:, u, :], g.par[:, bass.ds(i * 2 + (u + PAR["mu"]), 1)],
                                                   raw[:, u, 1:T + 1], ALU.mult, ALU.add).then_inc(raw_free[u], 1)


def rwkv_prepare_phase(nc, g, l, mix, ar, decay):
    with ExitStack() as ctx:
        def sb(name, *shape):
            return ctx.enter_context(nc.sbuf_tensor(name, [P, *shape], F32))

        up = sb("up", 3, P)
        sg, csum, em = (sb(n, NC, CH + 1) for n in ("sg", "csum", "em"))
        cm, ep = sg, csum
        a, vg, kk, sq, fk, rk = (sb(n, T) for n in ("a_gate", "v_gate", "kk", "kk_sq", "fk", "rk"))
        rn = sq
        ps = g.ps
        names = ("up_loaded", "tanhed", "z_ready", "sg_done", "csum_done", "cm_done", "e_done", "a_done", "vg_done", "vdiff",
                 "vgated", "v_done", "kk_raw", "sq_done", "kk_sum", "kk_max", "rn_ln", "rn_done", "kk_done", "f_done",
                 "k_done", "rk_done", "rk_sum", "step_done", "zeroed", "b_done", "ar_done")
        s = dict(zip(names, g.sems(" ".join("pp_" + n for n in names))))
        g.start()
        block = ctx.enter_context(nc.Block())

        def row(t, j):
            return t[:, bass.ds(j, 1), :].rearrange("p o t -> p (o t)")

        def chunks(ap):
            return ap.rearrange("p (c t) -> p c t", c=NC)

        @block.sync
        def _(sp):
            with sp.Fori(0, NP) as j:
                sp.wait_ge(s["step_done"], j + 1)
                sp.dma_start(up[:, :, :], g.d_up[bass.ds(l * NP + j, 1)].rearrange("o p a m -> p (o a) m")).then_inc(s["up_loaded"], 16)

        @block.tensor
        def _(pe):
            pe.wait_ge(s["tanhed"], 1)
            with pe.Fori(0, NP) as j:
                pe.wait_ge(s["up_loaded"], j * 16 + 16)
                for b in range(2):
                    cols = slice(b * HALF, (b + 1) * HALF)
                    nc.tensor.matmul(ps[:, b, :], up[0:64, 0, :], mix[0:64, 12, cols], start=True, stop=True)
                    nc.tensor.matmul(ps[:, 2 + b, :], up[64:128, 1, :], mix[64:128, 12, cols], start=True, stop=True)
                    mm = nc.tensor.matmul(ps[:, 4 + b, :], up[0:V_LORA, 2, :], mix[0:V_LORA, 13, cols], start=True, stop=True)
                mm.then_inc(s["z_ready"], 1)
                pe.wait_ge(s["sq_done"], j + 1)
                for b in range(2):
                    mm = nc.tensor.matmul(ps[:, 6 + b, :], g.con("blocks"), sq[:, b * HALF:(b + 1) * HALF], start=True, stop=True)
                mm.then_inc(s["kk_sum"], 1)
                pe.wait_ge(s["rk_done"], j + 1)
                for b in range(2):
                    mm = nc.tensor.matmul(ps[:, b, :], g.con("blocks"), rk[:, b * HALF:(b + 1) * HALF], start=True, stop=True)
                mm.then_inc(s["rk_sum"], 1)

        def two(b0):
            return ps[:, b0:b0 + 2, :].rearrange("p b n -> p (b n)")

        @block.scalar
        def _(act):
            nc.scalar.activation(mix[0:W_LORA, 12, :], mix[0:W_LORA, 12, :], ACT.Tanh).then_inc(s["tanhed"], 1)
            with act.Fori(0, NP) as j:
                act.wait_ge(s["step_done"], j + 1)
                nc.scalar.activation(sq[:, :], row(mix, j + 4), ACT.Square, scale=g.par[:, bass.ds(j + PAR["k_k"], 1)])\
                    .then_inc(s["sq_done"], 1)
                act.wait_ge(s["z_ready"], j + 1)
                nc.scalar.activation(sg[:, :, 1:CH + 1], chunks(two(0)), ACT.Sigmoid, bias=g.par[:, bass.ds(j + PAR["w0"], 1)])\
                    .then_inc(s["sg_done"], 1)
                nc.scalar.activation(a[:, :], two(2), ACT.Sigmoid, bias=g.par[:, bass.ds(j + PAR["a0"], 1)]).then_inc(s["a_done"], 1)
                nc.scalar.activation(vg[:, :], two(4), ACT.Sigmoid, bias=g.par[:, bass.ds(j + PAR["v0"], 1)]).then_inc(s["vg_done"], 1)
                act.wait_ge(s["kk_max"], j + 1)
                nc.scalar.activation(rn[:, :], fk[:, :], ACT.Ln, scale=float(2 ** KK_SHIFT)).then_inc(s["rn_ln"], 1)
                act.wait_ge(s["rn_ln"], j + 1)
                nc.scalar.activation(rn[:, :], rn[:, :], ACT.Exp, scale=-0.5, bias=g.eps(0.5 * KK_SHIFT * math.log(2.0)))\
                    .then_inc(s["rn_done"], 1)
                act.wait_ge(s["cm_done"], j + 1)
                nc.scalar.activation(ep[:, :, :], cm[:, :, :], ACT.Exp, scale=-DECAY).then_inc(s["e_done"], 1)
                nc.scalar.activation(em[:, :, :], cm[:, :, :], ACT.Exp, scale=DECAY).then_inc(s["e_done"], 1)

        @block.gpsimd
        def _(pool):
            with pool.Fori(0, NP) as j:
                pool.wait_ge(s["step_done"], j + 1)
                nc.gpsimd.tensor_tensor(rk[:, :], row(g.v, j), row(mix, j + 8), ALU.subtract).then_inc(s["vdiff"], 1)
                pool.wait_ge(s["vdiff"], j + 1)
                pool.wait_ge(s["vg_done"], j + 1)
                nc.gpsimd.tensor_tensor(vg[:, :], rk[:, :], vg[:, :], ALU.mult).then_inc(s["vgated"], 1)

        @block.vector
        def _(dve):
            dve.sem_inc(s["step_done"], 1)
            with dve.Fori(0, NP) as j:
                nc.vector.memset(sg[:, :, 0:1], 0.0).then_inc(s["zeroed"], 1)
                nc.vector.tensor_scalar(kk[:, :], row(mix, j + 4), g.par[:, bass.ds(j + PAR["k_k"], 1)], None, ALU.mult).then_inc(s["kk_raw"], 1)
                dve.wait_ge(s["kk_sum"], j + 1)
                nc.vector.tensor_scalar(fk[:, :], two(6), 1e-24, None, ALU.max).then_inc(s["kk_max"], 1)
                dve.wait_ge(s["sg_done"], j + 1)
                dve.wait_ge(s["zeroed"], j + 1)
                nc.vector.tensor_tensor_scan(csum[:, :, :].rearrange("p c t -> p (c t)"), g.con("restart"),
                                             sg[:, :, :].rearrange("p c t -> p (c t)"), 0.0, ALU.mult, ALU.add)\
                    .then_inc(s["csum_done"], 1)
                dve.wait_ge(s["csum_done"], j + 1)
                nc.vector.tensor_tensor(cm[:, :, :], csum[:, :, :], bc(csum[:, :, CH // 2:CH // 2 + 1], P, NC, CH + 1), ALU.subtract)\
                    .then_inc(s["cm_done"], 1)
                dve.wait_ge(s["vgated"], j + 1)
                nc.vector.scalar_tensor_tensor(row(g.v, j), vg[:, :], g.pcol("flag", 0), row(mix, j + 8), ALU.mult, ALU.add)\
                    .then_inc(s["v_done"], 1)
                dve.wait_ge(s["a_done"], j + 1)
                dve.wait_ge(s["rn_ln"], j + 1)
                nc.vector.tensor_scalar(fk[:, :], a[:, :], 1.0, g.par[:, bass.ds(j + PAR["k_a"], 1)], ALU.subtract, ALU.mult)\
                    .then_inc(s["f_done"], 1)
                dve.wait_ge(s["f_done"], j + 1)
                dve.wait_ge(s["sq_done"], j + 1)
                nc.vector.scalar_tensor_tensor(row(mix, j + 4), fk[:, :], 1.0, row(mix, j + 4), ALU.add, ALU.mult)\
                    .then_inc(s["k_done"], 1)
                dve.wait_ge(s["k_done"], j + 1)
                dve.wait_ge(s["v_done"], j + 1)
                nc.vector.scalar_tensor_tensor(rk[:, :], row(mix, j), g.par[:, bass.ds(j + PAR["r_k"], 1)], row(mix, j + 4), ALU.mult, ALU.mult)\
                    .then_inc(s["rk_done"], 1)
                dve.wait_ge(s["rn_done"], j + 1)
                dve.wait_ge(s["kk_raw"], j + 1)
                nc.vector.tensor_tensor(kk[:, :], kk[:, :], rn[:, :], ALU.mult).then_inc(s["kk_done"], 1)
                dve.wait_ge(s["kk_done"], j + 1)
                nc.vector.tensor_tensor(a[:, :], a[:, :], kk[:, :], ALU.mult).then_inc(s["b_done"], 1)
                dve.wait_ge(s["e_done"], j * 2 + 2)
                arj = ar[:, bass.ds(j, 1)].rearrange("p o c x t -> p (o c) x t")
                nc.vector.scalar_tensor_tensor(arj[:, :, 0, :], ep[:, :, 0:CH], -1.0, chunks(kk[:, :]), ALU.mult, ALU.mult)
                nc.vector.tensor_tensor(arj[:, :, 1, :], ep[:, :, 1:CH + 1], chunks(row(mix, j)), ALU.mult).then_inc(s["ar_done"], 1)
                dve.wait_ge(s["b_done"], j + 1)
                dve.wait_ge(s["ar_done"], j + 1)
                nc.vector.tensor_tensor(chunks(row(mix, j)), em[:, :, 1:CH + 1], chunks(a[:, :]), ALU.mult)
                nc.vector.tensor_tensor(chunks(row(mix, j + 4)), em[:, :, 1:CH + 1], chunks(row(mix, j + 4)), ALU.mult)
                nc.vector.tensor_tensor(row(decay, j)[:, 0:NC - 1], ep[:, 0:NC - 1, CH], em[:, 1:NC, 0], ALU.mult)
                dve.wait_ge(s["rk_sum"], j + 1)
                nc.vector.tensor_tensor(row(mix, j + 8), two(0), row(g.v, j), ALU.mult).then_inc(s["step_done"], 1)


def rwkv_chunk_phase(nc, g, l, mix, ar, decay):
    with ExitStack() as ctx:
        def sb(name, *shape):
            return ctx.enter_context(nc.sbuf_tensor(name, [P, *shape], F32))

        bp, kp = sb("b_padded", NP, 2, CH), sb("k_padded", NP, 2, CH)
        a_in, v_in = sb("a_in", NP, CH), sb("v_in", NP, CH)
        am = g.y[:, 0:NP, :].rearrange("p j t -> p (j t)").rearrange("p (h x t) -> p h x t", h=NH, x=4)
        ab, xi = (mix[:, n, :].rearrange("p (h t) -> p h t", h=NH) for n in (12, 13))
        gi = sb("inverse", NH, CH)
        zm = sb("z_masked", NH, CH // 2)
        bkt, vt = sb("bk_tokens", 2, NP, 2, HD), sb("v_tokens", NH, HD)
        bt, kt = (bkt[:, n, :, :, :].rearrange("p j o i -> p (j o) i") for n in range(2))
        ws, us = sb("w_in_sbuf", NH, HD), sb("u_in_sbuf", NH, HD)
        st, st2, sbd = sb("state", NP, HD), sb("state_sum", NP, HD), sb("state_diag", NP, 2, HD)
        ps = g.ps
        names = ("staged", "a_staged", "t_made", "t_ready", "a_made", "a_masked", "ab_made", "ab_ready", "g_ready", "x_made",
                 "x_ready", "z_made", "z_masked", "dg_made", "w_made", "w_ready", "u_made", "u_ready", "s_made", "state_ready",
                 "y_made", "y_ready", "unit_done", "s_added", "s_scaled")
        s = dict(zip(names, g.loop_sems(*["rc_" + n for n in names])))
        zeroed, padded = g.sems("rc_zeroed rc_padded")
        g.start()
        block = ctx.enter_context(nc.Block())
        bf, kf = mix[:, 0:NP, :], mix[:, NP:2 * NP, :]
        yf = bf

        def tokens(c):
            return bass.ds(c * CH, CH)

        def odd(ap, n):
            return ap.rearrange("p h (b two n) -> p h b two n", two=2, n=n)[:, :, :, 1, :]

        @block.gpsimd
        def _(pool):
            nc.gpsimd.memset(bp[:, :, :, :], 0.0).then_inc(padded, 1)
            nc.gpsimd.memset(kp[:, :, :, :], 0.0).then_inc(padded, 1)
            pool.wait_ge(padded, 2)
            with pool.Fori(0, NC) as c:
                pool.wait_ge(s["a_staged"], c + 1)
                pool.wait_ge(s["a_made"], c * NH + 1)
                for half in range(2):
                    rows = slice(half * HD, half * HD + HD)
                    pool.wait_ge(s["staged"], c * 5 + 2 * half + 1)
                    nc.gpsimd.tensor_copy(bp[rows, :, half, :], bf[rows, :, tokens(c)]).then_inc(s["staged"], 1)
                    nc.gpsimd.tensor_copy(kp[rows, :, half, :], kf[rows, :, tokens(c)]).then_inc(s["staged"], 1)
                pool.wait_ge(s["staged"], c * 5 + 5)
                nc.gpsimd.tensor_copy(v_in[:, :, :], g.v[:, :, tokens(c)]).then_inc(s["staged"], 1)
                pool.wait_ge(s["staged"], c * 5 + 6)
                pool.wait_ge(s["w_made"], c + 1)
                nc.gpsimd.tensor_copy(a_in[:, :, :], ar[:, :, bass.ds(c, 1), 0, :].rearrange("p j o t -> p j (o t)")).then_inc(s["a_staged"], 1)

        @block.tensor
        def _(pe):
            ident = g.con("ident")
            with pe.Fori(0, NC) as c:
                pe.wait_ge(s["staged"], c * 5 + 6)
                pe.wait_ge(s["w_ready"], c + 1)
                pe.wait_ge(s["u_ready"], c + 1)
                for j in range(NP):
                    mm = nc.tensor.transpose(ps[:, 5, j * P:(j + 1) * P], v_in[:, j, :], ident)
                mm.then_inc(s["t_made"], 1)
                for odd_head in range(2):
                    rows = slice(odd_head * HD, odd_head * HD + HD)
                    for n, src in enumerate((bp, kp)):
                        for j in range(NP):
                            cols = slice((n * NP + j) * HD, (n * NP + j + 1) * HD)
                            mm = nc.tensor.transpose(ps[:, 3 + odd_head, cols], src[rows, j, odd_head, :], ident[rows, rows])
                    mm.then_inc(s["t_made"], 1)
                pe.wait_ge(s["y_ready"], c + 1)
                pe.wait_ge(s["s_added"], c + 1)
                for h in range(NH):
                    if h >= 3:
                        pe.wait_ge(s["a_masked"], c * NH + h - 1)
                    moving = ar[:, h // 2, bass.ds(c, 1), :, :].rearrange("p o x t -> p (o x t)")
                    nc.tensor.matmul(ps[:, h % 3, 0:2 * CH], bp[:, h // 2, h % 2, :], moving, start=True, stop=True)
                    nc.tensor.matmul(ps[:, h % 3, 2 * CH:4 * CH], kp[:, h // 2, h % 2, :], moving, start=True, stop=True).then_inc(s["a_made"], 1)
                for q in range(2):
                    pe.wait_ge(s["a_masked"], c * NH + 4 * q + 5)
                    for h in range(4 * q, 4 * q + 4):
                        mm = nc.tensor.transpose(ps[:, 6 + q, (h % 4) * CH:(h % 4 + 1) * CH], am[:, h, 0, :], ident)
                    mm.then_inc(s["ab_made"], 1)
                pe.wait_ge(s["a_staged"], c + 2)
                pe.wait_ge(s["t_ready"], c * 3 + 4)
                pe.wait_ge(s["state_ready"], c + 1)
                for j in range(NP):
                    nc.tensor.matmul(ps[:, 4, j * P:(j + 1) * P], a_in[:, j, :], sbd[:, j, :, :].rearrange("p h i -> p (h i)"),
                                     start=j == 0, stop=False, skip_group_check=True)
                for h in range(NH):
                    mm = nc.tensor.matmul(ps[:, 4, h * HD:(h + 1) * HD], am[:, h, 2, :], vt[:, h, :], start=False, stop=h == NH - 1,
                                          skip_group_check=True)
                mm.then_inc(s["w_made"], 1)
                for lev in range(7):
                    n = 1 << lev
                    if lev:
                        for q in range(2):
                            pe.wait_ge(s["g_ready"], c * 14 + 2 * (lev - 1) + q + 2)
                            if lev == 1:
                                pe.wait_ge(s["ab_ready"], c * 2 + q + 2)
                            for h in range(4 * q, 4 * q + 4):
                                mm = nc.tensor.matmul(ps[:, q, (h % 4) * HD:(h % 4 + 1) * HD], ab[:, h, :],
                                                      odd(gi[:, h:h + 1, :], n).rearrange("p o b n -> p (o b) n"), start=True, stop=True)
                            mm.then_inc(s["z_made"], 1)
                        for q in range(2):
                            pe.wait_ge(s["z_masked"], c * 12 + 2 * (lev - 1) + q + 2)
                            pe.wait_ge(s["x_ready"], c * 12 + 2 * (lev - 1) + q + 2)
                            for h in range(4 * q, 4 * q + 4):
                                mm = nc.tensor.matmul(ps[:, 2 + q, (h % 4) * HD:(h % 4 + 1) * HD], xi[:, h, :], zm[:, h, :],
                                                      start=True, stop=True)
                            mm.then_inc(s["dg_made"], 1)
                    if lev < 6:
                        for q in range(2):
                            pe.wait_ge(s["g_ready"], c * 14 + 2 * lev + q + 2)
                            if lev == 0:
                                pe.wait_ge(s["ab_ready"], c * 2 + q + 2)
                            for h in range(4 * q, 4 * q + 4):
                                mm = nc.tensor.transpose(ps[:, 6 + q, (h % 4) * CH:(h % 4 + 1) * CH], gi[:, h, :], ident)
                            mm.then_inc(s["x_made"], 1)
                pe.wait_ge(s["w_ready"], c + 2)
                pe.wait_ge(s["g_ready"], c * 14 + 15)
                for h in range(NH):
                    mm = nc.tensor.matmul(ps[:, 5, h * HD:(h + 1) * HD], gi[:, h, :], ws[:, h, :], start=True, stop=True)
                mm.then_inc(s["u_made"], 1)
                for j in range(NP):
                    nc.tensor.matmul(ps[:, 0, j * P:(j + 1) * P], sbd[:, j, :, :].rearrange("p h i -> p (h i)"),
                                     ar[:, j, bass.ds(c, 1), 1, :].rearrange("p o t -> p (o t)"), start=j == 0, stop=False,
                                     skip_group_check=True)

                def y_part(values, which, last):
                    for h in range(NH):
                        rows = slice((h % 2) * HD, (h % 2) * HD + HD)
                        mm = nc.tensor.matmul(ps[rows, 0, (h // 2) * P:(h // 2 + 1) * P], values[:, h, :], am[:, h, which, :],
                                              start=False, stop=last, skip_group_check=True)
                    return mm

                def s_part(tok, values, first):
                    for h in range(NH):
                        rows = slice((h % 2) * HD, (h % 2) * HD + HD)
                        mm = nc.tensor.matmul(ps[rows, 1, (h // 2) * HD:(h // 2 + 1) * HD], tok[:, h, :], values[:, h, :],
                                              start=first and h < 2, stop=not first, skip_group_check=True)
                    return mm

                y_part(vt, 3, False)
                s_part(kt, vt, True)
                pe.wait_ge(s["u_ready"], c + 2)
                s_part(bt, us, False).then_inc(s["s_made"], 1)
                y_part(us, 1, True).then_inc(s["y_made"], 1)

        @block.scalar
        def _(act):
            with act.Fori(0, NC) as c:
                act.wait_ge(s["t_made"], c * 3 + 2)
                nc.scalar.activation(vt[:, :, :].rearrange("p h i -> p (h i)"), ps[:, 5, :], ACT.Copy).then_inc(s["t_ready"], 1)
                for odd_head in range(2):
                    act.wait_ge(s["t_made"], c * 3 + odd_head + 3)
                    nc.scalar.activation(bkt[:, :, :, odd_head, :], ps[:, 3 + odd_head, :].rearrange("p (x j i) -> p x j i", x=2, j=NP),
                                         ACT.Copy).then_inc(s["t_ready"], 1)
                for q in range(2):
                    act.wait_ge(s["ab_made"], c * 2 + q + 2)
                    nc.scalar.activation(ab[:, 4 * q:4 * q + 4, :].rearrange("p h t -> p (h t)"), ps[:, 6 + q, :], ACT.Copy)\
                        .then_inc(s["ab_ready"], 1)
                act.wait_ge(s["w_made"], c + 2)
                nc.scalar.activation(ws[:, :, :].rearrange("p h i -> p (h i)"), ps[:, 4, :], ACT.Copy).then_inc(s["w_ready"], 1)
                for lev in range(6):
                    for q in range(2):
                        act.wait_ge(s["x_made"], c * 12 + 2 * lev + q + 2)
                        nc.scalar.activation(xi[:, 4 * q:4 * q + 4, :].rearrange("p h t -> p (h t)"), ps[:, 6 + q, :], ACT.Copy)\
                            .then_inc(s["x_ready"], 1)
                act.wait_ge(s["u_made"], c + 2)
                nc.scalar.activation(us[:, :, :].rearrange("p h i -> p (h i)"), ps[:, 5, :], ACT.Copy).then_inc(s["u_ready"], 1)
                act.wait_ge(s["y_made"], c + 2)
                nc.scalar.activation(yf[:, :, tokens(c)], ps[:, 0, :].rearrange("p (j t) -> p j t", j=NP), ACT.Copy).then_inc(s["y_ready"], 1)

        @block.vector
        def _(dve):
            nc.vector.memset(st[:, :, :], 0.0).then_inc(zeroed, 1)
            nc.vector.memset(decay[:, :, NC - 1:NC], 0.0).then_inc(zeroed, 1)
            nc.vector.memset(sbd[:, :, :, :], 0.0).then_inc(zeroed, 1)
            dve.wait_ge(zeroed, 3)
            amask = g.con("amask")
            with dve.Fori(0, NC) as c:
                for h in range(NH):
                    dve.wait_ge(s["a_made"], c * NH + h + 2)
                    if h == 0:
                        dve.wait_ge(s["y_made"], c + 1)
                    nc.vector.tensor_tensor(am[:, h, :, :].rearrange("p x t -> p (x t)"), ps[:, h % 3, :], amask, ALU.mult)\
                        .then_inc(s["a_masked"], 1)
                for q in range(2):
                    heads = slice(4 * q, 4 * q + 4)
                    dve.wait_ge(s["a_masked"], c * NH + 4 * q + 5)
                    nc.vector.tensor_tensor(gi[:, heads, :], am[:, heads, 0, :], bc(g.con("unit").unsqueeze(1), P, 4, CH), ALU.mult)\
                        .then_inc(s["unit_done"], 1)
                    dve.wait_ge(s["unit_done"], c * 2 + q + 2)
                    nc.vector.tensor_tensor(gi[:, heads, :], gi[:, heads, :], bc(g.con("ident").unsqueeze(1), P, 4, CH), ALU.add)\
                        .then_inc(s["g_ready"], 1)
                for lev in range(1, 7):
                    n = 1 << lev
                    mask = g.con("level")[:, (lev - 1) * HD:lev * HD]
                    for q in range(2):
                        dve.wait_ge(s["z_made"], c * 12 + 2 * (lev - 1) + q + 2)
                        nc.vector.tensor_tensor(zm[:, 4 * q:4 * q + 4, :], ps[:, q, 0:4 * HD].rearrange("p (h n) -> p h n", h=4),
                                                bc(mask.unsqueeze(1), P, 4, HD), ALU.mult).then_inc(s["z_masked"], 1)
                    for q in range(2):
                        heads = slice(4 * q, 4 * q + 4)
                        dve.wait_ge(s["dg_made"], c * 12 + 2 * (lev - 1) + q + 2)
                        to = odd(gi[:, heads, :], n)
                        nc.vector.tensor_tensor(to, ps[:, 2 + q, 0:4 * HD].rearrange("p (h b n) -> p h b n", h=4, n=n), to, ALU.add)\
                            .then_inc(s["g_ready"], 1)
                dve.wait_ge(s["s_made"], c + 2)
                dve.wait_ge(s["state_ready"], c + 1)
                nc.vector.tensor_tensor(st2[:, :, :], ps[:, 1, 0:NP * HD].rearrange("p (j i) -> p j i", j=NP), st[:, :, :], ALU.add)\
                    .then_inc(s["s_added"], 1)
                dve.wait_ge(s["s_added"], c + 2)
                nc.vector.tensor_tensor(st[:, :, :], st2[:, :, :], bc(decay[:, :, bass.ds(c, 1)], P, NP, HD), ALU.mult).then_inc(s["s_scaled"], 1)
                dve.wait_ge(s["s_scaled"], c + 2)
                nc.vector.tensor_copy(sbd[0:HD, :, 0, :], st[0:HD, :, :])
                nc.vector.tensor_copy(sbd[HD:P, :, 1, :], st[HD:P, :, :]).then_inc(s["state_ready"], 1)


def rwkv_finish_phase(nc, g, l, mix):
    with ExitStack() as ctx:
        yc, sq, lg = (ctx.enter_context(nc.sbuf_tensor(n, [P, T], F32)) for n in ("gn_centred", "gn_sq", "gn_lg"))
        ps = g.ps
        names = ("mean", "centred", "squared", "var", "ln", "rstd", "scaled", "done")
        s = dict(zip(names, g.loop_sems(*["gn_" + n for n in names])))
        g.start()
        block = ctx.enter_context(nc.Block())

        def row(t, j):
            return t[:, bass.ds(j, 1), :].rearrange("p o t -> p (o t)")

        def two(b0):
            return ps[:, b0:b0 + 2, :].rearrange("p b n -> p (b n)")

        @block.tensor
        def _(pe):
            with pe.Fori(0, NP) as j:
                pe.wait_ge(s["centred"], j + 1)
                for b in range(2):
                    mm = nc.tensor.matmul(ps[:, b, :], g.con("blocks"), mix[:, bass.ds(j, 1), b * HALF:(b + 1) * HALF].rearrange("p o t -> p (o t)"),
                                          start=True, stop=True)
                mm.then_inc(s["mean"], 1)
                pe.wait_ge(s["squared"], j + 2)
                for b in range(2):
                    mm = nc.tensor.matmul(ps[:, 2 + b, :], g.con("blocks"), sq[:, b * HALF:(b + 1) * HALF], start=True, stop=True)
                mm.then_inc(s["var"], 1)

        @block.scalar
        def _(act):
            with act.Fori(0, NP) as j:
                act.wait_ge(s["centred"], j + 2)
                nc.scalar.activation(sq[:, :], yc[:, :], ACT.Square).then_inc(s["squared"], 1)
                act.wait_ge(s["var"], j + 2)
                act.wait_ge(s["scaled"], j + 1)
                nc.scalar.activation(lg[:, :], two(2), ACT.Ln, scale=1.0 / HD, bias=g.eps(GN_EPS)).then_inc(s["ln"], 1)
                act.wait_ge(s["ln"], j + 2)
                nc.scalar.activation(lg[:, :], lg[:, :], ACT.Exp, scale=-0.5).then_inc(s["rstd"], 1)

        @block.vector
        def _(dve):
            with dve.Fori(0, NP) as j:
                dve.wait_ge(s["mean"], j + 2)
                dve.wait_ge(s["done"], j + 1)
                nc.vector.scalar_tensor_tensor(yc[:, :], two(0), -1.0 / HD, row(mix, j), ALU.mult, ALU.add).then_inc(s["centred"], 1)
                dve.wait_ge(s["rstd"], j + 2)
                nc.vector.scalar_tensor_tensor(yc[:, :], yc[:, :], g.par[:, bass.ds(j + PAR["ln_w"], 1)], lg[:, :], ALU.mult, ALU.mult)\
                    .then_inc(s["scaled"], 1)
                dve.wait_ge(s["scaled"], j + 2)
                nc.vector.scalar_tensor_tensor(row(g.y, j), yc[:, :], g.par[:, bass.ds(j + PAR["ln_b"], 1)], row(mix, j + 8), ALU.add, ALU.add)\
                    .then_inc(s["done"], 1)


def gmlp_phase(nc, g, l):
    with ExitStack() as ctx:
        def sb(name, *shape):
            return ctx.enter_context(nc.sbuf_tensor(name, [P, *shape], F32))

        slots, wgv, gv = sb("gu_slots", 2, KD, P), sb("gv_weights", KD, BW), sb("gv", NC, BW)
        ln, ws, bs = sb("gmlp_ln", 2, BW), sb("mixing", NH, CH), sb("mixing_bias", NP, CH)
        stats, mv, rstd, t = sb("stats", NC, 6), sb("mean_var", NC, 2), sb("gv_rstd", NC), sb("mixed_v", 2, NP * CH)
        ps = g.ps
        w_loaded, free, done = ([g.sem(f"gu_{n}{u}") for u in range(2)] for n in ("w_loaded", "free", "done"))
        (gv_loaded, ln_loaded, ws_loaded, bs_loaded, ws_masked, gv_made, gelued, stat, aggregated, logged, rooted, normed, scaled,
         shifted, mixed, biased, gated) = g.sems("gv_loaded ln_loaded ws_loaded bs_loaded ws_masked gv_made gelued stat aggregated "
                                                 "logged rooted normed scaled shifted mixed biased gated")
        g.start()
        block = ctx.enter_context(nc.Block())

        @block.sync
        def _(sp):
            sp.dma_start(wgv[:, :, :], g.d_wgv[bass.ds(l, 1)].rearrange("o p k m -> p (o k) m")).then_inc(gv_loaded, 16)
            sp.dma_start(ln[:, :, :], g.d_gln[bass.ds(l, 1)].rearrange("o p a n -> p (o a) n")).then_inc(ln_loaded, 16)
            sp.dma_start(ws[:, :, :], g.d_ws[bass.ds(l, 1)].rearrange("o p h t -> p (o h) t")).then_inc(ws_loaded, 16)
            sp.dma_start(bs[:, :, :], g.d_bs[bass.ds(l, 1)].rearrange("o p j t -> p (o j) t")).then_inc(bs_loaded, 16)
            load_tiles(sp, g, l, T_GU, 4, slots, w_loaded, done)

        @block.tensor
        def _(pe):
            pe.wait_ge(gv_loaded, 16)
            for c in range(NC):
                if c >= 4:
                    pe.wait_ge(gelued, c - 3)
                for k in range(KD):
                    mm = nc.tensor.matmul(ps[:, 4 + c % 4, :], g.h[:, k, c * CH:(c + 1) * CH], wgv[:, k, :], start=k == 0, stop=k == KD - 1)
                mm.then_inc(gv_made, 1)
            project(nc, g, pe, slots, g.h, (0, 2), w_loaded, free, done, 4)
            pe.wait_ge(ws_masked, 1)
            for c in range(NC):
                pe.wait_ge(shifted, c + 1)
                if c >= 2:
                    pe.wait_ge(biased, c - 1)
                for h in range(NH):
                    rows = slice((h % 2) * HD, (h % 2) * HD + HD)
                    mm = nc.tensor.matmul(ps[rows, 4 + c % 2, (h // 2) * CH:(h // 2 + 1) * CH], gv[:, c, h * HD:(h + 1) * HD], ws[:, h, :],
                                          start=True, stop=True)
                mm.then_inc(mixed, 1)

        @block.scalar
        def _(act):
            for c in range(NC):
                act.wait_ge(gv_made, c + 1)
                nc.scalar.activation(gv[:, c, :], ps[:, 4 + c % 4, :], ACT.Gelu).then_inc(gelued, 1)
            for u in range(2):
                act.sem_inc(free[u], 1)
            with act.Fori(0, 2) as i:
                for u in range(2):
                    act.wait_ge(done[u], i + 1)
                    nc.scalar.activation(g.y[:, bass.ds(i * 2 + (u + 4), 1), :].rearrange("p o t -> p (o t)"),
                                         ps[:, 2 * u:2 * u + 2, :].rearrange("p b n -> p (b n)"), ACT.Gelu).then_inc(free[u], 1)
            act.wait_ge(aggregated, NC)
            nc.scalar.activation(rstd[:, :], mv[:, :, 1], ACT.Ln, bias=g.eps(LN_EPS)).then_inc(logged, 1)
            act.wait_ge(logged, 1)
            nc.scalar.activation(rstd[:, :], rstd[:, :], ACT.Exp, scale=-0.5).then_inc(rooted, 1)

        @block.gpsimd
        def _(pool):
            pool.wait_ge(ws_loaded, 16)
            nc.gpsimd.affine_select(out=ws[:, :, :], in_=ws[:, :, :], compare_op=ALU.is_ge, fill=0.0, base=0,
                                    pattern=[[0, NH], [1, CH]], channel_multiplier=-1).then_inc(ws_masked, 1)
            pool.wait_ge(ln_loaded, 16)
            for c in range(NC):
                pool.wait_ge(normed, c + 1)
                nc.gpsimd.tensor_tensor(gv[:, c, :], gv[:, c, :], ln[:, 0, :], ALU.mult).then_inc(scaled, 1)
                pool.wait_ge(scaled, c + 1)
                nc.gpsimd.tensor_tensor(gv[:, c, :], gv[:, c, :], ln[:, 1, :], ALU.add).then_inc(shifted, 1)

        @block.vector
        def _(dve):
            for c in range(NC):
                dve.wait_ge(gelued, c + 1)
                nc.vector.bn_stats(stats[:, c, :], gv[:, c, :]).then_inc(stat, 1)
                dve.wait_ge(stat, c + 1)
                nc.vector.bn_aggr(mv[:, c, :], stats[:, c, :]).then_inc(aggregated, 1)
            dve.wait_ge(rooted, 1)
            for c in range(NC):
                nc.vector.tensor_scalar(gv[:, c, :], gv[:, c, :], mv[:, c, 0:1], rstd[:, c:c + 1], ALU.subtract, ALU.mult).then_inc(normed, 1)
            dve.wait_ge(bs_loaded, 16)
            for u in range(2):
                dve.wait_ge(free[u], 3)
            for c in range(NC):
                dve.wait_ge(mixed, c + 1)
                if c >= 2:
                    dve.wait_ge(gated, c - 1)
                nc.vector.tensor_tensor(t[:, c % 2, :], ps[:, 4 + c % 2, :], bs[:, :, :].rearrange("p j t -> p (j t)"), ALU.add).then_inc(biased, 1)
                dve.wait_ge(biased, c + 1)
                u = g.y[:, 4:8, c * CH:(c + 1) * CH]
                nc.vector.tensor_tensor(u, t[:, c % 2, :].rearrange("p (j t) -> p j t", j=NP), u, ALU.mult).then_inc(gated, 1)


def latent_phase(nc, g, l, lat, kr):
    with ExitStack() as ctx:
        def sb(name, *shape):
            return ctx.enter_context(nc.sbuf_tensor(name, [P, *shape], F32))

        slots, sq, acc, rstd, turned = sb("lat_slots", 2, KD, P), sb("lat_sq", T), sb("lat_acc", 2, T), sb("lat_rstd", 2, T), sb("turned", T)
        ps = g.ps
        w_loaded, free, done = ([g.sem(f"la_{n}{u}") for u in range(2)] for n in ("w_loaded", "free", "done"))
        squared, added, summed, logged, rooted, rot, normed = g.sems("la_squared la_added la_summed la_logged la_rooted la_rot la_normed")
        g.start()
        block = ctx.enter_context(nc.Block())

        @block.sync
        def _(sp):
            load_tiles(sp, g, l, T_LAT, N_LAT, slots, w_loaded, done)

        @block.tensor
        def _(pe):
            project(nc, g, pe, slots, g.h, (0, 2), w_loaded, free, done, N_LAT)
            for n, upto in ((0, 3), (1, 5)):
                pe.wait_ge(added, upto)
                for b in range(2):
                    mm = nc.tensor.matmul(ps[:, 4 + 2 * n + b, :], g.ones[:, :], acc[:, n, b * HALF:(b + 1) * HALF], start=True, stop=True)
                mm.then_inc(summed, 1)

        @block.scalar
        def _(act):
            for u in range(2):
                act.sem_inc(free[u], 1)
            with act.Fori(0, N_LAT // 2) as i:
                for u in range(2):
                    act.wait_ge(done[u], i + 1)
                    nc.scalar.activation(lat[:, bass.ds(i * 2 + u, 1), :].rearrange("p o t -> p (o t)"),
                                         ps[:, 2 * u:2 * u + 2, :].rearrange("p b n -> p (b n)"), ACT.Copy).then_inc(free[u], 1)
            for k in range(5):
                if k:
                    act.wait_ge(added, k)
                act.wait_ge(free[k % 2], k // 2 + 2)
                nc.scalar.activation(sq[:, :], lat[:, k, :], ACT.Square).then_inc(squared, 1)
            for n, width in ((0, Q_LORA), (1, KV_LORA)):
                act.wait_ge(summed, n + 1)
                nc.scalar.activation(rstd[:, n, :], ps[:, 4 + 2 * n:6 + 2 * n, :].rearrange("p b n -> p (b n)"), ACT.Ln,
                                     scale=1.0 / width, bias=g.eps(NORM_EPS)).then_inc(logged, 1)
            for n in range(2):
                act.wait_ge(logged, 2)
                nc.scalar.activation(rstd[:, n, :], rstd[:, n, :], ACT.Exp, scale=-0.5).then_inc(rooted, 1)

        @block.vector
        def _(dve):
            for k in range(5):
                dve.wait_ge(squared, k + 1)
                n = 0 if k < 3 else 1
                if k in (0, 3):
                    nc.vector.tensor_copy(acc[:, n, :], sq[:, :]).then_inc(added, 1)
                else:
                    dve.wait_ge(added, k)
                    nc.vector.tensor_tensor(acc[:, n, :], acc[:, n, :], sq[:, :], ALU.add).then_inc(added, 1)
            dve.wait_ge(free[1], 4)
            for u in range(2):
                nc.vector.tensor_tensor(kr[u][64:96, :], lat[64:96, 5, :], g.rope[64:96, :], ALU.mult).then_inc(rot, 1)
            nc.vector.tensor_tensor(turned[64:96, :], lat[96:128, 5, :], g.rope[96:128, :], ALU.mult).then_inc(rot, 1)
            dve.wait_ge(rot, 3)
            for u in range(2):
                nc.vector.tensor_tensor(kr[u][64:96, :], kr[u][64:96, :], turned[64:96, :], ALU.add)
            for n, (first, tiles, name) in enumerate(((0, 3, "q_norm"), (3, 2, "kv_norm"))):
                dve.wait_ge(rooted, n + 1)
                for k in range(tiles):
                    nc.vector.scalar_tensor_tensor(lat[:, first + k, :], lat[:, first + k, :], g.pcol(name, k), rstd[:, n, :], ALU.mult, ALU.mult)


def attention_phase(nc, g, l, lat, kr):
    with ExitStack() as ctx:
        def sb(name, *shape):
            return ctx.enter_context(nc.sbuf_tensor(name, [P, *shape], F32))

        hw = [sb(f"head_weights{u}", HALF) for u in range(2)]
        q = [sb(f"q_head{u}", T) for u in range(2)]
        wv, v, prob, pt = sb("wv", 2, BW), sb("v_all", NC, BW), sb("prob", 2, T), sb("prob_t", 2, NC, CH)
        otok, turned = sb("out_tokens", NC, P), sb("q_turned", T)
        mx, nm, den, rden = (sb(n, 2, NC) for n in ("row_max", "neg_max", "row_sum", "row_recip"))
        ps = g.ps
        hw_loaded = [g.sem(f"at_hw{u}") for u in range(2)]
        wv_loaded, = g.sems("at_wv")
        v_made, v_ready = g.sems("at_v_made at_v_ready")
        names = ("q_made", "k_made", "q_ready", "turn", "q_turned", "k_ready", "s_made", "masked", "maxed", "negated", "exped", "t_made",
                 "t_ready", "o_made", "recip", "o_ready", "y_made", "y_ready")
        s = dict(zip(names, g.loop_sems(*["at_" + n for n in names])))
        g.start()
        block = ctx.enter_context(nc.Block())
        UN = 2 * NC
        groups = [1 if m % NC < 4 else 2 for m in range(UN)]
        GT = sum(groups)

        @block.sync
        def _(sp):
            sp.dma_start(wv[:, :, :], g.d_wv[bass.ds(l, 1)].rearrange("o p k m -> p (o k) m")).then_inc(wv_loaded, 16)
            with sp.Fori(0, NP) as j:
                for u in range(2):
                    sp.wait_ge(s["k_made"], j * 2 + 1)
                    sp.dma_start(hw[u][:, :], g.d_whead[bass.ds(l * NH + 2 * j + u, 1)].rearrange("o p n -> p (o n)"))\
                        .then_inc(hw_loaded[u], 16)

        @block.tensor
        def _(pe):
            ident = g.con("ident")
            pe.wait_ge(wv_loaded, 16)
            for c in range(NC):
                if c >= 4:
                    pe.wait_ge(v_ready, c - 3)
                for k in range(2):
                    mm = nc.tensor.matmul(ps[:, 4 + c % 4, :], lat[:, 3 + k, c * CH:(c + 1) * CH], wv[:, k, :], start=k == 0, stop=k == 1)
                mm.then_inc(v_made, 1)
            pe.wait_ge(v_ready, NC)
            with pe.Fori(0, NP) as j:
                pe.wait_ge(s["o_ready"], j * UN + 1)
                pe.wait_ge(s["y_ready"], j * 2 + 1)
                for u in range(2):
                    pe.wait_ge(hw_loaded[u], j * 16 + 16)
                    if u:
                        pe.wait_ge(s["q_ready"], j * 2 + 2)
                        pe.wait_ge(s["turn"], j * 4 + 3)
                    for k in range(3):
                        for b in range(2):
                            mm = nc.tensor.matmul(ps[:, b, :], hw[u][:, k * P:(k + 1) * P], lat[:, k, b * HALF:(b + 1) * HALF],
                                                  start=k == 0, stop=k == 2)
                    mm.then_inc(s["q_made"], 1)
                    if u:
                        pe.wait_ge(s["k_ready"], j * 2 + 2)
                    for k in range(2):
                        for b in range(2):
                            mm = nc.tensor.matmul(ps[0:NOPE, 2 + b, :], hw[u][:, 3 * P + k * NOPE:3 * P + (k + 1) * NOPE],
                                                  lat[:, 3 + k, b * HALF:(b + 1) * HALF], start=k == 0, stop=k == 1)
                    mm.then_inc(s["k_made"], 1)

                def scores(m):
                    u, c = divmod(m, NC)
                    if c == 0:
                        pe.wait_ge(s["q_turned"], j * 2 + u + 2)
                        pe.wait_ge(s["k_ready"], j * 2 + u + 2)
                        pe.wait_ge(s["q_ready"], j * 2 + u + 2)
                    if m >= 2:
                        pe.wait_ge(s["exped"], j * UN + m)
                    n = (c + 1) * CH
                    for b in range((n + HALF - 1) // HALF):
                        w = min(HALF, n - b * HALF)
                        mm = nc.tensor.matmul(ps[:, 4 + 2 * (m % 2) + b, 0:w], q[u][0:QK, c * CH:(c + 1) * CH],
                                              kr[u][0:QK, b * HALF:b * HALF + w], start=True, stop=True)
                    mm.then_inc(s["s_made"], 1)

                def turn(m):
                    c = m % NC
                    pe.wait_ge(s["exped"], j * UN + m + 2)
                    if m == 0:
                        pe.wait_ge(s["k_ready"], j * 2 + 3)
                    for n in range(groups[m]):
                        before = sum(groups[:m]) + n
                        if before:
                            pe.wait_ge(s["t_ready"], j * GT + before + 1)
                        for blk in range(4 * n, min(4 * n + 4, c + 1)):
                            mm = nc.tensor.transpose(ps[:, 2 + n, (blk % 4) * CH:(blk % 4 + 1) * CH],
                                                     prob[:, m % 2, blk * CH:(blk + 1) * CH], ident)
                        mm.then_inc(s["t_made"], 1)

                def values(m):
                    u, c = divmod(m, NC)
                    pe.wait_ge(s["t_ready"], j * GT + sum(groups[:m + 1]) + 1)
                    if m == 0:
                        pe.wait_ge(s["q_turned"], j * 2 + 3)
                        pe.wait_ge(s["q_ready"], j * 2 + 3)
                    if m >= 2:
                        pe.wait_ge(s["o_ready"], j * UN + m)
                    for blk in range(c + 1):
                        mm = nc.tensor.matmul(ps[:, m % 2, 0:HD], pt[:, m % 2, blk, :], v[:, blk, bass.ds(j * P + u * HD, HD)],
                                              start=blk == 0, stop=blk == c)
                    mm.then_inc(s["o_made"], 1)

                scores(0)
                for m in range(UN):
                    if m + 1 < UN:
                        scores(m + 1)
                    turn(m)
                    if m:
                        values(m - 1)
                values(UN - 1)
                pe.wait_ge(s["o_ready"], j * UN + UN + 1)
                for n in range(2):
                    for c in range(4 * n, 4 * n + 4):
                        mm = nc.tensor.transpose(ps[:, 2 + n, (c % 4) * CH:(c % 4 + 1) * CH], otok[:, c, :], ident)
                    mm.then_inc(s["y_made"], 1)

        def two(b0, rows):
            return ps[rows, b0:b0 + 2, :].rearrange("p b n -> p (b n)")

        @block.scalar
        def _(act):
            for c in range(NC):
                act.wait_ge(v_made, c + 1)
                nc.scalar.activation(v[:, c, :], ps[:, 4 + c % 4, :], ACT.Copy).then_inc(v_ready, 1)
            with act.Fori(0, NP) as j:
                for u in range(2):
                    act.wait_ge(s["q_made"], j * 2 + u + 2)
                    nc.scalar.activation(q[u][0:NOPE, :], two(0, slice(0, NOPE)), ACT.Copy).then_inc(s["q_ready"], 1)
                    act.wait_ge(s["k_made"], j * 2 + u + 2)
                    nc.scalar.activation(kr[u][0:NOPE, :], two(2, slice(0, NOPE)), ACT.Copy).then_inc(s["k_ready"], 1)
                for m in range(UN):
                    u, c = divmod(m, NC)
                    n = (c + 1) * CH
                    act.wait_ge(s["negated"], j * UN + m + 2)
                    if m >= 2:
                        act.wait_ge(s["t_made"], j * GT + sum(groups[:m - 1]) + 1)
                    nc.scalar.activation(prob[:, m % 2, 0:n], ps[:, 4 + 2 * (m % 2):6 + 2 * (m % 2), :].rearrange("p b n -> p (b n)")[:, 0:n],
                                         ACT.Exp, scale=SCALE, bias=nm[:, u, c:c + 1], accum_out=den[:, u, c:c + 1]).then_inc(s["exped"], 1)
                for n in range(2):
                    act.wait_ge(s["y_made"], j * 2 + n + 2)
                    nc.scalar.activation(g.y[:, bass.ds(j + 8, 1), n * HALF:(n + 1) * HALF].rearrange("p o t -> p (o t)"), ps[:, 2 + n, :],
                                         ACT.Copy).then_inc(s["y_ready"], 1)

        @block.vector
        def _(dve):
            with dve.Fori(0, NP) as j:
                for u in range(2):
                    dve.wait_ge(s["q_made"], j * 2 + u + 2)
                    dve.wait_ge(s["q_turned"], j * 2 + u + 1)
                    nc.vector.tensor_tensor(q[u][64:96, :], two(0, slice(64, 96)), g.rope[64:96, :], ALU.mult).then_inc(s["turn"], 1)
                    nc.vector.tensor_tensor(turned[64:96, :], two(0, slice(96, 128)), g.rope[96:128, :], ALU.mult).then_inc(s["turn"], 1)
                    dve.wait_ge(s["turn"], j * 4 + 2 * u + 3)
                    nc.vector.tensor_tensor(q[u][64:96, :], q[u][64:96, :], turned[64:96, :], ALU.add).then_inc(s["q_turned"], 1)

                def rowmax(m):
                    u, c = divmod(m, NC)
                    both = ps[:, 4 + 2 * (m % 2):6 + 2 * (m % 2), :].rearrange("p b n -> p (b n)")
                    diag = both[:, c * CH:(c + 1) * CH]
                    dve.wait_ge(s["s_made"], j * UN + m + 2)
                    nc.vector.tensor_tensor(diag, diag, g.con("causal"), ALU.add).then_inc(s["masked"], 1)
                    dve.wait_ge(s["masked"], j * UN + m + 2)
                    nc.vector.reduce_max(mx[:, u, c:c + 1], both[:, 0:(c + 1) * CH], AX.X).then_inc(s["maxed"], 1)
                    dve.wait_ge(s["maxed"], j * UN + m + 2)
                    nc.vector.tensor_scalar(nm[:, u, c:c + 1], mx[:, u, c:c + 1], -SCALE, None, ALU.mult).then_inc(s["negated"], 1)

                def turned_blocks(m):
                    c = m % NC
                    for n in range(groups[m]):
                        dve.wait_ge(s["t_made"], j * GT + sum(groups[:m]) + n + 2)
                        w = min(4, c + 1 - 4 * n)
                        if m >= 2 and n == 0:
                            dve.wait_ge(s["o_made"], j * UN + m)
                        nc.vector.tensor_copy(pt[:, m % 2, 4 * n:4 * n + w, :].rearrange("p b t -> p (b t)"), ps[:, 2 + n, 0:w * CH])\
                            .then_inc(s["t_ready"], 1)

                def normalise(m):
                    u, c = divmod(m, NC)
                    nc.vector.reciprocal(rden[:, u, c:c + 1], den[:, u, c:c + 1]).then_inc(s["recip"], 1)
                    dve.wait_ge(s["recip"], j * UN + m + 2)
                    dve.wait_ge(s["o_made"], j * UN + m + 2)
                    nc.vector.tensor_scalar(otok[:, c, u * HD:(u + 1) * HD], ps[:, m % 2, 0:HD], rden[:, u, c:c + 1], None, ALU.mult)\
                        .then_inc(s["o_ready"], 1)

                rowmax(0)
                for m in range(UN):
                    if m + 1 < UN:
                        rowmax(m + 1)
                    turned_blocks(m)
                    if m:
                        normalise(m - 1)
                normalise(UN - 1)


def gate_phase(nc, g, l):
    with ExitStack() as ctx:
        slots = ctx.enter_context(nc.sbuf_tensor("gate_slots", [P, 2, KD, P], F32))
        sig = ctx.enter_context(nc.sbuf_tensor("gate_sig", [P, 2, T], F32))
        t = ctx.enter_context(nc.sbuf_tensor("gate_silu", [P, 2, T], F32))
        w_loaded, done = ([g.sem(f"ga_{n}{u}") for u in range(2)] for n in ("w_loaded", "done"))
        free = [g.loop_sems(f"ga_free{u}")[0] for u in range(2)]
        sig_ready, gated = ([g.loop_sems(f"ga_{n}{u}")[0] for u in range(2)] for n in ("sig", "gated"))
        g.start()
        block = ctx.enter_context(nc.Block())

        @block.sync
        def _(sp):
            load_tiles(sp, g, l, T_GATE, N_GATE, slots, w_loaded, done)

        @block.tensor
        def _(pe):
            project(nc, g, pe, slots, g.h, (0, 2), w_loaded, free, done, N_GATE)

        def two(u):
            return g.ps[:, 2 * u:2 * u + 2, :].rearrange("p b n -> p (b n)")

        @block.scalar
        def _(act):
            with act.Fori(0, N_GATE // 2) as i:
                for u in range(2):
                    act.wait_ge(done[u], i + 1)
                    act.wait_ge(free[u], i + 1)
                    nc.scalar.activation(sig[:, u, :], two(u), ACT.Sigmoid).then_inc(sig_ready[u], 1)

        @block.vector
        def _(dve):
            with dve.Fori(0, N_GATE // 2) as i:
                for u in range(2):
                    y = g.y[:, bass.ds(i * 2 + u, 1), :].rearrange("p o t -> p (o t)")
                    dve.wait_ge(sig_ready[u], i + 2)
                    nc.vector.tensor_tensor(t[:, u, :], two(u), sig[:, u, :], ALU.mult).then_inc(free[u], 1)
                    dve.wait_ge(free[u], i + 2)
                    nc.vector.tensor_tensor(y, y, t[:, u, :], ALU.mult).then_inc(gated[u], 1)


def merge_phase(nc, g, l, mixed):
    with ExitStack() as ctx:
        slots = ctx.enter_context(nc.sbuf_tensor("merge_slots", [P, NBR, KD + 4, P], F32))
        sig = ctx.enter_context(nc.sbuf_tensor("merge_sig", [P, 2, T], F32))
        t = ctx.enter_context(nc.sbuf_tensor("merge_term", [P, 2, T], F32))
        w_loaded = [g.sem(f"me_w{n}") for n in range(NBR)]
        names = ("gate_made", "made", "sig", "term", "added")
        s = dict(zip(names, g.loop_sems(*["me_" + n for n in names])))
        g.start()
        block = ctx.enter_context(nc.Block())
        UN = 2 * NBR

        @block.sync
        def _(sp):
            with sp.Fori(0, KD // 2) as i:
                for m in range(UN):
                    if m < NBR:
                        sp.wait_ge(s["made"], i * UN + 1 if m == NBR - 1 else i * UN + 1)
                    else:
                        sp.wait_ge(s["made"], i * UN + m - NBR + 2)
                    sp.dma_start(slots[:, m % NBR], g.d_wm[bass.ds(l * (NBR * KD) + i * UN + m, 1)].rearrange("o p k m -> p (o k) m"))\
                        .then_inc(w_loaded[m % NBR], 16)

        @block.tensor
        def _(pe):
            with pe.Fori(0, KD // 2) as i:
                for m in range(UN):
                    b0 = 4 * (m % 2)
                    pe.wait_ge(w_loaded[m % NBR], i * 32 + 16 * (m // NBR) + 16)
                    pe.wait_ge(s["term"], i * UN + max(m - 1, 0) + 1 if m >= 2 else i * UN + 1 if m == 1 else i * UN + 1)
                    for k in range(KD):
                        for b in range(2):
                            mm = nc.tensor.matmul(g.ps[:, b0 + b, :], slots[:, m % NBR, k, :], g.h[:, k, b * HALF:(b + 1) * HALF],
                                                  start=k == 0, stop=k == KD - 1)
                    mm.then_inc(s["gate_made"], 1)
                    for k in range(4):
                        for b in range(2):
                            mm = nc.tensor.matmul(g.ps[:, b0 + 2 + b, :], slots[:, m % NBR, KD + k, :],
                                                  g.y[:, 4 * (m % NBR) + k, b * HALF:(b + 1) * HALF], start=k == 0, stop=k == 3)
                    mm.then_inc(s["made"], 1)

        def two(b0):
            return g.ps[:, b0:b0 + 2, :].rearrange("p b n -> p (b n)")

        @block.scalar
        def _(act):
            with act.Fori(0, KD // 2) as i:
                for m in range(UN):
                    act.wait_ge(s["gate_made"], i * UN + m + 2)
                    act.wait_ge(s["term"], i * UN + max(m - 1, 0) + 1)
                    nc.scalar.activation(sig[:, m % 2, :], two(4 * (m % 2)), ACT.Sigmoid).then_inc(s["sig"], 1)

        @block.vector
        def _(dve):
            with dve.Fori(0, KD // 2) as i:
                for m in range(UN):
                    d, n = divmod(m, NBR)
                    out = mixed[:, bass.ds(i * 2 + d, 1), :].rearrange("p o t -> p (o t)")
                    dve.wait_ge(s["sig"], i * UN + m + 2)
                    dve.wait_ge(s["made"], i * UN + m + 2)
                    if n == 0:
                        nc.vector.tensor_tensor(out, two(4 * (m % 2) + 2), sig[:, m % 2, :], ALU.mult).then_inc(s["term"], 1)
                    else:
                        nc.vector.tensor_tensor(t[:, n - 1, :], two(4 * (m % 2) + 2), sig[:, m % 2, :], ALU.mult).then_inc(s["term"], 1)
                        dve.wait_ge(s["term"], i * UN + m + 2)
                        if n == 2:
                            dve.wait_ge(s["added"], i * 4 + 2 * d + 2)
                        nc.vector.tensor_tensor(out, out, t[:, n - 1, :], ALU.add).then_inc(s["added"], 1)


def out_phase(nc, g, l, mixed):
    with ExitStack() as ctx:
        slots = ctx.enter_context(nc.sbuf_tensor("out_slots", [P, 2, KD, P], F32))
        sq, acc, lg, rstd = (ctx.enter_context(nc.sbuf_tensor(n, [P, T], F32)) for n in ("o_sq", "o_acc", "o_lg", "o_rstd"))
        x, o = g.y, g.h
        w_loaded, free, done = ([g.sem(f"ou_{n}{u}") for u in range(2)] for n in ("w_loaded", "free", "done"))
        x_loaded, = g.sems("ou_x_loaded")
        summed, logged, rooted, scaled, updated, stored = g.sems("ou_summed ou_logged ou_rooted ou_scaled ou_updated ou_stored")
        squared, added = g.loop_sems("ou_squared", "ou_added")
        g.start()
        block = ctx.enter_context(nc.Block())

        @block.sync
        def _(sp):
            def load(i, u):
                sp.dma_start(slots[:, u], g.d_wo[bass.ds(l * KD + 2 * i + u, 1)].rearrange("o p k m -> p (o k) m")).then_inc(w_loaded[u], 16)

            load(0, 0)
            load(0, 1)
            sp.dma_start(x[:, 0:KD, :], g.d_out).then_inc(x_loaded, 16)
            with sp.Fori(1, KD // 2) as i:
                for u in range(2):
                    sp.wait_ge(done[u], i)
                    load(i, u)
            sp.wait_ge(x_loaded, 16)
            for k in range(KD):
                sp.wait_ge(updated, k + 1)
                sp.dma_start(g.d_out[:, k, :], x[:, k, :]).then_inc(stored, 16)
            sp.wait_ge(stored, 16 * KD)

        @block.tensor
        def _(pe):
            project(nc, g, pe, slots, mixed, (0, 2), w_loaded, free, done, KD)
            pe.wait_ge(added, KD + 1)
            for b in range(2):
                mm = nc.tensor.matmul(g.ps[:, 4 + b, :], g.ones[:, :], acc[:, b * HALF:(b + 1) * HALF], start=True, stop=True)
            mm.then_inc(summed, 1)

        def two(b0):
            return g.ps[:, b0:b0 + 2, :].rearrange("p b n -> p (b n)")

        @block.scalar
        def _(act):
            for u in range(2):
                act.sem_inc(free[u], 1)
            with act.Fori(0, KD // 2) as i:
                for u in range(2):
                    act.wait_ge(done[u], i + 1)
                    act.wait_ge(added, i * 2 + u + 1)
                    nc.scalar.activation(sq[:, :], two(2 * u), ACT.Square).then_inc(squared, 1)
                    nc.scalar.activation(o[:, bass.ds(i * 2 + u, 1), :].rearrange("p o t -> p (o t)"), two(2 * u), ACT.Copy).then_inc(free[u], 1)
            act.wait_ge(summed, 1)
            nc.scalar.activation(lg[:, :], two(4), ACT.Ln, scale=1.0 / D, bias=g.eps(NORM_EPS)).then_inc(logged, 1)
            act.wait_ge(logged, 1)
            nc.scalar.activation(rstd[:, :], lg[:, :], ACT.Exp, scale=-0.5).then_inc(rooted, 1)

        @block.vector
        def _(dve):
            nc.vector.memset(acc[:, :], 0.0).then_inc(scaled, 1)
            dve.wait_ge(scaled, 1)
            with dve.Fori(0, KD) as i:
                dve.wait_ge(squared, i + 2)
                dve.wait_ge(added, i + 1)
                nc.vector.tensor_tensor(acc[:, :], acc[:, :], sq[:, :], ALU.add).then_inc(added, 1)
            dve.wait_ge(rooted, 1)
            dve.wait_ge(x_loaded, 16)
            for k in range(KD):
                nc.vector.scalar_tensor_tensor(o[:, k, :], o[:, k, :], g.pcol("post", k), rstd[:, :], ALU.mult, ALU.mult).then_inc(scaled, 1)
                dve.wait_ge(scaled, k + 2)
                nc.vector.tensor_tensor(x[:, k, :], x[:, k, :], o[:, k, :], ALU.add).then_inc(updated, 1)


def setup_phase(nc, g):
    C1 = 6.28125
    C2 = 0.0019350051879882812
    C3 = 2 * math.pi - C1 - C2
    MAGIC = 1.5 * 2 ** 23
    with ExitStack() as ctx:
        pos = ctx.enter_context(nc.sbuf_tensor("pos", [P, T], I32))
        ang, turns, rest = (ctx.enter_context(nc.sbuf_tensor(n, [P, T], F32)) for n in ("ang", "turns", "rest"))
        con_loaded, pos_loaded, x_copied, filled, step, reduced, folded, done = g.sems("con pos x_copied filled step reduced folded roped")
        g.start()
        block = ctx.enter_context(nc.Block())
        rows = slice(64, 128)

        @block.sync
        def _(sp):
            sp.dma_start(g.consts[:, :], g.d_con).then_inc(con_loaded, 16)
            sp.dma_start(pos[rows, :], g.d_pos.partition_broadcast(64)).then_inc(pos_loaded, 16)
            sp.dma_start(g.d_out, g.d_x).then_inc(x_copied, 16)
            sp.wait_ge(con_loaded, 16)
            sp.wait_ge(x_copied, 16)

        @block.vector
        def _(dve):
            nc.vector.memset(g.ones[:, :], 1.0)
            nc.vector.memset(g.v[:, :, :], 0.0)
            for n, value in enumerate(g.small_values):
                nc.vector.memset(g.small[:, n:n + 1], value).then_inc(filled, 1)
            dve.wait_ge(con_loaded, 16)
            dve.wait_ge(pos_loaded, 16)
            n = [0]

            def chained(ins):
                n[0] += 1
                ins.then_inc(step, 1)
                dve.wait_ge(step, n[0])

            chained(nc.vector.tensor_copy(ang[rows, :], pos[rows, :]))
            chained(nc.vector.tensor_scalar(ang[rows, :], ang[rows, :], g.con("freq")[rows, :], None, ALU.mult))
            chained(nc.vector.tensor_scalar(turns[rows, :], ang[rows, :], 1.0 / (2 * math.pi), MAGIC, ALU.mult, ALU.add))
            chained(nc.vector.tensor_scalar(turns[rows, :], turns[rows, :], MAGIC, None, ALU.subtract))
            for part in (C1, C2, C3):
                chained(nc.vector.scalar_tensor_tensor(ang[rows, :], turns[rows, :], -part, ang[rows, :], ALU.mult, ALU.add))
            chained(nc.vector.tensor_scalar(rest[rows, :], ang[rows, :], 3.1415925, -3.1415925, ALU.min, ALU.max))
            chained(nc.vector.scalar_tensor_tensor(ang[64:96, :], rest[64:96, :], -1.0, rest[64:96, :], ALU.mult, ALU.min))
            nc.vector.tensor_scalar(rest[64:96, :], ang[64:96, :], math.pi / 2, None, ALU.add).then_inc(folded, 1)

        @block.scalar
        def _(act):
            act.wait_ge(folded, 1)
            nc.scalar.activation(g.rope[rows, :], rest[rows, :], ACT.Sin).then_inc(done, 1)


def build(nc, d_x, d_pos, d_con, d_par, d_wt, d_up, d_wgv, d_gln, d_ws, d_bs, d_whead, d_wv, d_wm, d_wo, d_out):
    g = Core()
    g.d_x, g.d_pos, g.d_con, g.d_par, g.d_wt, g.d_up, g.d_wgv, g.d_gln = d_x, d_pos, d_con, d_par, d_wt, d_up, d_wgv, d_gln
    g.d_ws, g.d_bs, g.d_whead, g.d_wv, g.d_wm, g.d_wo, g.d_out = d_ws, d_bs, d_whead, d_wv, d_wm, d_wo, d_out
    g.small_values = [NORM_EPS, GN_EPS, LN_EPS, 0.5 * KK_SHIFT * math.log(2.0)]
    with ExitStack() as ctx:
        def sb(name, *shape):
            return ctx.enter_context(nc.sbuf_tensor(name, [P, *shape], F32))

        g.h = sb("h", KD, T)
        g.v = sb("v_first", NP, T)
        g.y = sb("y", NBR * NP, T)
        g.consts, g.ones, g.rope, g.par = sb("consts", N_CON), sb("ones", P), sb("rope", T), sb("par", N_PAR)
        g.small = sb("small", len(g.small_values))
        g.ps = ctx.enter_context(nc.psum_tensor("ps", [P, 8, HALF], F32))
        g.con = lambda name: g.consts[:, CON[name][0]:CON[name][0] + CON[name][1]]
        g.pcol = lambda name, k: g.par[:, PAR[name] + k:PAR[name] + k + 1]
        g.eps = lambda value: g.small[:, g.small_values.index(value):g.small_values.index(value) + 1]

        pool = [ctx.enter_context(nc.semaphore(f"s{i}")) for i in range(40)]
        used, started = [], []

        def sem(name):
            used.append(pool[len(used)])
            return used[-1]

        g.sem = sem
        g.sems = lambda names: [sem(n) for n in names.split()]

        def loop_sems(*names):
            got = [sem(n) for n in names]
            started.extend(got)
            return got

        def start():
            for x in used:
                nc.sync.sem_clear(x)
            for x in started:
                nc.sync.sem_inc(x, 1)
            nc.all_engine_barrier()
            used.clear()
            started.clear()

        g.loop_sems, g.start = loop_sems, start
        setup_phase(nc, g)
        with nc.Fori(0, L) as l:
            norm_phase(nc, g, l)
            with ExitStack() as rw:
                mix = rw.enter_context(nc.sbuf_tensor("mix", [P, N_RW, T], F32))
                decay = rw.enter_context(nc.sbuf_tensor("decay", [P, NP, NC], F32))
                ar = g.y[:, NP:NBR * NP, :].rearrange("p j t -> p (j t)").rearrange("p (j c x t) -> p j c x t", j=NP, c=NC, x=2)
                rwkv_project_phase(nc, g, l, mix)
                rwkv_prepare_phase(nc, g, l, mix, ar, decay)
                rwkv_chunk_phase(nc, g, l, mix, ar, decay)
                rwkv_finish_phase(nc, g, l, mix)
            gmlp_phase(nc, g, l)
            with ExitStack() as at:
                lat = at.enter_context(nc.sbuf_tensor("latents", [P, N_LAT, T], F32))
                kr = [at.enter_context(nc.sbuf_tensor(f"k_head{u}", [P, T], F32)) for u in range(2)]
                latent_phase(nc, g, l, lat, kr)
                attention_phase(nc, g, l, lat, kr)
            gate_phase(nc, g, l)
            with ExitStack() as me:
                mixed = me.enter_context(nc.sbuf_tensor("mixed", [P, KD, T], F32))
                merge_phase(nc, g, l, mixed)
                out_phase(nc, g, l, mixed)


def constants():
    con = np.zeros((P, N_CON), np.float32)

    def put(name, value):
        con[:, CON[name][0]:CON[name][0] + CON[name][1]] = value

    i, j = np.arange(P)[:, None], np.arange(P)[None, :]
    put("ident", i == j)
    put("blocks", i // HD == j // HD)
    put("amask", np.concatenate([i < j, i <= j, i < j, i <= j], 1))
    put("unit", (i % 2 == 0) & (j == i + 1))
    level = []
    for lev in range(1, 7):
        n = 1 << lev
        cols = np.arange(P).reshape(-1, 2, n)[:, 1, :].reshape(1, -1)
        level.append(i // n == cols // n - 1)
    put("level", np.concatenate(level, 1))
    put("causal", np.where(j <= i, 0.0, MASKED))
    put("restart", np.tile(np.arange(CH + 1) > 0, NC)[None, :])
    freq = (np.float32(1.0) / (np.float32(10000.0) ** (np.arange(0, ROPE, 2, dtype=np.float32) / np.float32(ROPE)))).astype(np.float32)
    column = np.zeros(P, np.float32)
    column[64:96] = np.tile(freq, 2)
    column[96:128] = np.concatenate([-freq, freq])
    put("freq", column[:, None])
    return con


def tiles(w):
    k, m = w.shape
    return w.reshape(k // P, P, m // P, P).transpose(2, 1, 0, 3)


def columns(v):
    return v.reshape(-1, P).T


def lay_out(x, positions, w_in, pre_norm, post_norm, rwkv_mu, rwkv_w0, rwkv_w_up, rwkv_a0, rwkv_a_up, rwkv_k_k, rwkv_k_a, rwkv_r_k,
            rwkv_ln_w, rwkv_ln_b, rwkv_v0, rwkv_v_down, rwkv_v_up, gmlp_ln_w, gmlp_ln_b, gmlp_w_s, gmlp_b_s, mla_q_norm, mla_w_uq,
            mla_kv_norm, mla_w_ukv, w_branch, w_out):
    z = lambda *shape: np.zeros(shape, np.float32)
    par, wt, up, wgv, gln, ws, bs, whead, wv, wm, wo = ([] for _ in range(11))
    for l in range(L):
        v0 = rwkv_v0[l - 1] if l else z(BW)
        v_down = rwkv_v_down[l - 1] if l else z(D, V_LORA)
        v_up = rwkv_v_up[l - 1] if l else z(V_LORA, BW)
        par.append(np.concatenate([columns(a) for a in (
            pre_norm[l], post_norm[l], np.concatenate([rwkv_mu[l], z(P)]), rwkv_w0[l], rwkv_a0[l], rwkv_k_k[l], rwkv_k_a[l],
            rwkv_r_k[l].reshape(-1), rwkv_ln_w[l], rwkv_ln_b[l], v0, mla_q_norm[l], mla_kv_norm[l],
            np.full(P, 1.0 if l else 0.0, np.float32))], 1))
        w = w_in[l]
        kr = w[:, O_KR:O_KR + ROPE]
        half = ROPE // 2
        swap = lambda a: np.concatenate([a[:, half:], a[:, :half]], 1)
        wide = np.concatenate([w[:, :O_RWG], v_down, z(D, P - V_LORA), w[:, O_GU:O_GV], w[:, O_CQ:O_KR], z(D, 64), kr, swap(kr),
                               w[:, O_RWG:O_GU], w[:, O_GG:O_CQ], w[:, O_MG:O_MERGE]], 1)
        wt.append(tiles(wide))
        u = z(NP, P, 3, P)
        for j in range(NP):
            cols = slice(j * P, (j + 1) * P)
            u[j, :64, 0], u[j, 64:, 1], u[j, :V_LORA, 2] = rwkv_w_up[l][:, cols], rwkv_a_up[l][:, cols], v_up[:, cols]
        up.append(u)
        wgv.append(w[:, O_GV:O_GG].reshape(KD, P, BW).transpose(1, 0, 2))
        gln.append(np.broadcast_to(np.stack([gmlp_ln_w[l], gmlp_ln_b[l]])[None], (P, 2, BW)))
        ws.append(gmlp_w_s[l].transpose(2, 0, 1))
        bs.append(np.repeat(gmlp_b_s[l], HD, axis=0).reshape(NP, P, CH).transpose(1, 0, 2))
        uq = mla_w_uq[l].reshape(Q_LORA, NH, QK)
        ukv = mla_w_ukv[l].reshape(KV_LORA, NH, NOPE + HD)
        for h in range(NH):
            one = np.concatenate([uq[:, h], swap(uq[:, h, NOPE:])], 1)
            whead.append(np.concatenate([one.reshape(3, P, P).transpose(1, 0, 2).reshape(P, -1),
                                         ukv[:, h, :NOPE].reshape(2, P, NOPE).transpose(1, 0, 2).reshape(P, -1)], 1))
        wv.append(ukv[:, :, NOPE:].reshape(KV_LORA, BW).reshape(2, P, BW).transpose(1, 0, 2))
        gates = tiles(w[:, O_MERGE:]).reshape(NBR, KD, P, KD, P)
        branch = np.stack([tiles(w_branch[l, n]) for n in range(NBR)])
        wm.append(np.concatenate([gates, branch], 3).transpose(1, 0, 2, 3, 4).reshape(KD * NBR, P, KD + 4, P))
        wo.append(tiles(w_out[l]))
    cat = lambda a: np.ascontiguousarray(np.concatenate(a, 0))
    stack = lambda a: np.ascontiguousarray(np.stack(a, 0))
    return {
        "x": np.ascontiguousarray(x[0].T.reshape(KD, P, T).transpose(1, 0, 2)), "pos": np.ascontiguousarray(positions.reshape(1, T)),
        "con": constants(), "par": stack(par), "wt": cat(wt), "up": cat(up), "wgv": stack(wgv), "gln": stack(gln), "ws": stack(ws),
        "bs": stack(bs), "whead": stack(whead), "wv": stack(wv), "wm": cat(wm), "wo": cat(wo),
    }


def kernel(**inputs):
    import concourse.bacc as _bacc
    from concourse.bass_utils import run_bass_kernel_spmd as _run

    arrays = lay_out(**{k: np.asarray(v) for k, v in inputs.items()})
    nc = _bacc.Bacc("TRN2", target_bir_lowering=False, num_devices=1)
    args = {f"d_{k}": nc.dram_tensor(f"in_{k}", a.shape, mybir.dt.from_np(a.dtype), kind="ExternalInput").ap() for k, a in arrays.items()}
    out = nc.dram_tensor("out_x", (P, KD, T), F32, kind="ExternalOutput").ap()
    build(nc, d_out=out, **args)
    r = _run(nc, [{f"in_{k}": a for k, a in arrays.items()}], core_ids=[0])
    got = r.results[0]["out_x"]
    return np.ascontiguousarray(got.transpose(1, 0, 2).reshape(D, T).T)[None]
```

```python
import math
from contextlib import ExitStack

import numpy as np

import concourse.bass as bass
from concourse import mybir

F32 = mybir.dt.float32
F32R = mybir.dt.float32r
I32 = mybir.dt.int32
ACT = mybir.ActivationFunctionType
ALU = mybir.AluOpType
AX = mybir.AxisListType

P = 128
D = 1024
KD = D // P
T = 1024
HALF = 512
L = 2
BW = 512
NBR = 3
CH = 128
NC = T // CH
HD = 64
NH = 8
NP = NH // 2
W_LORA, A_LORA, V_LORA = 64, 64, 32
NOPE, ROPE = 64, 32
QK = NOPE + ROPE
Q_LORA, KV_LORA = 384, 256
NORM_EPS, GN_EPS, LN_EPS = 1e-6, 64e-5, 1e-5
DECAY = math.exp(-0.5)
KK_SHIFT = 16
SCALE = QK ** -0.5
MASKED = -1e30

SIZES = (3 * BW + W_LORA + A_LORA, BW, BW, BW, BW, Q_LORA, KV_LORA, ROPE, BW, NBR * D)
OFF = [0] + [int(o) for o in np.cumsum(SIZES)]
(O_RW, O_RWG, O_GU, O_GV, O_GG, O_CQ, O_CKV, O_KR, O_MG, O_MERGE) = OFF[:10]

N_RW = 14
T_GU = N_RW
T_LAT = T_GU + 4
N_LAT = 6
T_GATE = T_LAT + N_LAT
N_GATE = 12
N_WT = T_GATE + N_GATE

PAR = {}
_at = 0
for _name, _n in (("pre", 8), ("post", 8), ("mu", N_RW), ("w0", 4), ("a0", 4), ("k_k", 4), ("k_a", 4),
                  ("r_k", 4), ("ln_w", 4), ("ln_b", 4), ("v0", 4), ("q_norm", 3), ("kv_norm", 2), ("flag", 1)):
    PAR[_name] = _at
    _at += _n
N_PAR = _at

CON = {}
_at = 0
for _name, _n in (("ident", P), ("blocks", P), ("amask", 4 * P), ("unit", P), ("level", 6 * HD),
                  ("causal", P), ("restart", NC * (CH + 1)), ("freq", 1)):
    CON[_name] = (_at, _n)
    _at += _n
N_CON = _at


class Core:
    pass


def bc(ap, *shape):
    return ap.to_broadcast(list(shape))


def two(ps, b0, rows=slice(0, P)):
    return ps[rows, b0:b0 + 2, :].rearrange("p b n -> p (b n)")


def row(t, j):
    return t[:, bass.ds(j, 1), :].rearrange("p o t -> p (o t)")


class Stream:

    def __init__(self, nc, g, ctx, tag, source, first, n, view=None):
        self.nc, self.g, self.source, self.first, self.n = nc, g, source, first, n
        if view is None:
            self.raw = ctx.enter_context(nc.sbuf_tensor(f"{tag}_raw", [P, 2, KD, P], F32))
            self.parts = ctx.enter_context(nc.sbuf_tensor(f"{tag}_parts", [P, 2, 2, KD, P], F32R))
        else:
            self.raw, self.parts = view
        self.loaded, self.rounded, self.split_done, self.done = (
            [g.sem(f"{tag}_{name}{u}") for u in range(2)] for name in ("loaded", "rounded", "split", "done"))

    def load(self, sp, i, u):
        sp.dma_start(self.raw[:, u], self.source[bass.ds(self.first + 2 * i + u, 1)].rearrange("o p k m -> p (o k) m"))\
            .then_inc(self.loaded[u], 16)

    def loads(self, sp):
        for u in range(2):
            self.load(sp, 0, u)
        self.more_loads(sp)

    def more_loads(self, sp, between=None):
        with sp.Fori(1, self.n // 2) as i:
            for u in range(2):
                sp.wait_ge(self.split_done[u], i)
                self.load(sp, i, u)
            if between:
                between(i)

    def round(self, act, i, u):
        act.wait_ge(self.loaded[u], i * 16 + 16)
        self.nc.scalar.activation(self.parts[:, u, 0], self.raw[:, u], ACT.Copy).then_inc(self.rounded[u], 1)

    def rounds(self, act, empty):
        for u in range(2):
            self.round(act, 0, u)
        self.more_rounds(act, empty)

    def more_rounds(self, act, empty):
        with act.Fori(0, self.n // 2 - 1) as i:
            for u in range(2):
                act.wait_ge(self.done[u], i + 1)
                empty(i, u)
                self.round(act, i + 1, u)
        for u in range(2):
            act.wait_ge(self.done[u], self.n // 2)
            empty(self.n // 2 - 1, u)

    def split(self, pool, i, u):
        pool.wait_ge(self.rounded[u], i + 1)
        self.nc.gpsimd.tensor_tensor(self.parts[:, u, 1], self.raw[:, u], self.parts[:, u, 0].bitcast(F32), ALU.subtract)\
            .then_inc(self.split_done[u], 1)

    def splits(self, pool):
        for u in range(2):
            self.split(pool, 0, u)
        self.more_splits(pool)

    def more_splits(self, pool):
        with pool.Fori(1, self.n // 2) as i:
            for u in range(2):
                self.split(pool, i, u)

    def products(self, k, u, rhs, banks):
        return products_of_parts(self.nc, k, lambda b: self.g.ps[:, banks[u] + b, :], lambda part: self.parts[:, u, part, k, :], rhs)

    def project(self, pe, rhs, banks, free, first=0):
        with pe.Fori(first, self.n // 2) as i:
            for u in range(2):
                pe.wait_ge(self.split_done[u], i + 1)
                pe.wait_ge(free[u], i + 1)
                for k in range(KD):
                    mm = self.products(k, u, rhs, banks)
                mm.then_inc(self.done[u], 1)


def products_of_parts(nc, k, out, weights, rhs):
    for w, x in ((0, 0), (0, 1), (1, 0)):
        for b in range(2):
            mm = nc.tensor.matmul(out(b), weights(w), rhs[:, x, k, b * HALF:(b + 1) * HALF],
                                  start=k == 0 and (w, x) == (0, 0), stop=k == KD - 1 and w == 1)
    return mm


def rwkv_project_phase(nc, g, l, h, mix):
    with ExitStack() as ctx:
        raw = g.y[:, 8:10, :].rearrange("p u (k m) -> p u k m", k=KD)
        parts = ctx.enter_context(nc.sbuf_tensor("rp_parts", [P, 2, 2, KD, P], F32R))
        w = Stream(nc, g, ctx, "rp", g.d_wt, l * N_WT, N_RW, (raw, parts))
        shifted = g.y[:, 4:8, :].rearrange("p a t -> p (a t)")[:, 0:2 * (T + 1)].rearrange("p (u t) -> p u t", u=2)
        diff = g.y[:, 0:2, :]
        x, x_rstd = g.y, g.y[:, 11, :]
        free, mixed = ([g.loop_sems(f"rp_{name}{u}")[0] for u in range(2)] for name in ("free", "mixed"))
        diffed = [g.sem(f"rp_diff{u}") for u in range(2)]
        par_loaded, zeroed, scaled, rounded, even_split, odd_split, spilled = g.sems(
            "par_loaded rp_zeroed h_scaled h_rounded h_even_split h_odd_split h_spilled")
        g.start()
        block = ctx.enter_context(nc.Block())

        @block.sync
        def _(sp):
            sp.dma_start(g.par[:, :], g.d_par[bass.ds(l, 1)].rearrange("o p n -> p (o n)")).then_inc(par_loaded, 16)
            for u in range(2):
                w.load(sp, 0, u)
            sp.wait_ge(even_split, KD // 2)
            sp.wait_ge(odd_split, KD // 2)

            def spill(k):
                sp.dma_start(g.d_h[:, :, bass.ds(k, 1), :], h[:, :, bass.ds(k, 1), :].bitcast(F32)).then_inc(spilled, 16)

            w.more_loads(sp, lambda i: spill(i - 1))
            for k in range(N_RW // 2 - 1, KD):
                spill(k)
            sp.wait_ge(spilled, 16 * KD)

        @block.gpsimd
        def _(pool):
            for u in range(2):
                w.split(pool, 0, u)
            for k in range(1, KD, 2):
                pool.wait_ge(rounded, k + 1)
                nc.gpsimd.tensor_tensor(h[:, 1, k, :], mix[:, k, :], h[:, 0, k, :].bitcast(F32), ALU.subtract).then_inc(odd_split, 1)
            w.more_splits(pool)

        @block.tensor
        def _(pe):
            for u in range(2):
                pe.wait_ge(w.split_done[u], 1)
            for k in range(KD):
                pe.wait_ge(odd_split if k % 2 else even_split, k // 2 + 1)
                for u in range(2):
                    mm = w.products(k, u, h, (0, 2))
                    if k == KD - 1:
                        mm.then_inc(w.done[u], 1)
            w.project(pe, h, (0, 2), free, 1)

        @block.scalar
        def _(act):
            for u in range(2):
                w.round(act, 0, u)
            for k in range(KD):
                act.wait_ge(scaled, k + 1)
                nc.scalar.activation(h[:, 0, k, :], mix[:, k, :], ACT.Copy).then_inc(rounded, 1)

            def empty(i, u):
                act.wait_ge(mixed[u], i + 1)
                act.wait_ge(zeroed, 1)
                nc.scalar.activation(shifted[:, u, 1:T + 1], two(g.ps, 2 * u), ACT.Copy).then_inc(free[u], 1)

            w.more_rounds(act, empty)

        @block.vector
        def _(dve):
            dve.wait_ge(par_loaded, 16)
            for k in range(KD):
                nc.vector.scalar_tensor_tensor(mix[:, k, :], x[:, k, :], g.pcol("pre", k), x_rstd, ALU.mult, ALU.mult).then_inc(scaled, 1)
                if k % 2:
                    dve.wait_ge(rounded, k)
                    nc.vector.tensor_tensor(h[:, 1, k - 1, :], mix[:, k - 1, :], h[:, 0, k - 1, :].bitcast(F32), ALU.subtract)\
                        .then_inc(even_split, 1)
            dve.wait_ge(scaled, KD)
            nc.vector.memset(shifted[:, :, 0:1], 0.0).then_inc(zeroed, 1)
            dve.wait_ge(zeroed, 1)
            with dve.Fori(0, N_RW // 2) as i:
                for u in range(2):
                    dve.wait_ge(free[u], i + 2)
                    nc.vector.tensor_tensor(diff[:, u, :], shifted[:, u, 0:T], shifted[:, u, 1:T + 1], ALU.subtract).then_inc(diffed[u], 1)
                    dve.wait_ge(diffed[u], i + 1)
                    nc.vector.scalar_tensor_tensor(row(mix, i * 2 + u), diff[:, u, :], g.par[:, bass.ds(i * 2 + (u + PAR["mu"]), 1)],
                                                   shifted[:, u, 1:T + 1], ALU.mult, ALU.add).then_inc(mixed[u], 1)


def rwkv_prepare_phase(nc, g, l, mix, ar, decay, v):
    with ExitStack() as ctx:
        def sb(name, *shape):
            return ctx.enter_context(nc.sbuf_tensor(name, [P, *shape], F32))

        up = sb("up", 2, 3, P)
        sg, csum, em = (sb(n, 2, NC, CH + 1) for n in ("sg", "csum", "em"))
        cm, ep = sg, csum
        a, vg, fk, rk = (sb(n, 2, T) for n in ("a_gate", "v_gate", "fk", "rk"))
        kk, sq = g.y[:, 0:2, :], g.y[:, 2:4, :]
        rn = sq
        ps = g.ps
        names = ("tanhed", "zw_ready", "zv_ready", "sg_done", "csum_done", "cm_done", "e_done", "a_done", "vg_done", "vdiff",
                 "vgated", "v_done", "kk_raw", "sq_done", "kk_sum", "kk_max", "rn_ln", "rn_done", "f_done",
                 "k_done", "rk_done", "rk_sum", "zeroed", "b_done", "ar_done", "v_loaded")
        s = dict(zip(names, g.sems(" ".join("pp_" + n for n in names))))
        s["step_done"], s["kk_done"] = g.loop_sems("pp_step_done", "pp_kk_done")
        s["first_done"], = g.loop_sems("pp_first_done")
        up_loaded = [g.sem(f"pp_up{u}") for u in range(2)]
        g.start()
        block = ctx.enter_context(nc.Block())
        both = range(2)

        def chunks(ap):
            return ap.rearrange("p (c t) -> p c t", c=NC)

        def pcol(name, j):
            return g.par[:, bass.ds(j + PAR[name], 1)]


        @block.sync
        def _(sp):
            for i in range(NP // 2):
                for u in both:
                    if i:
                        sp.wait_ge(s["zv_ready"], i * 2 + u - 1)
                    sp.dma_start(up[:, u], g.d_up[bass.ds(l * NP + 2 * i + u, 1)].rearrange("o p a m -> p (o a) m")).then_inc(up_loaded[u], 16)
                if i == 0:
                    sp.dma_start(v[:, :, :], g.d_v).then_inc(s["v_loaded"], 16)
            sp.wait_ge(s["step_done"], NP // 2 + 1)
            sp.dma_start(g.d_v, v[:, :, :]).then_inc(g.v_stored, 16)

        @block.tensor
        def _(pe):
            pe.wait_ge(s["tanhed"], 1)
            with pe.Fori(0, NP // 2) as i:
                def project_up(u, parts):
                    for n in parts:
                        for b in range(2):
                            mm = nc.tensor.matmul(ps[:, 2 * n + b, :], up[:, u, n, :], mix[:, 13 if n == 2 else 12, b * HALF:(b + 1) * HALF],
                                                  start=True, stop=True)
                    return mm

                def head_sums(b0, src):
                    for b in range(2):
                        mm = nc.tensor.matmul(ps[:, b0 + b, :], g.con("blocks"), src[:, b * HALF:(b + 1) * HALF], start=True, stop=True)
                    return mm

                for u in both:
                    pe.wait_ge(s["sq_done"], i * 2 + u + 1)
                    if u:
                        pe.wait_ge(s["kk_max"], i * 2 + 1)
                    else:
                        pe.wait_ge(s["first_done"], i + 1)
                    head_sums(6, sq[:, u, :]).then_inc(s["kk_sum"], 1)
                    pe.wait_ge(up_loaded[u], i * 16 + 16)
                    if u:
                        pe.wait_ge(s["sg_done"], i * 2 + 1)
                    project_up(u, (0,)).then_inc(s["zw_ready"], 1)
                    if u:
                        pe.wait_ge(s["vg_done"], i * 2 + 1)
                    else:
                        pe.wait_ge(s["step_done"], i + 1)
                    project_up(u, (1, 2)).then_inc(s["zv_ready"], 1)
                for u in both:
                    pe.wait_ge(s["rk_done"], i * 2 + u + 1)
                    pe.wait_ge(s["vg_done" if u else "kk_max"], i * 2 + 2)
                    head_sums(4 if u else 6, rk[:, u, :]).then_inc(s["rk_sum"], 1)

        @block.scalar
        def _(act):
            nc.scalar.activation(mix[0:W_LORA, 12, :], mix[0:W_LORA, 12, :], ACT.Tanh).then_inc(s["tanhed"], 1)
            with act.Fori(0, NP // 2) as i:
                for u in both:
                    act.wait_ge(s["kk_done"], i * 2 + 1)
                    nc.scalar.activation(sq[:, u, :], row(mix, i * 2 + (u + 4)), ACT.Square, scale=pcol("k_k", i * 2 + u)).then_inc(s["sq_done"], 1)
                for u in both:
                    act.wait_ge(s["zw_ready"], i * 2 + u + 1)
                    act.wait_ge(s["zeroed"], i * 2 + u + 1)
                    nc.scalar.activation(sg[:, u, :, 1:CH + 1], chunks(two(ps, 0)), ACT.Sigmoid, bias=pcol("w0", i * 2 + u)).then_inc(s["sg_done"], 1)
                    act.wait_ge(s["zv_ready"], i * 2 + u + 1)
                    act.wait_ge(s["step_done"], i + 1)
                    nc.scalar.activation(a[:, u, :], two(ps, 2), ACT.Sigmoid, bias=pcol("a0", i * 2 + u)).then_inc(s["a_done"], 1)
                    nc.scalar.activation(vg[:, u, :], two(ps, 4), ACT.Sigmoid, bias=pcol("v0", i * 2 + u)).then_inc(s["vg_done"], 1)
                for u in both:
                    act.wait_ge(s["kk_max"], i * 2 + u + 1)
                    nc.scalar.activation(rn[:, u, :], fk[:, u, :], ACT.Ln, scale=float(2 ** KK_SHIFT)).then_inc(s["rn_ln"], 1)
                for u in both:
                    act.wait_ge(s["rn_ln"], i * 2 + u + 1)
                    nc.scalar.activation(rn[:, u, :], rn[:, u, :], ACT.Exp, scale=-0.5, bias=g.eps(0.5 * KK_SHIFT * math.log(2.0)))\
                        .then_inc(s["rn_done"], 1)
                for u in both:
                    act.wait_ge(s["cm_done"], i * 2 + u + 1)
                    nc.scalar.activation(ep[:, u], cm[:, u], ACT.Exp, scale=-DECAY)
                    nc.scalar.activation(em[:, u], cm[:, u], ACT.Exp, scale=DECAY).then_inc(s["e_done"], 1)

        @block.gpsimd
        def _(pool):
            pool.wait_ge(s["v_loaded"], 16)
            with pool.Fori(0, NP // 2) as i:
                for u in both:
                    pool.wait_ge(s["step_done"], i + 1)
                    nc.gpsimd.tensor_tensor(rk[:, u, :], row(v, i * 2 + u), row(mix, i * 2 + (u + 8)), ALU.subtract).then_inc(s["vdiff"], 1)
                for u in both:
                    pool.wait_ge(s["vdiff"], i * 2 + u + 1)
                    pool.wait_ge(s["vg_done"], i * 2 + u + 1)
                    nc.gpsimd.tensor_tensor(vg[:, u, :], rk[:, u, :], vg[:, u, :], ALU.mult).then_inc(s["vgated"], 1)

        @block.vector
        def _(dve):
            for u in both:
                nc.vector.memset(sg[:, u, :, 0:1], 0.0).then_inc(s["zeroed"], 1)
            with dve.Fori(0, NP // 2) as i:
                for u in both:
                    dve.wait_ge(s["step_done"], i + 1)
                    nc.vector.tensor_scalar(kk[:, u, :], row(mix, i * 2 + (u + 4)), pcol("k_k", i * 2 + u), None, ALU.mult).then_inc(s["kk_raw"], 1)
                for u in both:
                    dve.wait_ge(s["kk_sum"], i * 2 + u + 1)
                    nc.vector.tensor_scalar(fk[:, u, :], two(ps, 6), 1e-24, None, ALU.max).then_inc(s["kk_max"], 1)
                for u in both:
                    dve.wait_ge(s["sg_done"], i * 2 + u + 1)
                    nc.vector.tensor_tensor_scan(csum[:, u].rearrange("p c t -> p (c t)"), g.con("restart"),
                                                 sg[:, u].rearrange("p c t -> p (c t)"), 0.0, ALU.mult, ALU.add).then_inc(s["csum_done"], 1)
                for u in both:
                    dve.wait_ge(s["csum_done"], i * 2 + u + 1)
                    nc.vector.tensor_tensor(cm[:, u], csum[:, u], bc(csum[:, u, :, CH // 2:CH // 2 + 1], P, NC, CH + 1), ALU.subtract)\
                        .then_inc(s["cm_done"], 1)
                for u in both:
                    dve.wait_ge(s["a_done"], i * 2 + u + 1)
                    dve.wait_ge(s["rn_ln"], i * 2 + u + 1)
                    nc.vector.tensor_scalar(fk[:, u, :], a[:, u, :], 1.0, pcol("k_a", i * 2 + u), ALU.subtract, ALU.mult).then_inc(s["f_done"], 1)
                for u in both:
                    dve.wait_ge(s["f_done"], i * 2 + u + 1)
                    dve.wait_ge(s["kk_raw"], i * 2 + u + 1)
                    k = row(mix, i * 2 + (u + 4))
                    nc.vector.scalar_tensor_tensor(k, fk[:, u, :], 1.0, k, ALU.add, ALU.mult).then_inc(s["k_done"], 1)
                for u in both:
                    dve.wait_ge(s["vgated"], i * 2 + u + 1)
                    nc.vector.scalar_tensor_tensor(row(v, i * 2 + u), vg[:, u, :], g.pcol("flag", 0), row(mix, i * 2 + (u + 8)), ALU.mult, ALU.add)\
                        .then_inc(s["v_done"], 1)
                for u in both:
                    dve.wait_ge(s["k_done"], i * 2 + u + 1)
                    dve.wait_ge(s["v_done"], i * 2 + u + 1)
                    nc.vector.scalar_tensor_tensor(rk[:, u, :], row(mix, i * 2 + u), pcol("r_k", i * 2 + u), row(mix, i * 2 + (u + 4)),
                                                   ALU.mult, ALU.mult).then_inc(s["rk_done"], 1)
                for u in both:
                    dve.wait_ge(s["rn_done"], i * 2 + u + 1)
                    nc.vector.tensor_tensor(kk[:, u, :], kk[:, u, :], rn[:, u, :], ALU.mult).then_inc(s["kk_done"], 1)
                for u in both:
                    dve.wait_ge(s["kk_done"], i * 2 + u + 2)
                    nc.vector.tensor_tensor(a[:, u, :], a[:, u, :], kk[:, u, :], ALU.mult).then_inc(s["b_done"], 1)
                for u in both:
                    dve.wait_ge(s["e_done"], i * 2 + u + 1)
                    nc.vector.memset(sg[:, u, :, 0:1], 0.0).then_inc(s["zeroed"], 1)
                    arj = ar[:, bass.ds(i * 2 + u, 1)].rearrange("p o c x t -> p (o c) x t")
                    nc.vector.scalar_tensor_tensor(arj[:, :, 0, :], ep[:, u, :, 0:CH], -1.0, chunks(kk[:, u, :]), ALU.mult, ALU.mult)
                    nc.vector.tensor_tensor(arj[:, :, 1, :], ep[:, u, :, 1:CH + 1], chunks(row(mix, i * 2 + u)), ALU.mult).then_inc(s["ar_done"], 1)
                for u in both:
                    dve.wait_ge(s["b_done"], i * 2 + u + 1)
                    dve.wait_ge(s["ar_done"], i * 2 + u + 1)
                    dve.wait_ge(s["rk_done"], i * 2 + u + 1)
                    nc.vector.tensor_tensor(chunks(row(mix, i * 2 + u)), em[:, u, :, 1:CH + 1], chunks(a[:, u, :]), ALU.mult)
                    k = row(mix, i * 2 + (u + 4))
                    nc.vector.tensor_tensor(chunks(k), em[:, u, :, 1:CH + 1], chunks(k), ALU.mult)
                    nc.vector.tensor_tensor(row(decay, i * 2 + u)[:, 0:NC - 1], ep[:, u, 0:NC - 1, CH], em[:, u, 1:NC, 0], ALU.mult)
                    dve.wait_ge(s["rk_sum"], i * 2 + u + 1)
                    nc.vector.tensor_tensor(row(mix, i * 2 + (u + 8)), two(ps, 4 if u else 6), row(v, i * 2 + u), ALU.mult)\
                        .then_inc(s["step_done" if u else "first_done"], 1)


def rwkv_chunk_phase(nc, g, l, mix, ar, decay, v):
    with ExitStack() as ctx:
        def sb(name, *shape):
            return ctx.enter_context(nc.sbuf_tensor(name, [P, *shape], F32))

        bp, kp = sb("b_padded", NP, 2, CH), sb("k_padded", NP, 2, CH)
        a_in, v_in = sb("a_in", NP, CH), sb("v_in", NP, CH)
        am = g.y[:, 0:NP, :].rearrange("p j t -> p (j t)").rearrange("p (h x t) -> p h x t", h=NH, x=4)
        ab, xi = (mix[:, n, :].rearrange("p (h t) -> p h t", h=NH) for n in (12, 13))
        gi = sb("inverse", NH, CH)
        zm = sb("z_masked", NH, CH // 2)
        bkt, vt = sb("bk_tokens", 2, NP, 2, HD), sb("v_tokens", NH, HD)
        bt, kt = (bkt[:, n, :, :, :].rearrange("p j o i -> p (j o) i") for n in range(2))
        ws, us = sb("w_in_sbuf", NH, HD), sb("u_in_sbuf", NH, HD)
        st, st2, sbd = sb("state", NP, HD), sb("state_sum", NP, HD), sb("state_diag", NP, 2, HD)
        ps = g.ps
        names = ("staged", "a_staged", "t_made", "t_ready", "a_made", "a_masked", "ab_made", "ab_ready", "g_ready", "x_made",
                 "x_ready", "z_made", "z_masked", "dg_made", "w_made", "w_ready", "u_made", "u_ready", "s_made", "state_ready",
                 "y_made", "y_ready", "unit_done", "s_added", "s_scaled")
        s = dict(zip(names, g.loop_sems(*["rc_" + n for n in names])))
        zeroed, padded, copied = g.sems("rc_zeroed rc_padded rc_v_copied")
        g.start()
        block = ctx.enter_context(nc.Block())
        bf, kf = mix[:, 0:NP, :], mix[:, NP:2 * NP, :]
        yf = bf

        def tokens(c):
            return bass.ds(c * CH, CH)

        def n_rows(lev):
            return CH if lev < 6 else HD

        def odd(ap, n):
            return ap.rearrange("p h (b two n) -> p h b two n", two=2, n=n)[:, :, :, 1, :]

        @block.sync
        def _(sp):
            sp.wait_ge(g.v_stored, l * 16 + 32)
            sp.sem_inc(copied, 1)

        @block.gpsimd
        def _(pool):
            nc.gpsimd.memset(bp[:, :, :, :], 0.0).then_inc(padded, 1)
            nc.gpsimd.memset(kp[:, :, :, :], 0.0).then_inc(padded, 1)
            pool.wait_ge(padded, 2)
            with pool.Fori(0, NC) as c:
                pool.wait_ge(s["a_staged"], c + 1)
                pool.wait_ge(s["a_made"], c * NH + 1)
                for half in range(2):
                    rows = slice(half * HD, half * HD + HD)
                    pool.wait_ge(s["staged"], c * 5 + 2 * half + 1)
                    nc.gpsimd.tensor_copy(bp[rows, :, half, :], bf[rows, :, tokens(c)]).then_inc(s["staged"], 1)
                    nc.gpsimd.tensor_copy(kp[rows, :, half, :], kf[rows, :, tokens(c)]).then_inc(s["staged"], 1)
                pool.wait_ge(s["staged"], c * 5 + 5)
                nc.gpsimd.tensor_copy(v_in[:, :, :], v[:, :, tokens(c)]).then_inc(s["staged"], 1)
                pool.wait_ge(s["staged"], c * 5 + 6)
                pool.wait_ge(s["w_made"], c + 1)
                nc.gpsimd.tensor_copy(a_in[:, :, :], ar[:, :, bass.ds(c, 1), 0, :].rearrange("p j o t -> p j (o t)")).then_inc(s["a_staged"], 1)

        @block.tensor
        def _(pe):
            ident = g.con("ident")
            with pe.Fori(0, NC) as c:
                pe.wait_ge(s["staged"], c * 5 + 6)
                pe.wait_ge(s["w_ready"], c + 1)
                pe.wait_ge(s["u_ready"], c + 1)
                for j in range(NP):
                    mm = nc.tensor.transpose(ps[:, 5, j * P:(j + 1) * P], v_in[:, j, :], ident)
                mm.then_inc(s["t_made"], 1)
                for odd_head in range(2):
                    rows = slice(odd_head * HD, odd_head * HD + HD)
                    for n, src in enumerate((bp, kp)):
                        for j in range(NP):
                            cols = slice((n * NP + j) * HD, (n * NP + j + 1) * HD)
                            mm = nc.tensor.transpose(ps[:, 3 + odd_head, cols], src[rows, j, odd_head, :], ident[rows, rows])
                    mm.then_inc(s["t_made"], 1)
                for h in range(NH):
                    if h == 0:
                        pe.wait_ge(s["s_added"], c + 1)
                    elif h == 2:
                        pe.wait_ge(s["y_ready"], c + 1)
                    elif h >= 3:
                        pe.wait_ge(s["a_masked"], c * NH + h - 1)
                    bank = (h + 1) % 3
                    moving = ar[:, h // 2, bass.ds(c, 1), :, :].rearrange("p o x t -> p (o x t)")
                    nc.tensor.matmul(ps[:, bank, 0:2 * CH], bp[:, h // 2, h % 2, :], moving, start=True, stop=True)
                    nc.tensor.matmul(ps[:, bank, 2 * CH:4 * CH], kp[:, h // 2, h % 2, :], moving, start=True, stop=True).then_inc(s["a_made"], 1)
                    if h in (5, 7):
                        q = (h - 5) // 2
                        pe.wait_ge(s["a_masked"], c * NH + 4 * q + 5)
                        for hh in range(4 * q, 4 * q + 4):
                            mm = nc.tensor.transpose(ps[:, 6 + q, (hh % 4) * CH:(hh % 4 + 1) * CH], am[:, hh, 0, :], ident)
                        mm.then_inc(s["ab_made"], 1)

                def make_w():
                    pe.wait_ge(s["a_staged"], c + 2)
                    pe.wait_ge(s["t_ready"], c * 3 + 4)
                    pe.wait_ge(s["state_ready"], c + 1)
                    for j in range(NP):
                        nc.tensor.matmul(ps[:, 4, j * P:(j + 1) * P], a_in[:, j, :], sbd[:, j, :, :].rearrange("p h i -> p (h i)"),
                                         start=j == 0, stop=False, skip_group_check=True)
                    for h in range(NH):
                        mm = nc.tensor.matmul(ps[:, 4, h * HD:(h + 1) * HD], am[:, h, 2, :], vt[:, h, :], start=False, stop=h == NH - 1,
                                              skip_group_check=True)
                    mm.then_inc(s["w_made"], 1)

                def make_xz(lev, q):
                    n = 1 << lev
                    pe.wait_ge(s["g_ready"], c * 14 + 2 * (lev - 1) + q + 2)
                    for h in range(4 * q, 4 * q + 4):
                        mm = nc.tensor.transpose(ps[:, 6 + q, (h % 4) * CH:(h % 4 + 1) * CH], gi[:, h, :], ident)
                    mm.then_inc(s["x_made"], 1)
                    if lev == 1:
                        pe.wait_ge(s["ab_ready"], c * 2 + q + 2)
                    for h in range(4 * q, 4 * q + 4):
                        mm = nc.tensor.matmul(ps[0:n_rows(lev), q, (h % 4) * HD:(h % 4 + 1) * HD], ab[:, h, 0:n_rows(lev)],
                                              odd(gi[:, h:h + 1, :], n).rearrange("p o b n -> p (o b) n"), start=True, stop=True)
                    mm.then_inc(s["z_made"], 1)

                def make_dg(lev, q):
                    pe.wait_ge(s["z_masked"], c * 12 + 2 * (lev - 1) + q + 2)
                    pe.wait_ge(s["x_ready"], c * 12 + 2 * (lev - 1) + q + 2)
                    for h in range(4 * q, 4 * q + 4):
                        mm = nc.tensor.matmul(ps[0:n_rows(lev), 2 + q, (h % 4) * HD:(h % 4 + 1) * HD], xi[:, h, 0:n_rows(lev)], zm[:, h, :],
                                              start=True, stop=True)
                    mm.then_inc(s["dg_made"], 1)

                for q in range(2):
                    pe.wait_ge(s["ab_ready"], c * 2 + q + 2)
                for lev in range(1, 7):
                    make_xz(lev, 0)
                    if lev == 1:
                        make_w()
                    else:
                        make_dg(lev - 1, 1)
                    make_dg(lev, 0)
                    make_xz(lev, 1)
                make_dg(6, 1)
                for j in range(NP):
                    nc.tensor.matmul(ps[:, 0, j * P:(j + 1) * P], sbd[:, j, :, :].rearrange("p h i -> p (h i)"),
                                     ar[:, j, bass.ds(c, 1), 1, :].rearrange("p o t -> p (o t)"), start=j == 0, stop=False,
                                     skip_group_check=True)

                def y_part(values, which, last):
                    for h in range(NH):
                        rows = slice((h % 2) * HD, (h % 2) * HD + HD)
                        mm = nc.tensor.matmul(ps[rows, 0, (h // 2) * P:(h // 2 + 1) * P], values[:, h, :], am[:, h, which, :],
                                              start=False, stop=last, skip_group_check=True)
                    return mm

                def s_part(tok, values, first):
                    for h in range(NH):
                        rows = slice((h % 2) * HD, (h % 2) * HD + HD)
                        mm = nc.tensor.matmul(ps[rows, 1, (h // 2) * HD:(h // 2 + 1) * HD], tok[:, h, :], values[:, h, :],
                                              start=first and h < 2, stop=not first, skip_group_check=True)
                    return mm

                y_part(vt, 3, False)
                pe.wait_ge(s["w_ready"], c + 2)
                pe.wait_ge(s["g_ready"], c * 14 + 15)
                for h in range(NH):
                    mm = nc.tensor.matmul(ps[:, 5, h * HD:(h + 1) * HD], gi[:, h, :], ws[:, h, :], start=True, stop=True)
                mm.then_inc(s["u_made"], 1)
                s_part(kt, vt, True)
                pe.wait_ge(s["u_ready"], c + 2)
                s_part(bt, us, False).then_inc(s["s_made"], 1)
                y_part(us, 1, True).then_inc(s["y_made"], 1)

        @block.scalar
        def _(act):
            with act.Fori(0, NC) as c:
                act.wait_ge(s["t_made"], c * 3 + 2)
                nc.scalar.activation(vt[:, :, :].rearrange("p h i -> p (h i)"), ps[:, 5, :], ACT.Copy).then_inc(s["t_ready"], 1)
                for odd_head in range(2):
                    act.wait_ge(s["t_made"], c * 3 + odd_head + 3)
                    nc.scalar.activation(bkt[:, :, :, odd_head, :], ps[:, 3 + odd_head, :].rearrange("p (x j i) -> p x j i", x=2, j=NP),
                                         ACT.Copy).then_inc(s["t_ready"], 1)
                for q in range(2):
                    act.wait_ge(s["ab_made"], c * 2 + q + 2)
                    nc.scalar.activation(ab[:, 4 * q:4 * q + 4, :].rearrange("p h t -> p (h t)"), ps[:, 6 + q, :], ACT.Copy)\
                        .then_inc(s["ab_ready"], 1)
                for lev in range(6):
                    if lev == 1:
                        act.wait_ge(s["w_made"], c + 2)
                        nc.scalar.activation(ws[:, :, :].rearrange("p h i -> p (h i)"), ps[:, 4, :], ACT.Copy).then_inc(s["w_ready"], 1)
                    for q in range(2):
                        act.wait_ge(s["x_made"], c * 12 + 2 * lev + q + 2)
                        nc.scalar.activation(xi[:, 4 * q:4 * q + 4, :].rearrange("p h t -> p (h t)"), ps[:, 6 + q, :], ACT.Copy)\
                            .then_inc(s["x_ready"], 1)
                act.wait_ge(s["u_made"], c + 2)
                nc.scalar.activation(us[:, :, :].rearrange("p h i -> p (h i)"), ps[:, 5, :], ACT.Copy).then_inc(s["u_ready"], 1)
                act.wait_ge(s["y_made"], c + 2)
                nc.scalar.activation(yf[:, :, tokens(c)], ps[:, 0, :].rearrange("p (j t) -> p j t", j=NP), ACT.Copy).then_inc(s["y_ready"], 1)

        @block.vector
        def _(dve):
            nc.vector.memset(st[:, :, :], 0.0).then_inc(zeroed, 1)
            nc.vector.memset(decay[:, :, NC - 1:NC], 0.0).then_inc(zeroed, 1)
            nc.vector.memset(sbd[:, :, :, :], 0.0).then_inc(zeroed, 1)
            dve.wait_ge(zeroed, 3)
            amask = g.con("amask")
            with dve.Fori(0, NC) as c:
                for q in range(2):
                    heads = slice(4 * q, 4 * q + 4)
                    for h in range(4 * q, 4 * q + 4):
                        dve.wait_ge(s["a_made"], c * NH + h + 2)
                        if h == 0:
                            dve.wait_ge(s["y_made"], c + 1)
                        nc.vector.tensor_tensor(am[:, h, :, :].rearrange("p x t -> p (x t)"), ps[:, (h + 1) % 3, :], amask, ALU.mult)\
                            .then_inc(s["a_masked"], 1)
                    dve.wait_ge(s["a_masked"], c * NH + 4 * q + 5)
                    nc.vector.tensor_tensor(gi[:, heads, :], am[:, heads, 0, :], bc(g.con("unit").unsqueeze(1), P, 4, CH), ALU.mult)\
                        .then_inc(s["unit_done"], 1)
                    dve.wait_ge(s["unit_done"], c * 2 + q + 2)
                    nc.vector.tensor_tensor(gi[:, heads, :], gi[:, heads, :], bc(g.con("ident").unsqueeze(1), P, 4, CH), ALU.add)\
                        .then_inc(s["g_ready"], 1)
                def mask_z(lev, q):
                    mask = g.con("level")[:, (lev - 1) * HD:lev * HD]
                    dve.wait_ge(s["z_made"], c * 12 + 2 * (lev - 1) + q + 2)
                    nc.vector.tensor_tensor(zm[:, 4 * q:4 * q + 4, :], ps[:, q, 0:4 * HD].rearrange("p (h n) -> p h n", h=4),
                                            bc(mask.unsqueeze(1), P, 4, HD), ALU.mult).then_inc(s["z_masked"], 1)

                def add_dg(lev, q):
                    n = 1 << lev
                    dve.wait_ge(s["dg_made"], c * 12 + 2 * (lev - 1) + q + 2)
                    to = odd(gi[0:n_rows(lev), 4 * q:4 * q + 4, :], n)
                    nc.vector.tensor_tensor(to, ps[0:n_rows(lev), 2 + q, 0:4 * HD].rearrange("p (h b n) -> p h b n", h=4, n=n), to, ALU.add)\
                        .then_inc(s["g_ready"], 1)

                for lev in range(1, 7):
                    mask_z(lev, 0)
                    if lev > 1:
                        add_dg(lev - 1, 1)
                    add_dg(lev, 0)
                    mask_z(lev, 1)
                add_dg(6, 1)
                dve.wait_ge(s["s_made"], c + 2)
                dve.wait_ge(s["state_ready"], c + 1)
                nc.vector.tensor_tensor(st2[:, :, :], ps[:, 1, 0:NP * HD].rearrange("p (j i) -> p j i", j=NP), st[:, :, :], ALU.add)\
                    .then_inc(s["s_added"], 1)
                dve.wait_ge(s["s_added"], c + 2)
                nc.vector.tensor_tensor(st[:, :, :], st2[:, :, :], bc(decay[:, :, bass.ds(c, 1)], P, NP, HD), ALU.mult).then_inc(s["s_scaled"], 1)
                dve.wait_ge(s["s_scaled"], c + 2)
                nc.vector.tensor_copy(sbd[0:HD, :, 0, :], st[0:HD, :, :])
                nc.vector.tensor_copy(sbd[HD:P, :, 1, :], st[HD:P, :, :]).then_inc(s["state_ready"], 1)


def rwkv_finish_phase(nc, g, l, mix, h):
    with ExitStack() as ctx:
        yc, sq, lg = (ctx.enter_context(nc.sbuf_tensor(n, [P, 2, T], F32)) for n in ("gn_centred", "gn_sq", "gn_lg"))
        ps = g.ps
        names = ("mean", "centred", "squared", "var", "ln", "rstd", "scaled", "done")
        mean, centred, squared, var, logged, rooted, scaled, done = g.sems(" ".join("gn_" + n for n in names))
        h_loaded = g.sem("h_loaded")
        g.start()
        block = ctx.enter_context(nc.Block())

        @block.sync
        def _(sp):
            sp.dma_start(h[:, :, :, :].bitcast(F32), g.d_h).then_inc(h_loaded, 16)
            sp.wait_ge(h_loaded, 16)

        @block.tensor
        def _(pe):
            def head_sums(b0, src):
                for b in range(2):
                    mm = nc.tensor.matmul(ps[:, b0 + b, :], g.con("blocks"), src[:, b * HALF:(b + 1) * HALF], start=True, stop=True)
                return mm

            for j in range(NP + 1):
                if j < NP:
                    if j >= 2:
                        pe.wait_ge(centred, j - 1)
                    head_sums(2 * (j % 2), mix[:, j, :]).then_inc(mean, 1)
                if j:
                    pe.wait_ge(squared, j)
                    if j >= 3:
                        pe.wait_ge(logged, j - 2)
                    head_sums(4 + 2 * ((j - 1) % 2), sq[:, (j - 1) % 2, :]).then_inc(var, 1)

        @block.scalar
        def _(act):
            def square(j):
                act.wait_ge(centred, j + 1)
                if j >= 2:
                    act.wait_ge(var, j - 1)
                nc.scalar.activation(sq[:, j % 2, :], yc[:, j % 2, :], ACT.Square).then_inc(squared, 1)

            square(0)
            for j in range(NP):
                if j + 1 < NP:
                    square(j + 1)
                act.wait_ge(var, j + 1)
                if j >= 2:
                    act.wait_ge(scaled, j - 1)
                nc.scalar.activation(lg[:, j % 2, :], two(ps, 4 + 2 * (j % 2)), ACT.Ln, scale=1.0 / HD, bias=g.eps(GN_EPS)).then_inc(logged, 1)
                act.wait_ge(logged, j + 1)
                nc.scalar.activation(lg[:, j % 2, :], lg[:, j % 2, :], ACT.Exp, scale=-0.5).then_inc(rooted, 1)

        @block.vector
        def _(dve):
            def centre(j):
                dve.wait_ge(mean, j + 1)
                if j >= 2:
                    dve.wait_ge(done, j - 1)
                nc.vector.scalar_tensor_tensor(yc[:, j % 2, :], two(ps, 2 * (j % 2)), -1.0 / HD, mix[:, j, :], ALU.mult, ALU.add).then_inc(centred, 1)

            centre(0)
            centre(1)
            for j in range(NP):
                dve.wait_ge(rooted, j + 1)
                nc.vector.scalar_tensor_tensor(yc[:, j % 2, :], yc[:, j % 2, :], g.pcol("ln_w", j), lg[:, j % 2, :], ALU.mult, ALU.mult)\
                    .then_inc(scaled, 1)
                dve.wait_ge(scaled, j + 1)
                nc.vector.scalar_tensor_tensor(g.y[:, j, :], yc[:, j % 2, :], g.pcol("ln_b", j), mix[:, 8 + j, :], ALU.add, ALU.add)\
                    .then_inc(done, 1)
                if j + 2 < NP:
                    centre(j + 2)


def gmlp_phase(nc, g, l, h):
    with ExitStack() as ctx:
        def sb(name, *shape):
            return ctx.enter_context(nc.sbuf_tensor(name, [P, *shape], F32))

        w = Stream(nc, g, ctx, "gu", g.d_wt, l * N_WT + T_GU, 4)
        wgv = sb("gv_raw", 2, BW)
        wgv_parts = ctx.enter_context(nc.sbuf_tensor("gv_parts", [P, 2, KD, BW], F32R))
        gv = g.y[:, 8:12, :].rearrange("p a t -> p (a t)").rearrange("p (c n) -> p c n", c=NC)
        ln, ws, bs = sb("gmlp_ln", 2, BW), sb("mixing", NH, CH), sb("mixing_bias", NP, CH)
        stats, mv, rstd, t = sb("stats", NC, 6), sb("mean_var", NC, 2), sb("gv_rstd", NC), sb("mixed_v", 2, NP * CH)
        ps = g.ps
        free = [g.loop_sems(f"gu_free{u}")[0] for u in range(2)]
        gv_loaded = [g.sem(f"gv_loaded{u}") for u in range(2)]
        (gv_rounded, gv_split, ln_loaded, ws_loaded, bs_loaded, ws_masked, gv_made, gelued, stat, aggregated, logged, rooted, normed, scaled,
         shifted, mixed, biased, gated) = g.sems("gv_rounded gv_split ln_loaded ws_loaded bs_loaded ws_masked gv_made gelued stat aggregated "
                                                 "logged rooted normed scaled shifted mixed biased gated")
        g.start()
        block = ctx.enter_context(nc.Block())

        @block.sync
        def _(sp):
            for k in range(KD):
                if k >= 2:
                    sp.wait_ge(gv_split, k - 1)
                sp.dma_start(wgv[:, k % 2, :], g.d_wgv[bass.ds(l, 1), :, k, :].rearrange("o p m -> p (o m)")).then_inc(gv_loaded[k % 2], 16)
            sp.dma_start(ln[:, :, :], g.d_gln[bass.ds(l, 1)].rearrange("o p a n -> p (o a) n")).then_inc(ln_loaded, 16)
            sp.dma_start(ws[:, :, :], g.d_ws[bass.ds(l, 1)].rearrange("o p h t -> p (o h) t")).then_inc(ws_loaded, 16)
            sp.dma_start(bs[:, :, :], g.d_bs[bass.ds(l, 1)].rearrange("o p j t -> p (o j) t")).then_inc(bs_loaded, 16)
            w.loads(sp)

        @block.tensor
        def _(pe):
            def values(c, k):
                for x, part in ((0, 0), (1, 0), (0, 1)):
                    mm = nc.tensor.matmul(ps[:, 4 + c % 4, :], h[:, x, k, c * CH:(c + 1) * CH], wgv_parts[:, part, k, :],
                                          start=k == 0 and (x, part) == (0, 0), stop=k == KD - 1 and part == 1)
                return mm

            for k in range(KD):
                pe.wait_ge(gv_split, k + 1)
                for c in range(4):
                    mm = values(c, k)
                    if k == KD - 1:
                        mm.then_inc(gv_made, 1)
            for c in range(4, NC):
                pe.wait_ge(gelued, c - 3)
                for k in range(KD):
                    mm = values(c, k)
                mm.then_inc(gv_made, 1)
            w.project(pe, h, (0, 2), free)
            pe.wait_ge(ws_masked, 1)
            for c in range(NC):
                pe.wait_ge(shifted, c + 1)
                if c >= 2:
                    pe.wait_ge(biased, c - 1)
                for gr in range(NH):
                    rows = slice((gr % 2) * HD, (gr % 2) * HD + HD)
                    mm = nc.tensor.matmul(ps[rows, 4 + c % 2, (gr // 2) * CH:(gr // 2 + 1) * CH], gv[:, c, gr * HD:(gr + 1) * HD], ws[:, gr, :],
                                          start=True, stop=True)
                mm.then_inc(mixed, 1)

        @block.scalar
        def _(act):
            for k in range(KD):
                act.wait_ge(gv_loaded[k % 2], 16 * (k // 2) + 16)
                nc.scalar.activation(wgv_parts[:, 0, k, :], wgv[:, k % 2, :], ACT.Copy).then_inc(gv_rounded, 1)
            for u in range(2):
                w.round(act, 0, u)
            for c in range(NC):
                act.wait_ge(gv_made, c + 1)
                nc.scalar.activation(gv[:, c, :], ps[:, 4 + c % 4, :], ACT.Gelu).then_inc(gelued, 1)

            def empty(i, u):
                nc.scalar.activation(row(g.y, i * 2 + (u + 4)), two(ps, 2 * u), ACT.Gelu).then_inc(free[u], 1)

            act.wait_ge(aggregated, NC)
            nc.scalar.activation(rstd[:, :], mv[:, :, 1], ACT.Ln, bias=g.eps(LN_EPS)).then_inc(logged, 1)
            act.wait_ge(logged, 1)
            nc.scalar.activation(rstd[:, :], rstd[:, :], ACT.Exp, scale=-0.5).then_inc(rooted, 1)
            w.more_rounds(act, empty)

        @block.gpsimd
        def _(pool):
            pool.wait_ge(ws_loaded, 16)
            nc.gpsimd.affine_select(out=ws[:, :, :], in_=ws[:, :, :], compare_op=ALU.is_ge, fill=0.0, base=0,
                                    pattern=[[0, NH], [1, CH]], channel_multiplier=-1).then_inc(ws_masked, 1)
            w.splits(pool)

        @block.vector
        def _(dve):
            for k in range(KD):
                dve.wait_ge(gv_rounded, k + 1)
                nc.vector.tensor_tensor(wgv_parts[:, 1, k, :], wgv[:, k % 2, :], wgv_parts[:, 0, k, :].bitcast(F32), ALU.subtract)\
                    .then_inc(gv_split, 1)
            for c in range(NC):
                dve.wait_ge(gelued, c + 1)
                nc.vector.bn_stats(stats[:, c, :], gv[:, c, :]).then_inc(stat, 1)
                dve.wait_ge(stat, c + 1)
                nc.vector.bn_aggr(mv[:, c, :], stats[:, c, :]).then_inc(aggregated, 1)
            dve.wait_ge(rooted, 1)
            for c in range(NC):
                nc.vector.tensor_scalar(gv[:, c, :], gv[:, c, :], mv[:, c, 0:1], rstd[:, c:c + 1], ALU.subtract, ALU.mult).then_inc(normed, 1)
            dve.wait_ge(ln_loaded, 16)
            for c in range(NC):
                dve.wait_ge(normed, c + 1)
                nc.vector.tensor_tensor(gv[:, c, :], gv[:, c, :], ln[:, 0, :], ALU.mult).then_inc(scaled, 1)
            for c in range(NC):
                dve.wait_ge(scaled, c + 1)
                nc.vector.tensor_tensor(gv[:, c, :], gv[:, c, :], ln[:, 1, :], ALU.add).then_inc(shifted, 1)
            dve.wait_ge(bs_loaded, 16)
            for u in range(2):
                dve.wait_ge(free[u], 3)
            for c in range(NC):
                dve.wait_ge(mixed, c + 1)
                if c >= 2:
                    dve.wait_ge(gated, c - 1)
                nc.vector.tensor_tensor(t[:, c % 2, :], ps[:, 4 + c % 2, :], bs[:, :, :].rearrange("p j t -> p (j t)"), ALU.add).then_inc(biased, 1)
                dve.wait_ge(biased, c + 1)
                u = g.y[:, 4:8, c * CH:(c + 1) * CH]
                nc.vector.tensor_tensor(u, t[:, c % 2, :].rearrange("p (j t) -> p j t", j=NP), u, ALU.mult).then_inc(gated, 1)


def latent_phase(nc, g, l, h, lat, kr):
    with ExitStack() as ctx:
        def sb(name, *shape):
            return ctx.enter_context(nc.sbuf_tensor(name, [P, *shape], F32))

        w = Stream(nc, g, ctx, "la", g.d_wt, l * N_WT + T_LAT, N_LAT)
        sq, rstd, turned = sb("lat_sq", 2, T), sb("lat_rstd", 2, T), sb("turned", T)
        acc = g.y[:, 8:10, :]
        ps = g.ps
        free = [g.loop_sems(f"la_free{u}")[0] for u in range(2)]
        squared, used = ([g.loop_sems(f"la_{n}{u}")[0] for u in range(2)] for n in ("squared", "used"))
        summed, logged, rooted, rot = g.sems("la_summed la_logged la_rooted la_rot")
        g.start()
        block = ctx.enter_context(nc.Block())

        @block.sync
        def _(sp):
            w.loads(sp)

        @block.gpsimd
        def _(pool):
            w.splits(pool)

        @block.tensor
        def _(pe):
            w.project(pe, h, (0, 2), free)
            for n in range(2):
                pe.wait_ge(used[0], 3 + n)
                pe.wait_ge(used[1], 3)
                for b in range(2):
                    mm = nc.tensor.matmul(ps[:, 4 + 2 * n + b, :], g.ones[:, :], acc[:, n, b * HALF:(b + 1) * HALF], start=True, stop=True)
                mm.then_inc(summed, 1)

        @block.scalar
        def _(act):
            def empty(i, u):
                act.wait_ge(used[u], i + 1)
                nc.scalar.activation(sq[:, u, :], two(ps, 2 * u), ACT.Square).then_inc(squared[u], 1)
                nc.scalar.activation(row(lat, i * 2 + u), two(ps, 2 * u), ACT.Copy).then_inc(free[u], 1)

            w.rounds(act, empty)
            for n, width in ((0, Q_LORA), (1, KV_LORA)):
                act.wait_ge(summed, n + 1)
                nc.scalar.activation(rstd[:, n, :], ps[:, 4 + 2 * n:6 + 2 * n, :].rearrange("p b n -> p (b n)"), ACT.Ln,
                                     scale=1.0 / width, bias=g.eps(NORM_EPS)).then_inc(logged, 1)
            for n in range(2):
                act.wait_ge(logged, 2)
                nc.scalar.activation(rstd[:, n, :], rstd[:, n, :], ACT.Exp, scale=-0.5).then_inc(rooted, 1)

        @block.vector
        def _(dve):
            for k in range(5):
                dve.wait_ge(squared[k % 2], k // 2 + 2)
                n = 0 if k < 3 else 1
                if k in (0, 3):
                    nc.vector.tensor_copy(acc[:, n, :], sq[:, k % 2, :]).then_inc(used[k % 2], 1)
                else:
                    dve.wait_ge(used[(k - 1) % 2], (k - 1) // 2 + 2)
                    nc.vector.tensor_tensor(acc[:, n, :], acc[:, n, :], sq[:, k % 2, :], ALU.add).then_inc(used[k % 2], 1)
            dve.wait_ge(free[1], 4)
            for u in range(2):
                nc.vector.tensor_tensor(kr[u][64:96, :], lat[64:96, 5, :], g.rope[64:96, :], ALU.mult).then_inc(rot, 1)
            nc.vector.tensor_tensor(turned[64:96, :], lat[96:128, 5, :], g.rope[96:128, :], ALU.mult).then_inc(rot, 1)
            dve.wait_ge(rot, 3)
            for u in range(2):
                nc.vector.tensor_tensor(kr[u][64:96, :], kr[u][64:96, :], turned[64:96, :], ALU.add)
            for n, (first, tiles, name) in enumerate(((0, 3, "q_norm"), (3, 2, "kv_norm"))):
                dve.wait_ge(rooted, n + 1)
                for k in range(tiles):
                    nc.vector.scalar_tensor_tensor(lat[:, first + k, :], lat[:, first + k, :], g.pcol(name, k), rstd[:, n, :], ALU.mult, ALU.mult)


def attention_phase(nc, g, l, lat, kr):
    with ExitStack() as ctx:
        def sb(name, *shape):
            return ctx.enter_context(nc.sbuf_tensor(name, [P, *shape], F32))

        hw = [sb(f"head_weights{u}", HALF) for u in range(2)]
        q = [sb(f"q_head{u}", T) for u in range(2)]
        wv, v, prob, pt = sb("wv", 2, BW), sb("v_all", NC, BW), sb("prob", 2, T), sb("prob_t", 2, NC, CH)
        turned = prob[:, 0, :]
        otok = g.y[:, 11, :].rearrange("p (c n) -> p c n", c=NC)
        mx, nm, den, rden = (sb(n, 2, NC) for n in ("row_max", "neg_max", "row_sum", "row_recip"))
        ps = g.ps
        hw_loaded = [g.sem(f"at_hw{u}") for u in range(2)]
        wv_loaded, = g.sems("at_wv")
        v_made, v_ready = g.sems("at_v_made at_v_ready")
        names = ("q_made", "k_made", "q_ready", "turn", "q_turned", "k_ready", "s_made", "masked", "maxed", "negated", "exped", "t_made",
                 "t_ready", "o_made", "recip", "o_ready", "y_made", "y_ready")
        s = dict(zip(names, g.loop_sems(*["at_" + n for n in names])))
        g.start()
        block = ctx.enter_context(nc.Block())
        UN = 2 * NC
        groups = [1 if m % NC < 4 else 2 for m in range(UN)]
        GT = sum(groups)

        @block.sync
        def _(sp):
            sp.dma_start(wv[:, :, :], g.d_wv[bass.ds(l, 1)].rearrange("o p k m -> p (o k) m")).then_inc(wv_loaded, 16)
            with sp.Fori(0, NP) as j:
                for u in range(2):
                    sp.wait_ge(s["k_made"], j * 2 + 1)
                    sp.dma_start(hw[u][:, :], g.d_whead[bass.ds(l * NH + 2 * j + u, 1)].rearrange("o p n -> p (o n)"))\
                        .then_inc(hw_loaded[u], 16)

        @block.tensor
        def _(pe):
            ident = g.con("ident")
            pe.wait_ge(wv_loaded, 16)
            for c in range(NC):
                if c >= 4:
                    pe.wait_ge(v_ready, c - 3)
                for k in range(2):
                    mm = nc.tensor.matmul(ps[:, 4 + c % 4, :], lat[:, 3 + k, c * CH:(c + 1) * CH], wv[:, k, :], start=k == 0, stop=k == 1)
                mm.then_inc(v_made, 1)
            pe.wait_ge(v_ready, NC)
            with pe.Fori(0, NP) as j:
                pe.wait_ge(s["o_ready"], j * UN + 1)
                pe.wait_ge(s["y_ready"], j * 2 + 1)
                for u in range(2):
                    pe.wait_ge(hw_loaded[u], j * 16 + 16)
                    if u:
                        pe.wait_ge(s["q_ready"], j * 2 + 2)
                        pe.wait_ge(s["turn"], j * 4 + 3)
                    for k in range(3):
                        for b in range(2):
                            mm = nc.tensor.matmul(ps[:, b, :], hw[u][:, k * P:(k + 1) * P], lat[:, k, b * HALF:(b + 1) * HALF],
                                                  start=k == 0, stop=k == 2)
                    mm.then_inc(s["q_made"], 1)
                    if u:
                        pe.wait_ge(s["k_ready"], j * 2 + 2)
                    for k in range(2):
                        for b in range(2):
                            mm = nc.tensor.matmul(ps[0:NOPE, 2 + b, :], hw[u][:, 3 * P + k * NOPE:3 * P + (k + 1) * NOPE],
                                                  lat[:, 3 + k, b * HALF:(b + 1) * HALF], start=k == 0, stop=k == 1)
                    mm.then_inc(s["k_made"], 1)

                def scores(m):
                    u, c = divmod(m, NC)
                    if c == 0:
                        pe.wait_ge(s["q_turned"], j * 2 + u + 2)
                        pe.wait_ge(s["k_ready"], j * 2 + u + 2)
                        pe.wait_ge(s["q_ready"], j * 2 + u + 2)
                    if m >= 2:
                        pe.wait_ge(s["exped"], j * UN + m)
                    n = (c + 1) * CH
                    for b in range((n + HALF - 1) // HALF):
                        w = min(HALF, n - b * HALF)
                        mm = nc.tensor.matmul(ps[:, 4 + 2 * (m % 2) + b, 0:w], q[u][0:QK, c * CH:(c + 1) * CH],
                                              kr[u][0:QK, b * HALF:b * HALF + w], start=True, stop=True)
                    mm.then_inc(s["s_made"], 1)

                def turn(m):
                    c = m % NC
                    pe.wait_ge(s["exped"], j * UN + m + 2)
                    if m == 0:
                        pe.wait_ge(s["k_ready"], j * 2 + 3)
                    for n in range(groups[m]):
                        last = max((k for k in range(m) if groups[k] > n), default=None)
                        if last is not None:
                            pe.wait_ge(s["t_ready"], j * GT + sum(groups[:last]) + n + 2)
                        for blk in range(4 * n, min(4 * n + 4, c + 1)):
                            mm = nc.tensor.transpose(ps[:, 2 + n, (blk % 4) * CH:(blk % 4 + 1) * CH],
                                                     prob[:, m % 2, blk * CH:(blk + 1) * CH], ident)
                        mm.then_inc(s["t_made"], 1)

                def values(m):
                    u, c = divmod(m, NC)
                    pe.wait_ge(s["t_ready"], j * GT + sum(groups[:m + 1]) + 1)
                    if m == 0:
                        pe.wait_ge(s["q_turned"], j * 2 + 3)
                        pe.wait_ge(s["q_ready"], j * 2 + 3)
                    if m >= 2:
                        pe.wait_ge(s["o_ready"], j * UN + m)
                    for blk in range(c + 1):
                        mm = nc.tensor.matmul(ps[:, m % 2, 0:HD], pt[:, m % 2, blk, :], v[:, blk, bass.ds(j * P + u * HD, HD)],
                                              start=blk == 0, stop=blk == c)
                    mm.then_inc(s["o_made"], 1)

                scores(0)
                for m in range(UN):
                    if m + 1 < UN:
                        scores(m + 1)
                    turn(m)
                    if m:
                        values(m - 1)
                values(UN - 1)
                pe.wait_ge(s["o_ready"], j * UN + UN + 1)
                for n in range(2):
                    for c in range(4 * n, 4 * n + 4):
                        mm = nc.tensor.transpose(ps[:, 2 + n, (c % 4) * CH:(c % 4 + 1) * CH], otok[:, c, :], ident)
                    mm.then_inc(s["y_made"], 1)

        def two(b0, rows):
            return ps[rows, b0:b0 + 2, :].rearrange("p b n -> p (b n)")

        @block.scalar
        def _(act):
            for c in range(NC):
                act.wait_ge(v_made, c + 1)
                nc.scalar.activation(v[:, c, :], ps[:, 4 + c % 4, :], ACT.Copy).then_inc(v_ready, 1)
            with act.Fori(0, NP) as j:
                for u in range(2):
                    act.wait_ge(s["q_made"], j * 2 + u + 2)
                    nc.scalar.activation(q[u][0:NOPE, :], two(0, slice(0, NOPE)), ACT.Copy).then_inc(s["q_ready"], 1)
                    act.wait_ge(s["k_made"], j * 2 + u + 2)
                    nc.scalar.activation(kr[u][0:NOPE, :], two(2, slice(0, NOPE)), ACT.Copy).then_inc(s["k_ready"], 1)
                for m in range(UN):
                    u, c = divmod(m, NC)
                    n = (c + 1) * CH
                    act.wait_ge(s["negated"], j * UN + m + 2)
                    if m >= 2:
                        act.wait_ge(s["t_made"], j * GT + sum(groups[:m - 1]) + 1)
                    nc.scalar.activation(prob[:, m % 2, 0:n], ps[:, 4 + 2 * (m % 2):6 + 2 * (m % 2), :].rearrange("p b n -> p (b n)")[:, 0:n],
                                         ACT.Exp, scale=SCALE, bias=nm[:, u, c:c + 1], accum_out=den[:, u, c:c + 1]).then_inc(s["exped"], 1)
                act.wait_ge(s["y_made"], j * 2 + 3)
                for n in range(2):
                    nc.scalar.activation(g.y[:, bass.ds(j + 8, 1), n * HALF:(n + 1) * HALF].rearrange("p o t -> p (o t)"), ps[:, 2 + n, :],
                                         ACT.Copy).then_inc(s["y_ready"], 1)

        @block.vector
        def _(dve):
            with dve.Fori(0, NP) as j:
                for u in range(2):
                    dve.wait_ge(s["q_made"], j * 2 + u + 2)
                    dve.wait_ge(s["q_turned"], j * 2 + u + 1)
                    nc.vector.tensor_tensor(q[u][64:96, :], two(0, slice(64, 96)), g.rope[64:96, :], ALU.mult).then_inc(s["turn"], 1)
                    nc.vector.tensor_tensor(turned[64:96, :], two(0, slice(96, 128)), g.rope[96:128, :], ALU.mult).then_inc(s["turn"], 1)
                    dve.wait_ge(s["turn"], j * 4 + 2 * u + 3)
                    nc.vector.tensor_tensor(q[u][64:96, :], q[u][64:96, :], turned[64:96, :], ALU.add).then_inc(s["q_turned"], 1)

                def rowmax(m):
                    u, c = divmod(m, NC)
                    both = ps[:, 4 + 2 * (m % 2):6 + 2 * (m % 2), :].rearrange("p b n -> p (b n)")
                    diag = both[:, c * CH:(c + 1) * CH]
                    dve.wait_ge(s["s_made"], j * UN + m + 2)
                    nc.vector.tensor_tensor(diag, diag, g.con("causal"), ALU.add).then_inc(s["masked"], 1)
                    dve.wait_ge(s["masked"], j * UN + m + 2)
                    nc.vector.reduce_max(mx[:, u, c:c + 1], both[:, 0:(c + 1) * CH], AX.X).then_inc(s["maxed"], 1)
                    dve.wait_ge(s["maxed"], j * UN + m + 2)
                    nc.vector.tensor_scalar(nm[:, u, c:c + 1], mx[:, u, c:c + 1], -SCALE, None, ALU.mult).then_inc(s["negated"], 1)

                def turned_blocks(m):
                    c = m % NC
                    for n in range(groups[m]):
                        dve.wait_ge(s["t_made"], j * GT + sum(groups[:m]) + n + 2)
                        w = min(4, c + 1 - 4 * n)
                        if m >= 2 and n == 0:
                            dve.wait_ge(s["o_made"], j * UN + m)
                        nc.vector.tensor_copy(pt[:, m % 2, 4 * n:4 * n + w, :].rearrange("p b t -> p (b t)"), ps[:, 2 + n, 0:w * CH])\
                            .then_inc(s["t_ready"], 1)

                def normalise(m):
                    u, c = divmod(m, NC)
                    nc.vector.reciprocal(rden[:, u, c:c + 1], den[:, u, c:c + 1]).then_inc(s["recip"], 1)
                    dve.wait_ge(s["recip"], j * UN + m + 2)
                    dve.wait_ge(s["o_made"], j * UN + m + 2)
                    nc.vector.tensor_scalar(otok[:, c, u * HD:(u + 1) * HD], ps[:, m % 2, 0:HD], rden[:, u, c:c + 1], None, ALU.mult)\
                        .then_inc(s["o_ready"], 1)

                rowmax(0)
                for m in range(UN):
                    if m + 1 < UN:
                        rowmax(m + 1)
                    turned_blocks(m)
                    if m:
                        normalise(m - 1)
                normalise(UN - 1)


def gate_phase(nc, g, l, h):
    with ExitStack() as ctx:
        w = Stream(nc, g, ctx, "ga", g.d_wt, l * N_WT + T_GATE, N_GATE)
        sig = ctx.enter_context(nc.sbuf_tensor("gate_sig", [P, 2, T], F32))
        t = ctx.enter_context(nc.sbuf_tensor("gate_silu", [P, 2, T], F32))
        free = [g.loop_sems(f"ga_free{u}")[0] for u in range(2)]
        sig_ready, gated = ([g.loop_sems(f"ga_{n}{u}")[0] for u in range(2)] for n in ("sig", "gated"))
        g.start()
        block = ctx.enter_context(nc.Block())

        @block.sync
        def _(sp):
            w.loads(sp)

        @block.gpsimd
        def _(pool):
            w.splits(pool)

        @block.tensor
        def _(pe):
            w.project(pe, h, (0, 2), free)

        @block.scalar
        def _(act):
            def empty(i, u):
                act.wait_ge(free[u], i + 1)
                nc.scalar.activation(sig[:, u, :], two(g.ps, 2 * u), ACT.Sigmoid).then_inc(sig_ready[u], 1)

            w.rounds(act, empty)

        @block.vector
        def _(dve):
            with dve.Fori(0, N_GATE // 2) as i:
                for u in range(2):
                    y = row(g.y, i * 2 + u)
                    dve.wait_ge(sig_ready[u], i + 2)
                    nc.vector.tensor_tensor(t[:, u, :], two(g.ps, 2 * u), sig[:, u, :], ALU.mult).then_inc(free[u], 1)
                    dve.wait_ge(free[u], i + 2)
                    nc.vector.tensor_tensor(y, y, t[:, u, :], ALU.mult).then_inc(gated[u], 1)


def merge_phase(nc, g, l, h, mixed):
    with ExitStack() as ctx:
        raw = ctx.enter_context(nc.sbuf_tensor("merge_raw", [P, 2, KD, P], F32))
        parts = ctx.enter_context(nc.sbuf_tensor("merge_parts", [P, 2, 2, KD, P], F32R))
        branch = ctx.enter_context(nc.sbuf_tensor("branch_slots", [P, 2, 4, P], F32))
        sig = ctx.enter_context(nc.sbuf_tensor("merge_sig", [P, 2, T], F32))
        t = ctx.enter_context(nc.sbuf_tensor("merge_term", [P, 2, T], F32))
        loaded, b_loaded = ([g.sem(f"me_{n}{u}") for u in range(2)] for n in ("w", "b"))
        names = ("rounded", "split", "gate_made", "made", "sig", "term", "added")
        s = dict(zip(names, g.loop_sems(*["me_" + n for n in names])))
        g.start()
        block = ctx.enter_context(nc.Block())
        UN = 2 * NBR

        @block.sync
        def _(sp):
            with sp.Fori(0, KD // 2) as i:
                for m in range(UN):
                    def source(d):
                        return d[bass.ds(l * (NBR * KD) + i * UN + m, 1)].rearrange("o p k m -> p (o k) m")

                    sp.wait_ge(s["split"], i * UN + max(m, 1))
                    sp.dma_start(raw[:, m % 2], source(g.d_wg)).then_inc(loaded[m % 2], 16)
                    sp.wait_ge(s["made"], i * UN + max(m, 1))
                    sp.dma_start(branch[:, m % 2], source(g.d_wb)).then_inc(b_loaded[m % 2], 16)

        @block.gpsimd
        def _(pool):
            with pool.Fori(0, KD // 2) as i:
                for m in range(UN):
                    pool.wait_ge(s["rounded"], i * UN + m + 2)
                    nc.gpsimd.tensor_tensor(parts[:, m % 2, 1], raw[:, m % 2], parts[:, m % 2, 0].bitcast(F32), ALU.subtract)\
                        .then_inc(s["split"], 1)

        @block.tensor
        def _(pe):
            with pe.Fori(0, KD // 2) as i:
                for m in range(UN):
                    b0 = 4 * (m % 2)
                    pe.wait_ge(s["split"], i * UN + m + 2)
                    pe.wait_ge(s["term"], i * UN + max(m, 1))
                    for k in range(KD):
                        mm = products_of_parts(nc, k, lambda b: g.ps[:, b0 + b, :], lambda part: parts[:, m % 2, part, k, :], h)
                    mm.then_inc(s["gate_made"], 1)
                    pe.wait_ge(b_loaded[m % 2], i * 48 + 16 * (m // 2) + 16)
                    for k in range(4):
                        for b in range(2):
                            mm = nc.tensor.matmul(g.ps[:, b0 + 2 + b, :], branch[:, m % 2, k, :],
                                                  g.y[:, 4 * (m % NBR) + k, b * HALF:(b + 1) * HALF], start=k == 0, stop=k == 3)
                    mm.then_inc(s["made"], 1)

        @block.scalar
        def _(act):
            with act.Fori(0, KD // 2) as i:
                for m in range(UN):
                    act.wait_ge(loaded[m % 2], i * 48 + 16 * (m // 2) + 16)
                    act.wait_ge(s["gate_made"], i * UN + max(m, 1))
                    nc.scalar.activation(parts[:, m % 2, 0], raw[:, m % 2], ACT.Copy).then_inc(s["rounded"], 1)
                    if m == 0:
                        continue
                    act.wait_ge(s["gate_made"], i * UN + m + 1)
                    act.wait_ge(s["term"], i * UN + max(m - 1, 1))
                    nc.scalar.activation(sig[:, (m - 1) % 2, :], two(g.ps, 4 * ((m - 1) % 2)), ACT.Sigmoid).then_inc(s["sig"], 1)
                act.wait_ge(s["gate_made"], i * UN + UN + 1)
                act.wait_ge(s["term"], i * UN + UN - 1)
                nc.scalar.activation(sig[:, 1, :], two(g.ps, 4), ACT.Sigmoid).then_inc(s["sig"], 1)

        @block.vector
        def _(dve):
            with dve.Fori(0, KD // 2) as i:
                for m in range(UN):
                    d, n = divmod(m, NBR)
                    out = row(mixed, i * 2 + d)
                    dve.wait_ge(s["sig"], i * UN + m + 2)
                    dve.wait_ge(s["made"], i * UN + m + 2)
                    if n == 0:
                        nc.vector.tensor_tensor(out, two(g.ps, 4 * (m % 2) + 2), sig[:, m % 2, :], ALU.mult).then_inc(s["term"], 1)
                    else:
                        nc.vector.tensor_tensor(t[:, n - 1, :], two(g.ps, 4 * (m % 2) + 2), sig[:, m % 2, :], ALU.mult).then_inc(s["term"], 1)
                        dve.wait_ge(s["term"], i * UN + m + 2)
                        if n == 2:
                            dve.wait_ge(s["added"], i * 4 + 2 * d + 2)
                        nc.vector.tensor_tensor(out, out, t[:, n - 1, :], ALU.add).then_inc(s["added"], 1)


def out_phase(nc, g, l, h, mixed):
    with ExitStack() as ctx:
        w = Stream(nc, g, ctx, "ou", g.d_wo, l * KD, KD)
        acc, rstd = (ctx.enter_context(nc.sbuf_tensor(n, [P, T], F32)) for n in ("o_acc", "o_rstd"))
        sq = ctx.enter_context(nc.sbuf_tensor("o_sq", [P, 2, T], F32))
        x, o = g.y, mixed
        free = [g.loop_sems(f"ou_free{u}")[0] for u in range(2)]
        x_loaded, summed, logged, rooted, scaled, updated, stored, m_rounded, m_split, x_squared, x_summed = g.sems(
            "ou_x_loaded ou_summed ou_logged ou_rooted ou_scaled ou_updated ou_stored ou_m_rounded ou_m_split x_squared x_summed")
        squared, added = g.loop_sems("ou_squared", "ou_added")
        late_updated = g.sem("ou_late_updated")
        g.start()
        block = ctx.enter_context(nc.Block())
        on_pool = (1, 4, 6)
        update = {}
        for k in range(KD):
            sem = late_updated if k in on_pool else updated
            update[k] = (sem, sum(1 for n in range(k + 1) if (n in on_pool) == (k in on_pool)))

        @block.sync
        def _(sp):
            for u in range(2):
                w.load(sp, 0, u)
            sp.dma_start(x[:, 0:KD, :], g.d_out).then_inc(x_loaded, 16)
            w.more_loads(sp)
            sp.wait_ge(x_loaded, 16)
            for k in range(KD):
                sp.wait_ge(*update[k])
                sp.dma_start(g.d_out[:, k, :], x[:, k, :]).then_inc(stored, 16)
            sp.wait_ge(stored, 16 * KD)

        @block.gpsimd
        def _(pool):
            w.splits(pool)
            pool.wait_ge(x_loaded, 16)
            for k in on_pool:
                pool.wait_ge(scaled, k + 2)
                nc.gpsimd.tensor_tensor(x[:, k, :], x[:, k, :], o[:, k, :], ALU.add).then_inc(late_updated, 1)

        @block.tensor
        def _(pe):
            for u in range(2):
                pe.wait_ge(w.split_done[u], 1)
            for k in range(KD):
                pe.wait_ge(m_split, k + 1)
                for u in range(2):
                    mm = w.products(k, u, h, (0, 2))
                    if k == KD - 1:
                        mm.then_inc(w.done[u], 1)
            w.project(pe, h, (0, 2), free, 1)
            pe.wait_ge(added, KD + 1)
            for b in range(2):
                mm = nc.tensor.matmul(g.ps[:, 4 + b, :], g.ones[:, :], acc[:, b * HALF:(b + 1) * HALF], start=True, stop=True)
            mm.then_inc(summed, 1)
            sum_of_squares(nc, g, pe, sq, x_squared, x_summed)

        @block.scalar
        def _(act):
            for u in range(2):
                w.round(act, 0, u)
            for k in range(KD):
                nc.scalar.activation(h[:, 0, k, :], mixed[:, k, :], ACT.Copy).then_inc(m_rounded, 1)
            act.wait_ge(m_split, KD)

            def empty(i, u):
                act.wait_ge(added, i * 2 + (u + 1))
                nc.scalar.activation(sq[:, 0, :], two(g.ps, 2 * u), ACT.Square).then_inc(squared, 1)
                nc.scalar.activation(row(o, i * 2 + u), two(g.ps, 2 * u), ACT.Copy).then_inc(free[u], 1)

            w.more_rounds(act, empty)
            act.wait_ge(summed, 1)
            nc.scalar.activation(rstd[:, :], two(g.ps, 4), ACT.Ln, scale=1.0 / D, bias=g.eps(NORM_EPS)).then_inc(logged, 1)
            act.wait_ge(logged, 1)
            nc.scalar.activation(rstd[:, :], rstd[:, :], ACT.Exp, scale=-0.5).then_inc(rooted, 1)
            for k in range(KD):
                act.wait_ge(*update[k])
                square(nc, g, act, sq, x, k, x_squared, x_summed)
            inverse_rms(nc, g, act, logged, 1, x_summed)

        @block.vector
        def _(dve):
            nc.vector.memset(acc[:, :], 0.0).then_inc(scaled, 1)
            for k in range(KD):
                dve.wait_ge(m_rounded, k + 1)
                nc.vector.tensor_tensor(h[:, 1, k, :], mixed[:, k, :], h[:, 0, k, :].bitcast(F32), ALU.subtract).then_inc(m_split, 1)
            dve.wait_ge(scaled, 1)
            with dve.Fori(0, KD) as i:
                dve.wait_ge(squared, i + 2)
                dve.wait_ge(added, i + 1)
                nc.vector.tensor_tensor(acc[:, :], acc[:, :], sq[:, 0, :], ALU.add).then_inc(added, 1)
            dve.wait_ge(rooted, 1)
            dve.wait_ge(x_loaded, 16)
            for k in range(KD):
                nc.vector.scalar_tensor_tensor(o[:, k, :], o[:, k, :], g.pcol("post", k), rstd[:, :], ALU.mult, ALU.mult).then_inc(scaled, 1)
                if k not in on_pool:
                    dve.wait_ge(scaled, k + 2)
                    nc.vector.tensor_tensor(x[:, k, :], x[:, k, :], o[:, k, :], ALU.add).then_inc(updated, 1)


def square(nc, g, act, sq, x, k, squared, summed):
    if k >= 2:
        act.wait_ge(summed, k - 1)
    nc.scalar.activation(sq[:, k % 2, :], x[:, k, :], ACT.Square).then_inc(squared, 1)


def sum_of_squares(nc, g, pe, sq, squared, summed):
    for k in range(KD):
        pe.wait_ge(squared, k + 1)
        for b in range(2):
            mm = nc.tensor.matmul(g.ps[:, 6 + b, :], g.ones[:, :], sq[:, k % 2, b * HALF:(b + 1) * HALF], start=k == 0, stop=k == KD - 1)
        mm.then_inc(summed, 1)


def inverse_rms(nc, g, act, logged, done, summed):
    act.wait_ge(summed, KD)
    nc.scalar.activation(g.y[:, 11, :], two(g.ps, 6), ACT.Ln, scale=1.0 / D, bias=g.eps(NORM_EPS)).then_inc(logged, 1)
    act.wait_ge(logged, done + 1)
    nc.scalar.activation(g.y[:, 11, :], g.y[:, 11, :], ACT.Exp, scale=-0.5)


def setup_phase(nc, g):
    C1 = 6.28125
    C2 = 0.0019350051879882812
    C3 = 2 * math.pi - C1 - C2
    MAGIC = 1.5 * 2 ** 23
    with ExitStack() as ctx:
        pos = ctx.enter_context(nc.sbuf_tensor("pos", [P, T], I32))
        ang, turns, rest = (ctx.enter_context(nc.sbuf_tensor(n, [P, T], F32)) for n in ("ang", "turns", "rest"))
        sq = ctx.enter_context(nc.sbuf_tensor("x_sq", [P, 2, T], F32))
        con_loaded, pos_loaded, x_copied, filled, step, zeroed, folded, roped, squared, summed, logged = g.sems(
            "con pos x_copied filled step zeroed folded roped squared summed logged")
        x_loaded = [g.sem(f"x_loaded{q}") for q in range(4)]
        zeros = ctx.enter_context(nc.sbuf_tensor("zeros", [P, NP, T], F32))
        g.start()
        block = ctx.enter_context(nc.Block())
        rows = slice(64, 128)

        @block.sync
        def _(sp):
            for q in range(4):
                sp.dma_start(g.y[:, 2 * q:2 * q + 2, :], g.d_x[:, 2 * q:2 * q + 2, :]).then_inc(x_loaded[q], 16)
            sp.dma_start(pos[rows, :], g.d_pos.partition_broadcast(64)).then_inc(pos_loaded, 16)
            sp.dma_start(g.consts[:, :], g.d_con).then_inc(con_loaded, 16)
            sp.wait_ge(zeroed, 1)
            sp.dma_start(g.d_v, zeros[:, :, :]).then_inc(g.v_stored, 16)
            for q in range(4):
                sp.wait_ge(x_loaded[q], 16)
            sp.dma_start(g.d_out, g.y[:, 0:KD, :]).then_inc(x_copied, 16)
            sp.wait_ge(con_loaded, 16)
            sp.wait_ge(x_copied, 16)
            sp.wait_ge(g.v_stored, 16)

        @block.tensor
        def _(pe):
            pe.wait_ge(filled, len(g.small_values) + 1)
            sum_of_squares(nc, g, pe, sq, squared, summed)

        @block.vector
        def _(dve):
            nc.vector.memset(g.ones[:, :], 1.0).then_inc(filled, 1)
            nc.vector.memset(zeros[:, :, :], 0.0).then_inc(zeroed, 1)
            for n, value in enumerate(g.small_values):
                nc.vector.memset(g.small[:, n:n + 1], value).then_inc(filled, 1)
            dve.wait_ge(con_loaded, 16)
            dve.wait_ge(pos_loaded, 16)
            n = [0]

            def chained(ins):
                n[0] += 1
                ins.then_inc(step, 1)
                dve.wait_ge(step, n[0])

            chained(nc.vector.tensor_copy(ang[rows, :], pos[rows, :]))
            chained(nc.vector.tensor_scalar(ang[rows, :], ang[rows, :], g.con("freq")[rows, :], None, ALU.mult))
            chained(nc.vector.tensor_scalar(turns[rows, :], ang[rows, :], 1.0 / (2 * math.pi), MAGIC, ALU.mult, ALU.add))
            chained(nc.vector.tensor_scalar(turns[rows, :], turns[rows, :], MAGIC, None, ALU.subtract))
            for part in (C1, C2, C3):
                chained(nc.vector.scalar_tensor_tensor(ang[rows, :], turns[rows, :], -part, ang[rows, :], ALU.mult, ALU.add))
            chained(nc.vector.tensor_scalar(rest[rows, :], ang[rows, :], 3.1415925, -3.1415925, ALU.min, ALU.max))
            chained(nc.vector.scalar_tensor_tensor(ang[64:96, :], rest[64:96, :], -1.0, rest[64:96, :], ALU.mult, ALU.min))
            nc.vector.tensor_scalar(rest[64:96, :], ang[64:96, :], math.pi / 2, None, ALU.add).then_inc(folded, 1)

        @block.scalar
        def _(act):
            for k in range(KD):
                act.wait_ge(x_loaded[k // 2], 16)
                square(nc, g, act, sq, g.y, k, squared, summed)
            act.wait_ge(filled, len(g.small_values) + 1)
            inverse_rms(nc, g, act, logged, 0, summed)
            act.wait_ge(folded, 1)
            nc.scalar.activation(g.rope[rows, :], rest[rows, :], ACT.Sin).then_inc(roped, 1)


def build(nc, d_x, d_pos, d_con, d_par, d_wt, d_up, d_wgv, d_gln, d_ws, d_bs, d_whead, d_wv, d_wg, d_wb, d_wo, d_out):
    g = Core()
    g.d_x, g.d_pos, g.d_con, g.d_par, g.d_wt, g.d_up, g.d_wgv, g.d_gln = d_x, d_pos, d_con, d_par, d_wt, d_up, d_wgv, d_gln
    g.d_ws, g.d_bs, g.d_whead, g.d_wv, g.d_wg, g.d_wb, g.d_wo, g.d_out = d_ws, d_bs, d_whead, d_wv, d_wg, d_wb, d_wo, d_out
    g.d_h = nc.dram_tensor("h_parts", (P, 2, KD, T), F32).ap()
    g.d_v = nc.dram_tensor("v_first", (P, NP, T), F32).ap()
    g.small_values = [NORM_EPS, GN_EPS, LN_EPS, 0.5 * KK_SHIFT * math.log(2.0)]
    with ExitStack() as ctx:
        def sb(name, *shape):
            return ctx.enter_context(nc.sbuf_tensor(name, [P, *shape], F32))

        g.y = sb("y", NBR * NP, T)
        g.consts, g.ones, g.rope, g.par = sb("consts", N_CON), sb("ones", P), sb("rope", T), sb("par", N_PAR)
        g.small = sb("small", len(g.small_values))
        g.ps = ctx.enter_context(nc.psum_tensor("ps", [P, 8, HALF], F32))
        g.con = lambda name: g.consts[:, CON[name][0]:CON[name][0] + CON[name][1]]
        g.pcol = lambda name, k: g.par[:, PAR[name] + k:PAR[name] + k + 1]
        g.eps = lambda value: g.small[:, g.small_values.index(value):g.small_values.index(value) + 1]

        pool = [ctx.enter_context(nc.semaphore(f"s{i}")) for i in range(40)]
        g.v_stored = ctx.enter_context(nc.semaphore("v_stored"))
        used, started = [], []

        def sem(name):
            used.append(pool[len(used)])
            return used[-1]

        g.sem = sem
        g.sems = lambda names: [sem(n) for n in names.split()]

        def loop_sems(*names):
            got = [sem(n) for n in names]
            started.extend(got)
            return got

        def start():
            for x in used:
                nc.sync.sem_clear(x)
            for x in started:
                nc.sync.sem_inc(x, 1)
            nc.all_engine_barrier()
            used.clear()
            started.clear()

        g.loop_sems, g.start = loop_sems, start
        setup_phase(nc, g)
        with nc.Fori(0, L) as l:
            with ExitStack() as rw:
                mix = rw.enter_context(nc.sbuf_tensor("mix", [P, N_RW, T], F32))
                ar = g.y[:, NP:NBR * NP, :].rearrange("p j t -> p (j t)").rearrange("p (j c x t) -> p j c x t", j=NP, c=NC, x=2)
                with nc.sbuf_tensor("h_first", [P, 2, KD, T], F32R, side="right") as h:
                    rwkv_project_phase(nc, g, l, h, mix)
                with ExitStack() as ch:
                    decay = ch.enter_context(nc.sbuf_tensor("decay", [P, NP, NC], F32))
                    v = ch.enter_context(nc.sbuf_tensor("v", [P, NP, T], F32))
                    rwkv_prepare_phase(nc, g, l, mix, ar, decay, v)
                    rwkv_chunk_phase(nc, g, l, mix, ar, decay, v)
                hs = ExitStack()
                h = hs.enter_context(nc.sbuf_tensor("h_again", [P, 2, KD, T], F32R, side="right"))
                rwkv_finish_phase(nc, g, l, mix, h)
            with hs:
                gmlp_phase(nc, g, l, h)
                with ExitStack() as at:
                    lat = at.enter_context(nc.sbuf_tensor("latents", [P, N_LAT, T], F32))
                    kr = [at.enter_context(nc.sbuf_tensor(f"k_head{u}", [P, T], F32)) for u in range(2)]
                    latent_phase(nc, g, l, h, lat, kr)
                    attention_phase(nc, g, l, lat, kr)
                gate_phase(nc, g, l, h)
                mixed = hs.enter_context(nc.sbuf_tensor("mixed", [P, KD, T], F32))
                merge_phase(nc, g, l, h, mixed)
                out_phase(nc, g, l, h, mixed)


def constants():
    con = np.zeros((P, N_CON), np.float32)

    def put(name, value):
        con[:, CON[name][0]:CON[name][0] + CON[name][1]] = value

    i, j = np.arange(P)[:, None], np.arange(P)[None, :]
    put("ident", i == j)
    put("blocks", i // HD == j // HD)
    put("amask", np.concatenate([i < j, i <= j, i < j, i <= j], 1))
    put("unit", (i % 2 == 0) & (j == i + 1))
    level = []
    for lev in range(1, 7):
        n = 1 << lev
        cols = np.arange(P).reshape(-1, 2, n)[:, 1, :].reshape(1, -1)
        level.append(i // n == cols // n - 1)
    put("level", np.concatenate(level, 1))
    put("causal", np.where(j <= i, 0.0, MASKED))
    put("restart", np.tile(np.arange(CH + 1) > 0, NC)[None, :])
    freq = (np.float32(1.0) / (np.float32(10000.0) ** (np.arange(0, ROPE, 2, dtype=np.float32) / np.float32(ROPE)))).astype(np.float32)
    column = np.zeros(P, np.float32)
    column[64:96] = np.tile(freq, 2)
    column[96:128] = np.concatenate([-freq, freq])
    put("freq", column[:, None])
    return con


def tiles(w):
    k, m = w.shape
    return w.reshape(k // P, P, m // P, P).transpose(2, 1, 0, 3)


def columns(v):
    return v.reshape(-1, P).T


def lay_out(x, positions, w_in, pre_norm, post_norm, rwkv_mu, rwkv_w0, rwkv_w_up, rwkv_a0, rwkv_a_up, rwkv_k_k, rwkv_k_a, rwkv_r_k,
            rwkv_ln_w, rwkv_ln_b, rwkv_v0, rwkv_v_down, rwkv_v_up, gmlp_ln_w, gmlp_ln_b, gmlp_w_s, gmlp_b_s, mla_q_norm, mla_w_uq,
            mla_kv_norm, mla_w_ukv, w_branch, w_out):
    z = lambda *shape: np.zeros(shape, np.float32)
    par, wt, up, wgv, gln, ws, bs, whead, wv, wg, wb, wo = ([] for _ in range(12))
    for l in range(L):
        v0 = rwkv_v0[l - 1] if l else z(BW)
        v_down = rwkv_v_down[l - 1] if l else z(D, V_LORA)
        v_up = rwkv_v_up[l - 1] if l else z(V_LORA, BW)
        par.append(np.concatenate([columns(a) for a in (
            pre_norm[l], post_norm[l], np.concatenate([rwkv_mu[l], z(P)]), rwkv_w0[l], rwkv_a0[l], rwkv_k_k[l], rwkv_k_a[l],
            rwkv_r_k[l].reshape(-1), rwkv_ln_w[l], rwkv_ln_b[l], v0, mla_q_norm[l], mla_kv_norm[l],
            np.full(P, 1.0 if l else 0.0, np.float32))], 1))
        w = w_in[l]
        kr = w[:, O_KR:O_KR + ROPE]
        half = ROPE // 2
        swap = lambda a: np.concatenate([a[:, half:], a[:, :half]], 1)
        wide = np.concatenate([w[:, :O_RWG], v_down, z(D, P - V_LORA), w[:, O_GU:O_GV], w[:, O_CQ:O_KR], z(D, 64), kr, swap(kr),
                               w[:, O_RWG:O_GU], w[:, O_GG:O_CQ], w[:, O_MG:O_MERGE]], 1)
        wt.append(tiles(wide))
        u = z(NP, P, 3, P)
        for j in range(NP):
            cols = slice(j * P, (j + 1) * P)
            u[j, :64, 0], u[j, 64:, 1], u[j, :V_LORA, 2] = rwkv_w_up[l][:, cols], rwkv_a_up[l][:, cols], v_up[:, cols]
        up.append(u)
        wgv.append(w[:, O_GV:O_GG].reshape(KD, P, BW).transpose(1, 0, 2))
        gln.append(np.broadcast_to(np.stack([gmlp_ln_w[l], gmlp_ln_b[l]])[None], (P, 2, BW)))
        ws.append(gmlp_w_s[l].transpose(2, 0, 1))
        bs.append(np.repeat(gmlp_b_s[l], HD, axis=0).reshape(NP, P, CH).transpose(1, 0, 2))
        uq = mla_w_uq[l].reshape(Q_LORA, NH, QK)
        ukv = mla_w_ukv[l].reshape(KV_LORA, NH, NOPE + HD)
        for h in range(NH):
            one = np.concatenate([uq[:, h], swap(uq[:, h, NOPE:])], 1)
            whead.append(np.concatenate([one.reshape(3, P, P).transpose(1, 0, 2).reshape(P, -1),
                                         ukv[:, h, :NOPE].reshape(2, P, NOPE).transpose(1, 0, 2).reshape(P, -1)], 1))
        wv.append(ukv[:, :, NOPE:].reshape(KV_LORA, BW).reshape(2, P, BW).transpose(1, 0, 2))
        gates = tiles(w[:, O_MERGE:]).reshape(NBR, KD, P, KD, P)
        branch = np.stack([tiles(w_branch[l, n]) for n in range(NBR)])
        wg.append(gates.transpose(1, 0, 2, 3, 4).reshape(KD * NBR, P, KD, P))
        wb.append(branch.transpose(1, 0, 2, 3, 4).reshape(KD * NBR, P, 4, P))
        wo.append(tiles(w_out[l]))
    cat = lambda a: np.ascontiguousarray(np.concatenate(a, 0))
    stack = lambda a: np.ascontiguousarray(np.stack(a, 0))
    return {
        "x": np.ascontiguousarray(x[0].T.reshape(KD, P, T).transpose(1, 0, 2)), "pos": np.ascontiguousarray(positions.reshape(1, T)),
        "con": constants(), "par": stack(par), "wt": cat(wt), "up": cat(up), "wgv": stack(wgv), "gln": stack(gln), "ws": stack(ws),
        "bs": stack(bs), "whead": stack(whead), "wv": stack(wv), "wg": cat(wg), "wb": cat(wb), "wo": cat(wo),
    }


def kernel(**inputs):
    import concourse.bacc as _bacc
    from concourse.bass_utils import run_bass_kernel_spmd as _run

    arrays = lay_out(**{k: np.asarray(v) for k, v in inputs.items()})
    nc = _bacc.Bacc("TRN2", target_bir_lowering=False, num_devices=1)
    args = {f"d_{k}": nc.dram_tensor(f"in_{k}", a.shape, mybir.dt.from_np(a.dtype), kind="ExternalInput").ap() for k, a in arrays.items()}
    out = nc.dram_tensor("out_x", (P, KD, T), F32, kind="ExternalOutput").ap()
    build(nc, d_out=out, **args)
    r = _run(nc, [{f"in_{k}": a for k, a in arrays.items()}], core_ids=[0])
    got = r.results[0]["out_x"]
    return np.ascontiguousarray(got.transpose(1, 0, 2).reshape(D, T).T)[None]
```

```python
import math
from contextlib import ExitStack

import numpy as np

import concourse.bass as bass
from concourse import mybir

F32 = mybir.dt.float32
F32R = mybir.dt.float32r
I32 = mybir.dt.int32
ACT = mybir.ActivationFunctionType
ALU = mybir.AluOpType
AX = mybir.AxisListType

P = 128
D = 1024
KD = D // P
T = 1024
HALF = 512
L = 2
BW = 512
NBR = 3
CH = 128
NC = T // CH
HD = 64
NH = 8
NP = NH // 2
W_LORA, A_LORA, V_LORA = 64, 64, 32
NOPE, ROPE = 64, 32
QK = NOPE + ROPE
Q_LORA, KV_LORA = 384, 256
NORM_EPS, GN_EPS, LN_EPS = 1e-6, 64e-5, 1e-5
DECAY = math.exp(-0.5)
KK_SHIFT = 16
SCALE = QK ** -0.5
MASKED = -1e30

SIZES = (3 * BW + W_LORA + A_LORA, BW, BW, BW, BW, Q_LORA, KV_LORA, ROPE, BW, NBR * D)
OFF = [0] + [int(o) for o in np.cumsum(SIZES)]
(O_RW, O_RWG, O_GU, O_GV, O_GG, O_CQ, O_CKV, O_KR, O_MG, O_MERGE) = OFF[:10]

N_RW = 14
T_GU = N_RW
T_LAT = T_GU + 4
N_LAT = 6
LAT_KV, LAT_KR, LAT_Q = 0, 2, 3
T_GATE = T_LAT + N_LAT
N_GATE = 12
T_MERGE = T_GATE + N_GATE
T_OUT = T_MERGE + NBR * KD
N_WT = T_OUT + KD

PAR = {}
_at = 0
for _name, _n in (("pre", 8), ("post", 8), ("mu", N_RW), ("w0", 4), ("a0", 4), ("k_k", 4), ("k_a", 4),
                  ("r_k", 4), ("ln_w", 4), ("ln_b", 4), ("v0", 4), ("q_norm", 3), ("kv_norm", 2), ("flag", 1)):
    PAR[_name] = _at
    _at += _n
N_PAR = _at

CON = {}
_at = 0
for _name, _n in (("ident", P), ("blocks", P), ("amask", 4 * P), ("unit", P), ("level", 6 * HD),
                  ("causal", P), ("restart", NC * (CH + 1)), ("freq", 1)):
    CON[_name] = (_at, _n)
    _at += _n
N_CON = _at


class Core:
    pass


def bc(ap, *shape):
    return ap.to_broadcast(list(shape))


def two(ps, b0, rows=slice(0, P)):
    return ps[rows, b0:b0 + 2, :].rearrange("p b n -> p (b n)")


def row(t, j):
    return t[:, bass.ds(j, 1), :].rearrange("p o t -> p (o t)")


class Stream:

    def __init__(self, nc, g, tag, slots, first, n, follows=False, leads=False):
        self.nc, self.g, self.first, self.n = nc, g, first, n
        self.raw, self.parts = slots
        self.follows, self.stop = follows, n // 2 + leads
        self.loaded, self.done = ([g.sem(f"{tag}_{name}{u}") for u in range(2)] for name in ("loaded", "done"))
        make = (lambda name: g.loop_sems(name)[0]) if follows else g.sem
        self.rounded, self.split_done = ([make(f"{tag}_{name}{u}") for u in range(2)] for name in ("rounded", "split"))

    def load(self, sp, i, u):
        sp.dma_start(self.raw[:, u], self.g.d_wt[bass.ds(self.first + 2 * i + u, 1)].rearrange("o p k m -> p (o k) m"))\
            .then_inc(self.loaded[u], 16)

    def loads(self, sp, after_first=None, between=None):
        if not self.follows:
            for u in range(2):
                self.load(sp, 0, u)
        if after_first:
            after_first()
        with sp.Fori(1, self.stop) as i:
            for u in range(2):
                sp.wait_ge(self.split_done[u], i)
                self.load(sp, i, u)
            if between:
                between(i)

    def round(self, act, i, u):
        act.wait_ge(self.loaded[u], i * 16 + (0 if self.follows else 16))
        self.nc.scalar.activation(self.parts[:, u, 0], self.raw[:, u], ACT.Copy).then_inc(self.rounded[u], 1)

    def first_rounds(self, act):
        if not self.follows:
            for u in range(2):
                self.round(act, 0, u)

    def more_rounds(self, act, empty, before_last=None):
        with act.Fori(0, self.stop - 1) as i:
            for u in range(2):
                act.wait_ge(self.done[u], i + 1)
                empty(i, u)
                self.round(act, i + 1, u)
        if before_last:
            before_last()
        if self.stop == self.n // 2:
            for u in range(2):
                act.wait_ge(self.done[u], self.stop)
                empty(self.stop - 1, u)

    def split(self, pool, i, u):
        pool.wait_ge(self.rounded[u], i + 1)
        self.nc.gpsimd.tensor_tensor(self.parts[:, u, 1], self.raw[:, u], self.parts[:, u, 0].bitcast(F32), ALU.subtract)\
            .then_inc(self.split_done[u], 1)

    def first_splits(self, pool):
        if not self.follows:
            for u in range(2):
                self.split(pool, 0, u)

    def more_splits(self, pool):
        with pool.Fori(1, self.stop) as i:
            for u in range(2):
                self.split(pool, i, u)

    def products(self, k, u, rhs, banks):
        return products_of_parts(self.nc, k, lambda b: self.g.ps[:, banks[u] + b, :], lambda part: self.parts[:, u, part, k, :], rhs)

    def project(self, pe, rhs, banks, free, first=0, stop=None):
        with pe.Fori(first, stop or self.n // 2) as i:
            for u in range(2):
                pe.wait_ge(self.split_done[u], i + 1)
                pe.wait_ge(free[u], i + 1)
                for k in range(KD):
                    mm = self.products(k, u, rhs, banks)
                mm.then_inc(self.done[u], 1)


def products_of_parts(nc, k, out, weights, rhs):
    for w, x in ((0, 0), (0, 1), (1, 0)):
        for b in range(2):
            mm = nc.tensor.matmul(out(b), weights(w), rhs[:, x, k, b * HALF:(b + 1) * HALF],
                                  start=k == 0 and (w, x) == (0, 0), stop=k == KD - 1 and w == 1)
    return mm


def rwkv_project_phase(nc, g, l, h, mix):
    with ExitStack() as ctx:
        raw = g.y[:, 8:10, :].rearrange("p u (k m) -> p u k m", k=KD)
        pieces = ((0, 1), (1, 2), (2, 4), (4, 6), (6, 8))
        x_loaded = [g.sem(f"x_loaded{n}") for n in range(len(pieces))]
        parts = ctx.enter_context(nc.sbuf_tensor("rp_parts", [P, 2, 2, KD, P], F32R))
        w = Stream(nc, g, "rp", (raw, parts), l * N_WT, N_RW)
        shifted = g.y[:, 4:8, :].rearrange("p a t -> p (a t)")[:, 0:2 * (T + 1)].rearrange("p (u t) -> p u t", u=2)
        diff = g.y[:, 0:2, :]
        x = g.y
        free, mixed = ([g.loop_sems(f"rp_{name}{u}")[0] for u in range(2)] for name in ("free", "mixed"))
        diffed = [g.sem(f"rp_diff{u}") for u in range(2)]
        par_loaded, zeroed, x_logged, x_rooted, scaled, rounded, even_split, odd_split, spilled = g.sems(
            "par_loaded rp_zeroed x_logged x_rooted h_scaled h_rounded h_even_split h_odd_split h_spilled")
        g.start()
        block = ctx.enter_context(nc.Block())

        @block.sync
        def _(sp):
            sp.dma_start(g.par[:, :], g.d_par[bass.ds(l, 1)].rearrange("o p n -> p (o n)")).then_inc(par_loaded, 16)

            def load_x():
                sp.wait_ge(g.x_copied, 16)
                for (first, last), sem in zip(pieces, x_loaded):
                    sp.dma_start(x[:, first:last, :], g.d_out[:, first:last, :]).then_inc(sem, 16)
                sp.wait_ge(even_split, KD // 2)
                sp.wait_ge(odd_split, KD // 2)

            def spill(k):
                sp.dma_start(g.d_h[:, :, bass.ds(k, 1), :], h[:, :, bass.ds(k, 1), :].bitcast(F32)).then_inc(spilled, 16)

            w.loads(sp, load_x, lambda i: spill(i - 1))
            for k in range(N_RW // 2 - 1, KD):
                spill(k)
            sp.wait_ge(spilled, 16 * KD)

        @block.gpsimd
        def _(pool):
            w.first_splits(pool)
            for k in range(1, KD, 2):
                pool.wait_ge(rounded, k + 1)
                nc.gpsimd.tensor_tensor(h[:, 1, k, :], mix[:, k, :], h[:, 0, k, :].bitcast(F32), ALU.subtract).then_inc(odd_split, 1)
            w.more_splits(pool)

        @block.tensor
        def _(pe):
            for u in range(2):
                pe.wait_ge(w.split_done[u], 1)
            for k in range(KD):
                pe.wait_ge(odd_split if k % 2 else even_split, k // 2 + 1)
                for u in range(2):
                    mm = w.products(k, u, h, (0, 2))
                    if k == KD - 1:
                        mm.then_inc(w.done[u], 1)
            w.project(pe, h, (0, 2), free, 1)

        @block.scalar
        def _(act):
            nc.scalar.activation(g.x_rstd[:, :], two(g.ps, 6), ACT.Ln, scale=1.0 / D, bias=g.eps(NORM_EPS)).then_inc(x_logged, 1)
            act.wait_ge(x_logged, 1)
            nc.scalar.activation(g.x_rstd[:, :], g.x_rstd[:, :], ACT.Exp, scale=-0.5).then_inc(x_rooted, 1)
            w.first_rounds(act)
            for k in range(KD):
                act.wait_ge(scaled, k + 1)
                nc.scalar.activation(h[:, 0, k, :], mix[:, k, :], ACT.Copy).then_inc(rounded, 1)

            def empty(i, u):
                act.wait_ge(mixed[u], i + 1)
                act.wait_ge(zeroed, 1)
                nc.scalar.activation(shifted[:, u, 1:T + 1], two(g.ps, 2 * u), ACT.Copy).then_inc(free[u], 1)

            w.more_rounds(act, empty)

        @block.vector
        def _(dve):
            dve.wait_ge(par_loaded, 16)
            dve.wait_ge(x_rooted, 1)
            for k in range(KD):
                dve.wait_ge(x_loaded[[k < last for _, last in pieces].index(True)], 16)
                nc.vector.scalar_tensor_tensor(mix[:, k, :], x[:, k, :], g.pcol("pre", k), g.x_rstd[:, :], ALU.mult, ALU.mult).then_inc(scaled, 1)
                if k % 2:
                    dve.wait_ge(rounded, k)
                    nc.vector.tensor_tensor(h[:, 1, k - 1, :], mix[:, k - 1, :], h[:, 0, k - 1, :].bitcast(F32), ALU.subtract)\
                        .then_inc(even_split, 1)
            dve.wait_ge(scaled, KD)
            nc.vector.memset(shifted[:, :, 0:1], 0.0).then_inc(zeroed, 1)
            dve.wait_ge(zeroed, 1)
            with dve.Fori(0, N_RW // 2) as i:
                for u in range(2):
                    dve.wait_ge(free[u], i + 2)
                    nc.vector.tensor_tensor(diff[:, u, :], shifted[:, u, 0:T], shifted[:, u, 1:T + 1], ALU.subtract).then_inc(diffed[u], 1)
                    dve.wait_ge(diffed[u], i + 1)
                    nc.vector.scalar_tensor_tensor(row(mix, i * 2 + u), diff[:, u, :], g.par[:, bass.ds(i * 2 + (u + PAR["mu"]), 1)],
                                                   shifted[:, u, 1:T + 1], ALU.mult, ALU.add).then_inc(mixed[u], 1)


def rwkv_prepare_phase(nc, g, l, mix, ar, decay, v):
    with ExitStack() as ctx:
        def sb(name, *shape):
            return ctx.enter_context(nc.sbuf_tensor(name, [P, *shape], F32))

        up = sb("up", 2, 3, P)
        sg, csum, em = (sb(n, 2, NC, CH + 1) for n in ("sg", "csum", "em"))
        cm, ep = sg, csum
        a, vg, fk, rk = (sb(n, 2, T) for n in ("a_gate", "v_gate", "fk", "rk"))
        kk, sq = g.y[:, 0:2, :], g.y[:, 2:4, :]
        rn = sq
        ps = g.ps
        names = ("tanhed", "zw_ready", "zv_ready", "sg_done", "csum_done", "cm_done", "e_done", "a_done", "vg_done", "vdiff",
                 "vgated", "v_done", "kk_raw", "sq_done", "kk_sum", "kk_max", "rn_ln", "rn_done", "f_done",
                 "k_done", "rk_done", "rk_sum", "zeroed", "b_done", "ar_done", "v_loaded")
        s = dict(zip(names, g.sems(" ".join("pp_" + n for n in names))))
        started = ("first_done", "step_done", "kk_done", "k_scaled")
        s.update(zip(started, g.loop_sems(*["pp_" + n for n in started])))
        up_loaded = [g.sem(f"pp_up{u}") for u in range(2)]
        g.start()
        block = ctx.enter_context(nc.Block())
        both = range(2)

        def chunks(ap):
            return ap.rearrange("p (c t) -> p c t", c=NC)

        def pcol(name, j):
            return g.par[:, bass.ds(j + PAR[name], 1)]


        @block.sync
        def _(sp):
            for i in range(NP // 2):
                for u in both:
                    if i:
                        sp.wait_ge(s["zv_ready"], i * 2 + u - 1)
                    sp.dma_start(up[:, u], g.d_up[bass.ds(l * NP + 2 * i + u, 1)].rearrange("o p a m -> p (o a) m")).then_inc(up_loaded[u], 16)
                if i == 0:
                    sp.dma_start(v[:, :, :], g.d_v).then_inc(s["v_loaded"], 16)
            sp.wait_ge(s["step_done"], NP // 2 + 1)
            sp.dma_start(g.d_v, v[:, :, :]).then_inc(g.v_stored, 16)

        @block.tensor
        def _(pe):
            pe.wait_ge(s["tanhed"], 1)
            with pe.Fori(0, NP // 2) as i:
                def project_up(u, parts):
                    for n in parts:
                        for b in range(2):
                            mm = nc.tensor.matmul(ps[:, 2 * n + b, :], up[:, u, n, :], mix[:, 13 if n == 2 else 12, b * HALF:(b + 1) * HALF],
                                                  start=True, stop=True)
                    return mm

                def head_sums(b0, src):
                    for b in range(2):
                        mm = nc.tensor.matmul(ps[:, b0 + b, :], g.con("blocks"), src[:, b * HALF:(b + 1) * HALF], start=True, stop=True)
                    return mm

                for u in both:
                    pe.wait_ge(up_loaded[u], i * 16 + 16)
                    if u:
                        pe.wait_ge(s["sg_done"], i * 2 + 1)
                    project_up(u, (0,)).then_inc(s["zw_ready"], 1)
                    pe.wait_ge(s["sq_done"], i * 2 + u + 1)
                    if u:
                        pe.wait_ge(s["kk_max"], i * 2 + 1)
                    else:
                        pe.wait_ge(s["first_done"], i + 1)
                    head_sums(6, sq[:, u, :]).then_inc(s["kk_sum"], 1)
                    if u:
                        pe.wait_ge(s["vg_done"], i * 2 + 1)
                    else:
                        pe.wait_ge(s["step_done"], i + 1)
                    project_up(u, (1, 2)).then_inc(s["zv_ready"], 1)
                for u in both:
                    pe.wait_ge(s["rk_done"], i * 2 + u + 1)
                    pe.wait_ge(s["vg_done" if u else "kk_max"], i * 2 + 2)
                    head_sums(4 if u else 6, rk[:, u, :]).then_inc(s["rk_sum"], 1)

        @block.scalar
        def _(act):
            nc.scalar.activation(mix[0:W_LORA, 12, :], mix[0:W_LORA, 12, :], ACT.Tanh).then_inc(s["tanhed"], 1)
            with act.Fori(0, NP // 2) as i:
                for u in both:
                    act.wait_ge(s["kk_done"], i * 2 + 1)
                    nc.scalar.activation(sq[:, u, :], row(mix, i * 2 + (u + 4)), ACT.Square, scale=pcol("k_k", i * 2 + u)).then_inc(s["sq_done"], 1)
                for u in both:
                    act.wait_ge(s["zw_ready"], i * 2 + u + 1)
                    act.wait_ge(s["zeroed"], i * 2 + u + 1)
                    nc.scalar.activation(sg[:, u, :, 1:CH + 1], chunks(two(ps, 0)), ACT.Sigmoid, bias=pcol("w0", i * 2 + u)).then_inc(s["sg_done"], 1)
                    act.wait_ge(s["zv_ready"], i * 2 + u + 1)
                    act.wait_ge(s["step_done"], i + 1)
                    nc.scalar.activation(a[:, u, :], two(ps, 2), ACT.Sigmoid, bias=pcol("a0", i * 2 + u)).then_inc(s["a_done"], 1)
                    nc.scalar.activation(kk[:, u, :], row(mix, i * 2 + (u + 4)), ACT.Copy, scale=pcol("k_k", i * 2 + u)).then_inc(s["kk_raw"], 1)
                    nc.scalar.activation(vg[:, u, :], two(ps, 4), ACT.Sigmoid, bias=pcol("v0", i * 2 + u)).then_inc(s["vg_done"], 1)
                for u in both:
                    act.wait_ge(s["kk_max"], i * 2 + u + 1)
                    nc.scalar.activation(rn[:, u, :], rn[:, u, :], ACT.Ln, scale=float(2 ** KK_SHIFT)).then_inc(s["rn_ln"], 1)
                for u in both:
                    act.wait_ge(s["rn_ln"], i * 2 + u + 1)
                    nc.scalar.activation(rn[:, u, :], rn[:, u, :], ACT.Exp, scale=-0.5, bias=g.eps(0.5 * KK_SHIFT * math.log(2.0)))\
                        .then_inc(s["rn_done"], 1)
                for u in both:
                    act.wait_ge(s["cm_done"], i * 2 + u + 1)
                    act.wait_ge(s["k_scaled"], i * 2 + 1)
                    nc.scalar.activation(ep[:, u], cm[:, u], ACT.Exp, scale=-DECAY)
                    nc.scalar.activation(em[:, u], cm[:, u], ACT.Exp, scale=DECAY).then_inc(s["e_done"], 1)

        @block.gpsimd
        def _(pool):
            pool.wait_ge(s["v_loaded"], 16)
            with pool.Fori(0, NP // 2) as i:
                for u in both:
                    pool.wait_ge(s["step_done"], i + 1)
                    nc.gpsimd.tensor_tensor(rk[:, u, :], row(v, i * 2 + u), row(mix, i * 2 + (u + 8)), ALU.subtract).then_inc(s["vdiff"], 1)
                for u in both:
                    pool.wait_ge(s["vdiff"], i * 2 + u + 1)
                    pool.wait_ge(s["vg_done"], i * 2 + u + 1)
                    nc.gpsimd.tensor_tensor(vg[:, u, :], rk[:, u, :], vg[:, u, :], ALU.mult).then_inc(s["vgated"], 1)
                for u in both:
                    pool.wait_ge(s["kk_done"], i * 2 + u + 2)
                    pool.wait_ge(s["f_done"], i * 2 + u + 1)
                    nc.gpsimd.tensor_tensor(a[:, u, :], a[:, u, :], kk[:, u, :], ALU.mult).then_inc(s["b_done"], 1)
                for u in both:
                    pool.wait_ge(s["e_done"], i * 2 + u + 1)
                    pool.wait_ge(s["rk_done"], i * 2 + u + 1)
                    k = row(mix, i * 2 + (u + 4))
                    nc.gpsimd.tensor_tensor(chunks(k), em[:, u, :, 1:CH + 1], chunks(k), ALU.mult).then_inc(s["k_scaled"], 1)

        @block.vector
        def _(dve):
            for u in both:
                nc.vector.memset(sg[:, u, :, 0:1], 0.0).then_inc(s["zeroed"], 1)
            with dve.Fori(0, NP // 2) as i:
                dve.wait_ge(s["step_done"], i + 1)
                for u in both:
                    dve.wait_ge(s["kk_sum"], i * 2 + u + 1)
                    nc.vector.tensor_scalar(rn[:, u, :], two(ps, 6), 1e-24, None, ALU.max).then_inc(s["kk_max"], 1)
                for u in both:
                    dve.wait_ge(s["sg_done"], i * 2 + u + 1)
                    nc.vector.tensor_tensor_scan(csum[:, u].rearrange("p c t -> p (c t)"), g.con("restart"),
                                                 sg[:, u].rearrange("p c t -> p (c t)"), 0.0, ALU.mult, ALU.add).then_inc(s["csum_done"], 1)
                for u in both:
                    dve.wait_ge(s["csum_done"], i * 2 + u + 1)
                    nc.vector.tensor_tensor(cm[:, u], csum[:, u], bc(csum[:, u, :, CH // 2:CH // 2 + 1], P, NC, CH + 1), ALU.subtract)\
                        .then_inc(s["cm_done"], 1)
                for u in both:
                    dve.wait_ge(s["a_done"], i * 2 + u + 1)
                    nc.vector.tensor_scalar(fk[:, u, :], a[:, u, :], 1.0, pcol("k_a", i * 2 + u), ALU.subtract, ALU.mult).then_inc(s["f_done"], 1)
                for u in both:
                    dve.wait_ge(s["f_done"], i * 2 + u + 1)
                    dve.wait_ge(s["kk_raw"], i * 2 + u + 1)
                    k = row(mix, i * 2 + (u + 4))
                    nc.vector.scalar_tensor_tensor(k, fk[:, u, :], 1.0, k, ALU.add, ALU.mult).then_inc(s["k_done"], 1)
                for u in both:
                    dve.wait_ge(s["vgated"], i * 2 + u + 1)
                    nc.vector.scalar_tensor_tensor(row(v, i * 2 + u), vg[:, u, :], g.pcol("flag", 0), row(mix, i * 2 + (u + 8)), ALU.mult, ALU.add)\
                        .then_inc(s["v_done"], 1)
                for u in both:
                    dve.wait_ge(s["k_done"], i * 2 + u + 1)
                    dve.wait_ge(s["v_done"], i * 2 + u + 1)
                    nc.vector.scalar_tensor_tensor(rk[:, u, :], row(mix, i * 2 + u), pcol("r_k", i * 2 + u), row(mix, i * 2 + (u + 4)),
                                                   ALU.mult, ALU.mult).then_inc(s["rk_done"], 1)
                for u in both:
                    dve.wait_ge(s["kk_raw"], i * 2 + u + 1)
                    dve.wait_ge(s["rn_done"], i * 2 + u + 1)
                    nc.vector.tensor_tensor(kk[:, u, :], kk[:, u, :], rn[:, u, :], ALU.mult).then_inc(s["kk_done"], 1)
                for u in both:
                    dve.wait_ge(s["e_done"], i * 2 + u + 1)
                    dve.wait_ge(s["kk_done"], i * 2 + u + 2)
                    nc.vector.memset(sg[:, u, :, 0:1], 0.0).then_inc(s["zeroed"], 1)
                    arj = ar[:, bass.ds(i * 2 + u, 1)].rearrange("p o c x t -> p (o c) x t")
                    nc.vector.scalar_tensor_tensor(arj[:, :, 0, :], ep[:, u, :, 0:CH], -1.0, chunks(kk[:, u, :]), ALU.mult, ALU.mult)
                    nc.vector.tensor_tensor(arj[:, :, 1, :], ep[:, u, :, 1:CH + 1], chunks(row(mix, i * 2 + u)), ALU.mult).then_inc(s["ar_done"], 1)
                for u in both:
                    dve.wait_ge(s["b_done"], i * 2 + u + 1)
                    dve.wait_ge(s["ar_done"], i * 2 + u + 1)
                    dve.wait_ge(s["rk_done"], i * 2 + u + 1)
                    nc.vector.tensor_tensor(chunks(row(mix, i * 2 + u)), em[:, u, :, 1:CH + 1], chunks(a[:, u, :]), ALU.mult)
                    nc.vector.tensor_tensor(row(decay, i * 2 + u)[:, 0:NC - 1], ep[:, u, 0:NC - 1, CH], em[:, u, 1:NC, 0], ALU.mult)
                    dve.wait_ge(s["rk_sum"], i * 2 + u + 1)
                    nc.vector.tensor_tensor(row(mix, i * 2 + (u + 8)), two(ps, 4 if u else 6), row(v, i * 2 + u), ALU.mult)\
                        .then_inc(s["step_done" if u else "first_done"], 1)


def rwkv_chunk_phase(nc, g, l, mix, ar, decay, v):
    with ExitStack() as ctx:
        def sb(name, *shape):
            return ctx.enter_context(nc.sbuf_tensor(name, [P, *shape], F32))

        bp, kp = sb("b_padded", NP, 2, CH), sb("k_padded", NP, 2, CH)
        a_in, v_in, bk_in = sb("a_in", NP, CH), sb("v_in", NP, CH), sb("bk_in", 2, NP, CH)
        am = g.y[:, 0:NP, :].rearrange("p j t -> p (j t)").rearrange("p (h x t) -> p h x t", h=NH, x=4)
        ab, xi = (mix[:, n, :].rearrange("p (h t) -> p h t", h=NH) for n in (12, 13))
        gi = sb("inverse", NH, CH)
        zm = sb("z_masked", NH, CH // 2)
        bkt, vt = sb("bk_tokens", 2, NH, HD), sb("v_tokens", NH, HD)
        bt, kt = bkt[:, 0], bkt[:, 1]
        ws, us = sb("w_in_sbuf", NH, HD), sb("u_in_sbuf", NH, HD)
        st, st2, sbd = sb("state", NP, HD), sb("state_sum", NP, HD), sb("state_diag", NP, 2, HD)
        ps = g.ps
        names = ("staged", "a_staged", "t_made", "t_ready", "a_made", "a_masked", "ab_made", "ab_ready", "g_ready", "x_made",
                 "x_ready", "z_made", "z_masked", "dg_made", "w_made", "w_ready", "u_made", "u_ready", "s_made", "state_ready",
                 "y_made", "y_ready", "unit_done", "s_added", "s_scaled")
        s = dict(zip(names, g.loop_sems(*["rc_" + n for n in names])))
        zeroed, padded, copied = g.sems("rc_zeroed rc_padded rc_v_copied")
        g.start()
        block = ctx.enter_context(nc.Block())
        bf, kf = mix[:, 0:NP, :], mix[:, NP:2 * NP, :]
        yf = bf

        def tokens(c):
            return bass.ds(c * CH, CH)

        def n_rows(lev):
            return CH if lev < 6 else HD

        def odd(ap, n):
            return ap.rearrange("p h (b two n) -> p h b two n", two=2, n=n)[:, :, :, 1, :]

        A_BANKS = (2, 6, 7)

        @block.sync
        def _(sp):
            sp.wait_ge(g.v_stored, l * 16 + 32)
            sp.sem_inc(copied, 1)

        @block.gpsimd
        def _(pool):
            pool.wait_ge(padded, 2)
            with pool.Fori(0, NC) as c:
                pool.wait_ge(s["a_staged"], c + 1)
                pool.wait_ge(s["a_made"], c * NH + 1)
                for half in range(2):
                    rows = slice(half * HD, half * HD + HD)
                    pool.wait_ge(s["staged"], c * 7 + 2 * half + 1)
                    nc.gpsimd.tensor_copy(bp[rows, :, half, :], bf[rows, :, tokens(c)]).then_inc(s["staged"], 1)
                    nc.gpsimd.tensor_copy(kp[rows, :, half, :], kf[rows, :, tokens(c)]).then_inc(s["staged"], 1)
                pool.wait_ge(s["staged"], c * 7 + 5)
                pool.wait_ge(s["t_made"], c * 3 + 1)
                nc.gpsimd.tensor_copy(v_in[:, :, :], v[:, :, tokens(c)]).then_inc(s["staged"], 1)
                for n, src in enumerate((bf, kf)):
                    nc.gpsimd.tensor_copy(bk_in[:, n, :, :], src[:, :, tokens(c)]).then_inc(s["staged"], 1)
                pool.wait_ge(s["staged"], c * 7 + 8)
                pool.wait_ge(s["w_made"], c + 1)
                nc.gpsimd.tensor_copy(a_in[:, :, :], ar[:, :, bass.ds(c, 1), 0, :].rearrange("p j o t -> p j (o t)")).then_inc(s["a_staged"], 1)

        @block.tensor
        def _(pe):
            ident = g.con("ident")
            with pe.Fori(0, NC) as c:
                def token_major():
                    pe.wait_ge(s["staged"], c * 7 + 8)
                    pe.wait_ge(s["w_ready"], c + 1)
                    pe.wait_ge(s["u_ready"], c + 1)
                    for bank, tiles in ((5, v_in), (3, bk_in[:, 0]), (4, bk_in[:, 1])):
                        for j in range(NP):
                            mm = nc.tensor.transpose(ps[:, bank, j * P:(j + 1) * P], tiles[:, j, :], ident)
                        mm.then_inc(s["t_made"], 1)

                def transpose_a(q):
                    pe.wait_ge(s["a_masked"], c * NH + 4 * q + 5)
                    pe.wait_ge(s["s_added" if q else "y_ready"], c + 1)
                    for h in range(4 * q, 4 * q + 4):
                        mm = nc.tensor.transpose(ps[:, q, (h % 4) * CH:(h % 4 + 1) * CH], am[:, h, 0, :], ident)
                    mm.then_inc(s["ab_made"], 1)

                pe.wait_ge(s["staged"], c * 7 + 5)
                for h in range(NH):
                    if h >= 3:
                        pe.wait_ge(s["a_masked"], c * NH + h - 1)
                    bank = A_BANKS[h % 3]
                    moving = ar[:, h // 2, bass.ds(c, 1), :, :].rearrange("p o x t -> p (o x t)")
                    nc.tensor.matmul(ps[:, bank, 0:2 * CH], bp[:, h // 2, h % 2, :], moving, start=True, stop=True)
                    nc.tensor.matmul(ps[:, bank, 2 * CH:4 * CH], kp[:, h // 2, h % 2, :], moving, start=True, stop=True).then_inc(s["a_made"], 1)
                    if h == 5:
                        transpose_a(0)
                token_major()
                transpose_a(1)

                def make_w():
                    pe.wait_ge(s["a_staged"], c + 2)
                    pe.wait_ge(s["t_ready"], c * 3 + 4)
                    pe.wait_ge(s["state_ready"], c + 1)
                    for j in range(NP):
                        nc.tensor.matmul(ps[:, 4, j * P:(j + 1) * P], a_in[:, j, :], sbd[:, j, :, :].rearrange("p h i -> p (h i)"),
                                         start=j == 0, stop=False, skip_group_check=True)
                    for h in range(NH):
                        mm = nc.tensor.matmul(ps[:, 4, h * HD:(h + 1) * HD], am[:, h, 2, :], vt[:, h, :], start=False, stop=h == NH - 1,
                                              skip_group_check=True)
                    mm.then_inc(s["w_made"], 1)

                def make_xz(lev, q):
                    n = 1 << lev
                    pe.wait_ge(s["g_ready"], c * 14 + 2 * (lev - 1) + q + 2)
                    for h in range(4 * q, 4 * q + 4):
                        mm = nc.tensor.transpose(ps[:, 6 + q, (h % 4) * CH:(h % 4 + 1) * CH], gi[:, h, :], ident)
                    mm.then_inc(s["x_made"], 1)
                    if lev == 1:
                        pe.wait_ge(s["ab_ready"], c * 2 + q + 2)
                    for h in range(4 * q, 4 * q + 4):
                        mm = nc.tensor.matmul(ps[0:n_rows(lev), q, (h % 4) * HD:(h % 4 + 1) * HD], ab[:, h, 0:n_rows(lev)],
                                              odd(gi[:, h:h + 1, :], n).rearrange("p o b n -> p (o b) n"), start=True, stop=True)
                    mm.then_inc(s["z_made"], 1)

                def make_dg(lev, q):
                    pe.wait_ge(s["z_masked"], c * 12 + 2 * (lev - 1) + q + 2)
                    pe.wait_ge(s["x_ready"], c * 12 + 2 * (lev - 1) + q + 2)
                    for h in range(4 * q, 4 * q + 4):
                        mm = nc.tensor.matmul(ps[0:n_rows(lev), 2 + q, (h % 4) * HD:(h % 4 + 1) * HD], xi[:, h, 0:n_rows(lev)], zm[:, h, :],
                                              start=True, stop=True)
                    mm.then_inc(s["dg_made"], 1)

                for lev in range(1, 7):
                    make_xz(lev, 0)
                    if lev == 1:
                        make_w()
                    else:
                        make_dg(lev - 1, 1)
                    make_dg(lev, 0)
                    make_xz(lev, 1)
                make_dg(6, 1)
                for j in range(NP):
                    nc.tensor.matmul(ps[:, 0, j * P:(j + 1) * P], sbd[:, j, :, :].rearrange("p h i -> p (h i)"),
                                     ar[:, j, bass.ds(c, 1), 1, :].rearrange("p o t -> p (o t)"), start=j == 0, stop=False,
                                     skip_group_check=True)

                def y_part(values, which, last):
                    for h in range(NH):
                        rows = slice((h % 2) * HD, (h % 2) * HD + HD)
                        mm = nc.tensor.matmul(ps[rows, 0, (h // 2) * P:(h // 2 + 1) * P], values[:, h, :], am[:, h, which, :],
                                              start=False, stop=last, skip_group_check=True)
                    return mm

                def s_part(tok, values, first):
                    for h in range(NH):
                        rows = slice((h % 2) * HD, (h % 2) * HD + HD)
                        mm = nc.tensor.matmul(ps[rows, 1, (h // 2) * HD:(h // 2 + 1) * HD], tok[:, h, :], values[:, h, :],
                                              start=first and h < 2, stop=not first, skip_group_check=True)
                    return mm

                y_part(vt, 3, False)
                pe.wait_ge(s["w_ready"], c + 2)
                pe.wait_ge(s["g_ready"], c * 14 + 15)
                for h in range(NH):
                    mm = nc.tensor.matmul(ps[:, 5, h * HD:(h + 1) * HD], gi[:, h, :], ws[:, h, :], start=True, stop=True)
                mm.then_inc(s["u_made"], 1)
                s_part(kt, vt, True)
                pe.wait_ge(s["u_ready"], c + 2)
                s_part(bt, us, False).then_inc(s["s_made"], 1)
                y_part(us, 1, True).then_inc(s["y_made"], 1)

        @block.scalar
        def _(act):
            with act.Fori(0, NC) as c:
                def copy_a(q):
                    act.wait_ge(s["ab_made"], c * 2 + q + 2)
                    nc.scalar.activation(ab[:, 4 * q:4 * q + 4, :].rearrange("p h t -> p (h t)"), ps[:, q, :], ACT.Copy).then_inc(s["ab_ready"], 1)

                copy_a(0)
                act.wait_ge(s["t_made"], c * 3 + 2)
                nc.scalar.activation(vt[:, :, :].rearrange("p h i -> p (h i)"), ps[:, 5, :], ACT.Copy).then_inc(s["t_ready"], 1)
                for n in range(2):
                    act.wait_ge(s["t_made"], c * 3 + n + 3)
                    nc.scalar.activation(bkt[:, n, :, :].rearrange("p h i -> p (h i)"), ps[:, 3 + n, :], ACT.Copy).then_inc(s["t_ready"], 1)
                copy_a(1)
                for lev in range(6):
                    if lev == 1:
                        act.wait_ge(s["w_made"], c + 2)
                        nc.scalar.activation(ws[:, :, :].rearrange("p h i -> p (h i)"), ps[:, 4, :], ACT.Copy).then_inc(s["w_ready"], 1)
                    for q in range(2):
                        act.wait_ge(s["x_made"], c * 12 + 2 * lev + q + 2)
                        nc.scalar.activation(xi[:, 4 * q:4 * q + 4, :].rearrange("p h t -> p (h t)"), ps[:, 6 + q, :], ACT.Copy)\
                            .then_inc(s["x_ready"], 1)
                act.wait_ge(s["u_made"], c + 2)
                nc.scalar.activation(us[:, :, :].rearrange("p h i -> p (h i)"), ps[:, 5, :], ACT.Copy).then_inc(s["u_ready"], 1)
                act.wait_ge(s["y_made"], c + 2)
                nc.scalar.activation(yf[:, :, tokens(c)], ps[:, 0, :].rearrange("p (j t) -> p j t", j=NP), ACT.Copy).then_inc(s["y_ready"], 1)

        @block.vector
        def _(dve):
            nc.vector.memset(bp[:, :, :, :], 0.0).then_inc(padded, 1)
            nc.vector.memset(kp[:, :, :, :], 0.0).then_inc(padded, 1)
            nc.vector.memset(st[:, :, :], 0.0).then_inc(zeroed, 1)
            nc.vector.memset(decay[:, :, NC - 1:NC], 0.0).then_inc(zeroed, 1)
            nc.vector.memset(sbd[:, :, :, :], 0.0).then_inc(zeroed, 1)
            dve.wait_ge(zeroed, 3)
            amask = g.con("amask")
            with dve.Fori(0, NC) as c:
                for h in range(NH):
                    dve.wait_ge(s["a_made"], c * NH + h + 2)
                    if h == 0:
                        dve.wait_ge(s["y_made"], c + 1)
                    nc.vector.tensor_tensor(am[:, h, :, :].rearrange("p x t -> p (x t)"), ps[:, A_BANKS[h % 3], :], amask, ALU.mult)\
                        .then_inc(s["a_masked"], 1)
                for q in range(2):
                    heads = slice(4 * q, 4 * q + 4)
                    dve.wait_ge(s["a_masked"], c * NH + 4 * q + 5)
                    nc.vector.tensor_tensor(gi[:, heads, :], am[:, heads, 0, :], bc(g.con("unit").unsqueeze(1), P, 4, CH), ALU.mult)\
                        .then_inc(s["unit_done"], 1)
                    dve.wait_ge(s["unit_done"], c * 2 + q + 2)
                    nc.vector.tensor_tensor(gi[:, heads, :], gi[:, heads, :], bc(g.con("ident").unsqueeze(1), P, 4, CH), ALU.add)\
                        .then_inc(s["g_ready"], 1)

                def mask_z(lev, q):
                    mask = g.con("level")[:, (lev - 1) * HD:lev * HD]
                    dve.wait_ge(s["z_made"], c * 12 + 2 * (lev - 1) + q + 2)
                    nc.vector.tensor_tensor(zm[:, 4 * q:4 * q + 4, :], ps[:, q, 0:4 * HD].rearrange("p (h n) -> p h n", h=4),
                                            bc(mask.unsqueeze(1), P, 4, HD), ALU.mult).then_inc(s["z_masked"], 1)

                def add_dg(lev, q):
                    n = 1 << lev
                    dve.wait_ge(s["dg_made"], c * 12 + 2 * (lev - 1) + q + 2)
                    to = odd(gi[0:n_rows(lev), 4 * q:4 * q + 4, :], n)
                    nc.vector.tensor_tensor(to, ps[0:n_rows(lev), 2 + q, 0:4 * HD].rearrange("p (h b n) -> p h b n", h=4, n=n), to, ALU.add)\
                        .then_inc(s["g_ready"], 1)

                for lev in range(1, 7):
                    mask_z(lev, 0)
                    if lev > 1:
                        add_dg(lev - 1, 1)
                    add_dg(lev, 0)
                    mask_z(lev, 1)
                add_dg(6, 1)
                dve.wait_ge(s["s_made"], c + 2)
                dve.wait_ge(s["state_ready"], c + 1)
                nc.vector.tensor_tensor(st2[:, :, :], ps[:, 1, 0:NP * HD].rearrange("p (j i) -> p j i", j=NP), st[:, :, :], ALU.add)\
                    .then_inc(s["s_added"], 1)
                dve.wait_ge(s["s_added"], c + 2)
                nc.vector.tensor_tensor(st[:, :, :], st2[:, :, :], bc(decay[:, :, bass.ds(c, 1)], P, NP, HD), ALU.mult).then_inc(s["s_scaled"], 1)
                dve.wait_ge(s["s_scaled"], c + 2)
                nc.vector.tensor_copy(sbd[0:HD, :, 0, :], st[0:HD, :, :])
                nc.vector.tensor_copy(sbd[HD:P, :, 1, :], st[HD:P, :, :]).then_inc(s["state_ready"], 1)


def rwkv_finish_phase(nc, g, l, mix, h):
    with ExitStack() as ctx:
        yc = mix[:, NP:2 * NP, :]
        sq = ctx.enter_context(nc.sbuf_tensor("gn_sq", [P, NP, T], F32))
        ps = g.ps
        mean, centred, squared, var, logged, rooted, scaled = g.sems("gn_mean gn_centred gn_squared gn_var gn_logged gn_rooted gn_scaled")
        h_loaded = g.sem("h_loaded")
        g.start()
        block = ctx.enter_context(nc.Block())

        @block.sync
        def _(sp):
            sp.dma_start(h[:, :, :, :].bitcast(F32), g.d_h).then_inc(h_loaded, 16)
            sp.wait_ge(h_loaded, 16)

        @block.tensor
        def _(pe):
            def head_sums(j, src):
                for b in range(2):
                    mm = nc.tensor.matmul(ps[:, 2 * j + b, :], g.con("blocks"), src[:, b * HALF:(b + 1) * HALF], start=True, stop=True)
                return mm

            for j in range(NP):
                head_sums(j, mix[:, j, :]).then_inc(mean, 1)
            for j in range(NP):
                pe.wait_ge(squared, j + 1)
                head_sums(j, sq[:, j, :]).then_inc(var, 1)

        @block.scalar
        def _(act):
            for j in range(NP):
                act.wait_ge(centred, j + 1)
                nc.scalar.activation(sq[:, j, :], yc[:, j, :], ACT.Square).then_inc(squared, 1)
            for j in range(NP):
                act.wait_ge(var, j + 1)
                nc.scalar.activation(sq[:, j, :], two(ps, 2 * j), ACT.Ln, scale=1.0 / HD, bias=g.eps(GN_EPS)).then_inc(logged, 1)
            for j in range(NP):
                act.wait_ge(logged, j + 1)
                nc.scalar.activation(sq[:, j, :], sq[:, j, :], ACT.Exp, scale=-0.5).then_inc(rooted, 1)

        @block.vector
        def _(dve):
            for j in range(NP):
                dve.wait_ge(mean, j + 1)
                nc.vector.scalar_tensor_tensor(yc[:, j, :], two(ps, 2 * j), -1.0 / HD, mix[:, j, :], ALU.mult, ALU.add).then_inc(centred, 1)
            for j in range(NP):
                dve.wait_ge(rooted, j + 1)
                nc.vector.scalar_tensor_tensor(yc[:, j, :], yc[:, j, :], g.pcol("ln_w", j), sq[:, j, :], ALU.mult, ALU.mult).then_inc(scaled, 1)
                dve.wait_ge(scaled, j + 1)
                nc.vector.scalar_tensor_tensor(g.y[:, j, :], yc[:, j, :], g.pcol("ln_b", j), mix[:, 2 * NP + j, :], ALU.add, ALU.add)


def gmlp_phase(nc, g, l, h, slots):
    with ExitStack() as ctx:
        def sb(name, *shape):
            return ctx.enter_context(nc.sbuf_tensor(name, [P, *shape], F32))

        w = Stream(nc, g, "gu", slots, l * N_WT + T_GU, 4, leads=True)
        wgv = sb("gv_raw", 2, BW)
        wgv_parts = ctx.enter_context(nc.sbuf_tensor("gv_parts", [P, 2, KD, BW], F32R))
        gv = g.y[:, 8:12, :].rearrange("p a t -> p (a t)").rearrange("p (c n) -> p c n", c=NC)
        ln, ws, bs = sb("gmlp_ln", 2, BW), sb("mixing", NH, CH), sb("mixing_bias", NP, CH)
        stats, mv, rstd, t = sb("stats", NC, 6), sb("mean_var", NC, 2), sb("gv_rstd", NC), sb("mixed_v", 2, NP * CH)
        ps = g.ps
        free = [g.loop_sems(f"gu_free{u}")[0] for u in range(2)]
        gv_loaded = [g.sem(f"gv_loaded{u}") for u in range(2)]
        (gv_rounded, gv_split, ln_loaded, ws_loaded, bs_loaded, ws_masked, gv_made, gelued, stat, aggregated, logged, rooted, normed, scaled,
         shifted, mixed, biased, gated) = g.sems("gv_rounded gv_split ln_loaded ws_loaded bs_loaded ws_masked gv_made gelued stat aggregated "
                                                 "logged rooted normed scaled shifted mixed biased gated")
        g.start()
        block = ctx.enter_context(nc.Block())

        @block.sync
        def _(sp):
            for k in range(KD):
                if k >= 2:
                    sp.wait_ge(gv_split, k - 1)
                sp.dma_start(wgv[:, k % 2, :], g.d_wgv[bass.ds(l, 1), :, k, :].rearrange("o p m -> p (o m)")).then_inc(gv_loaded[k % 2], 16)
            sp.dma_start(ln[:, :, :], g.d_gln[bass.ds(l, 1)].rearrange("o p a n -> p (o a) n")).then_inc(ln_loaded, 16)
            sp.dma_start(ws[:, :, :], g.d_ws[bass.ds(l, 1)].rearrange("o p h t -> p (o h) t")).then_inc(ws_loaded, 16)
            sp.dma_start(bs[:, :, :], g.d_bs[bass.ds(l, 1)].rearrange("o p j t -> p (o j) t")).then_inc(bs_loaded, 16)
            w.loads(sp)

        @block.tensor
        def _(pe):
            def values(c, k):
                for x, part in ((0, 0), (1, 0), (0, 1)):
                    mm = nc.tensor.matmul(ps[:, 4 + c % 4, :], h[:, x, k, c * CH:(c + 1) * CH], wgv_parts[:, part, k, :],
                                          start=k == 0 and (x, part) == (0, 0), stop=k == KD - 1 and part == 1)
                return mm

            for k in range(KD):
                pe.wait_ge(gv_split, k + 1)
                for c in range(4):
                    mm = values(c, k)
                    if k == KD - 1:
                        mm.then_inc(gv_made, 1)
            for c in range(4, NC):
                pe.wait_ge(gelued, c - 3)
                for k in range(KD):
                    mm = values(c, k)
                mm.then_inc(gv_made, 1)
            w.project(pe, h, (0, 2), free)
            pe.wait_ge(ws_masked, 1)
            for c in range(NC):
                pe.wait_ge(shifted, c + 1)
                if c >= 2:
                    pe.wait_ge(biased, c - 1)
                for gr in range(NH):
                    rows = slice((gr % 2) * HD, (gr % 2) * HD + HD)
                    mm = nc.tensor.matmul(ps[rows, 4 + c % 2, (gr // 2) * CH:(gr // 2 + 1) * CH], gv[:, c, gr * HD:(gr + 1) * HD], ws[:, gr, :],
                                          start=True, stop=True)
                mm.then_inc(mixed, 1)

        @block.scalar
        def _(act):
            for k in range(KD):
                act.wait_ge(gv_loaded[k % 2], 16 * (k // 2) + 16)
                nc.scalar.activation(wgv_parts[:, 0, k, :], wgv[:, k % 2, :], ACT.Copy).then_inc(gv_rounded, 1)
            w.first_rounds(act)
            for c in range(NC):
                act.wait_ge(gv_made, c + 1)
                nc.scalar.activation(gv[:, c, :], ps[:, 4 + c % 4, :], ACT.Gelu).then_inc(gelued, 1)

            def empty(i, u):
                nc.scalar.activation(row(g.y, i * 2 + (u + 4)), two(ps, 2 * u), ACT.Gelu).then_inc(free[u], 1)

            act.wait_ge(aggregated, NC)
            nc.scalar.activation(rstd[:, :], mv[:, :, 1], ACT.Ln, bias=g.eps(LN_EPS)).then_inc(logged, 1)
            act.wait_ge(logged, 1)
            nc.scalar.activation(rstd[:, :], rstd[:, :], ACT.Exp, scale=-0.5).then_inc(rooted, 1)
            w.more_rounds(act, empty)

        @block.gpsimd
        def _(pool):
            pool.wait_ge(ws_loaded, 16)
            nc.gpsimd.affine_select(out=ws[:, :, :], in_=ws[:, :, :], compare_op=ALU.is_ge, fill=0.0, base=0,
                                    pattern=[[0, NH], [1, CH]], channel_multiplier=-1).then_inc(ws_masked, 1)
            w.first_splits(pool)
            w.more_splits(pool)

        @block.vector
        def _(dve):
            for k in range(KD):
                dve.wait_ge(gv_rounded, k + 1)
                nc.vector.tensor_tensor(wgv_parts[:, 1, k, :], wgv[:, k % 2, :], wgv_parts[:, 0, k, :].bitcast(F32), ALU.subtract)\
                    .then_inc(gv_split, 1)
            for c in range(NC):
                dve.wait_ge(gelued, c + 1)
                nc.vector.bn_stats(stats[:, c, :], gv[:, c, :]).then_inc(stat, 1)
                dve.wait_ge(stat, c + 1)
                nc.vector.bn_aggr(mv[:, c, :], stats[:, c, :]).then_inc(aggregated, 1)
            dve.wait_ge(rooted, 1)
            for c in range(NC):
                nc.vector.tensor_scalar(gv[:, c, :], gv[:, c, :], mv[:, c, 0:1], rstd[:, c:c + 1], ALU.subtract, ALU.mult).then_inc(normed, 1)
            dve.wait_ge(ln_loaded, 16)
            for c in range(NC):
                dve.wait_ge(normed, c + 1)
                nc.vector.tensor_tensor(gv[:, c, :], gv[:, c, :], ln[:, 0, :], ALU.mult).then_inc(scaled, 1)
            for c in range(NC):
                dve.wait_ge(scaled, c + 1)
                nc.vector.tensor_tensor(gv[:, c, :], gv[:, c, :], ln[:, 1, :], ALU.add).then_inc(shifted, 1)
            dve.wait_ge(bs_loaded, 16)
            for u in range(2):
                dve.wait_ge(free[u], 3)
            for c in range(NC):
                dve.wait_ge(mixed, c + 1)
                if c >= 2:
                    dve.wait_ge(gated, c - 1)
                nc.vector.tensor_tensor(t[:, c % 2, :], ps[:, 4 + c % 2, :], bs[:, :, :].rearrange("p j t -> p (j t)"), ALU.add).then_inc(biased, 1)
                dve.wait_ge(biased, c + 1)
                u = g.y[:, 4:8, c * CH:(c + 1) * CH]
                nc.vector.tensor_tensor(u, t[:, c % 2, :].rearrange("p (j t) -> p j t", j=NP), u, ALU.mult).then_inc(gated, 1)


NOPE_ROWS = (slice(0, 64), slice(64, 128))
ROPE_ROWS = ((slice(64, 96), slice(96, 128)), (slice(0, 32), slice(32, 64)))
HEAD_ROWS = (slice(0, QK), slice(0, P))


def latent_phase(nc, g, l, h, slots, lat, kr, v):
    with ExitStack() as ctx:
        w = Stream(nc, g, "la", slots, l * N_WT + T_LAT, N_LAT, follows=True)
        wv = ctx.enter_context(nc.sbuf_tensor("wv", [P, 2, BW], F32))
        rstd = g.x_rstd
        sq, acc = g.y[:, 8:10, :], g.y[:, 10:12, :]
        turned = acc[:, 1, :]
        ps = g.ps
        free, squared, used = ([g.loop_sems(f"la_{n}{u}")[0] for u in range(2)] for n in ("free", "squared", "used"))
        wv_loaded, summed, logged, rooted, rot, kv_normed, v_made, v_ready = g.sems(
            "la_wv la_summed la_logged la_rooted la_rot la_kv_normed la_v_made la_v_ready")
        g.start()
        block = ctx.enter_context(nc.Block())
        norms = ((0, KV_LORA), (1, Q_LORA))
        sum_banks = (4, 0)

        @block.sync
        def _(sp):
            w.loads(sp)
            sp.dma_start(wv[:, :, :], g.d_wv[bass.ds(l, 1)].rearrange("o p k m -> p (o k) m")).then_inc(wv_loaded, 16)

        @block.gpsimd
        def _(pool):
            w.first_splits(pool)
            w.more_splits(pool)

        @block.tensor
        def _(pe):
            def channel_sum(n):
                for b in range(2):
                    mm = nc.tensor.matmul(ps[:, sum_banks[n] + b, :], g.ones[:, :], acc[:, n, b * HALF:(b + 1) * HALF], start=True, stop=True)
                mm.then_inc(summed, 1)

            def values(c):
                if c >= 4:
                    pe.wait_ge(v_ready, c - 3)
                for k in range(2):
                    mm = nc.tensor.matmul(ps[:, 4 + c % 4, :], lat[:, LAT_KV + k, c * CH:(c + 1) * CH], wv[:, k, :], start=k == 0, stop=k == 1)
                mm.then_inc(v_made, 1)

            w.project(pe, h, (0, 2), free, 0, 2)
            pe.wait_ge(used[1], 2)
            channel_sum(0)
            w.project(pe, h, (0, 2), free, 2, 3)
            pe.wait_ge(wv_loaded, 16)
            pe.wait_ge(kv_normed, 2)
            values(0)
            values(1)
            pe.wait_ge(used[1], 4)
            pe.wait_ge(free[0], 4)
            channel_sum(1)
            for c in range(2, NC):
                values(c)

        @block.scalar
        def _(act):
            def empty(i, u):
                act.wait_ge(used[u], i + 1)
                nc.scalar.activation(sq[:, u, :], two(ps, 2 * u), ACT.Square).then_inc(squared[u], 1)
                nc.scalar.activation(row(lat, i * 2 + u), two(ps, 2 * u), ACT.Copy).then_inc(free[u], 1)

            def root(n):
                act.wait_ge(summed, n + 1)
                if n:
                    act.wait_ge(kv_normed, 2)
                nc.scalar.activation(rstd[:, :], two(ps, sum_banks[n]), ACT.Ln, scale=1.0 / norms[n][1], bias=g.eps(NORM_EPS)).then_inc(logged, 1)
                act.wait_ge(logged, n + 1)
                nc.scalar.activation(rstd[:, :], rstd[:, :], ACT.Exp, scale=-0.5).then_inc(rooted, 1)

            w.first_rounds(act)
            w.more_rounds(act, empty, lambda: root(0))
            for c in range(NC):
                if c == 2:
                    root(1)
                act.wait_ge(v_made, c + 1)
                nc.scalar.activation(v[:, c, :], ps[:, 4 + c % 4, :], ACT.Copy).then_inc(v_ready, 1)

        @block.vector
        def _(dve):
            def add_square(k, n, first):
                dve.wait_ge(squared[k % 2], k // 2 + 2)
                if first:
                    nc.vector.tensor_copy(acc[:, n, :], sq[:, k % 2, :]).then_inc(used[k % 2], 1)
                else:
                    dve.wait_ge(used[(k - 1) % 2], (k - 1) // 2 + 2)
                    nc.vector.tensor_tensor(acc[:, n, :], acc[:, n, :], sq[:, k % 2, :], ALU.add).then_inc(used[k % 2], 1)

            add_square(0, 0, True)
            add_square(1, 0, False)
            dve.wait_ge(free[0], 3)
            dve.sem_inc(used[0], 1)
            for u in range(2):
                one, other = ROPE_ROWS[u]
                nc.vector.tensor_tensor(kr[u][one, :], lat[one, LAT_KR, :], g.rope[one, :], ALU.mult).then_inc(rot, 1)
                nc.vector.tensor_tensor(turned[one, :], lat[other, LAT_KR, :], g.rope[other, :], ALU.mult).then_inc(rot, 1)
            dve.wait_ge(rot, 4)
            for u in range(2):
                one = ROPE_ROWS[u][0]
                nc.vector.tensor_tensor(kr[u][one, :], kr[u][one, :], turned[one, :], ALU.add).then_inc(rot, 1)
            dve.wait_ge(rot, 6)
            add_square(3, 1, True)
            dve.wait_ge(rooted, 1)
            for k in range(2):
                kv = lat[:, LAT_KV + k, :]
                nc.vector.scalar_tensor_tensor(kv, kv, g.pcol("kv_norm", k), rstd[:, :], ALU.mult, ALU.mult).then_inc(kv_normed, 1)
            add_square(4, 1, False)
            add_square(5, 1, False)
            dve.wait_ge(rooted, 2)
            for k in range(3):
                q = lat[:, LAT_Q + k, :]
                nc.vector.scalar_tensor_tensor(q, q, g.pcol("q_norm", k), rstd[:, :], ALU.mult, ALU.mult)


def attention_phase(nc, g, l, lat, kr, v):
    with ExitStack() as ctx:
        def sb(name, *shape):
            return ctx.enter_context(nc.sbuf_tensor(name, [P, *shape], F32))

        hw = [sb(f"head_weights{u}", HALF) for u in range(2)]
        q = [sb(f"q_head{u}", T) for u in range(2)]
        prob, pt = sb("prob", 2, T), sb("prob_t", 2, NC, CH)
        turned = prob[:, 0, :]
        otok = g.y[:, 11, :].rearrange("p (c n) -> p c n", c=NC)
        mx, nm, den, rden = (sb(n, 2, NC) for n in ("row_max", "neg_max", "row_sum", "row_recip"))
        ps = g.ps
        hw_loaded = [g.sem(f"at_hw{u}") for u in range(2)]
        zeroed, = g.sems("at_zeroed")
        names = ("q_made", "k_made", "q_ready", "turn", "q_turned", "odd_turn", "odd_q_turned", "k_ready", "s_made",
                 "masked", "maxed", "negated", "exped", "t_made", "t_ready", "o_made", "recip", "o_ready", "y_made", "y_ready")
        s = dict(zip(names, g.loop_sems(*["at_" + n for n in names])))
        g.start()
        block = ctx.enter_context(nc.Block())
        UN = 2 * NC
        ORDER = (0, 2, 4, 6, 7, 5, 3, 1)
        unit = [(m // NC, ORDER[m % NC]) for m in range(UN)]
        groups = [1 if c < 4 else 2 for _, c in unit]
        GT = sum(groups)

        @block.sync
        def _(sp):
            with sp.Fori(0, NP) as j:
                for u in range(2):
                    sp.wait_ge(s["q_made"], j * 2 + 1)
                    sp.dma_start(hw[u][:, :], g.d_whead[bass.ds(l * NH + 2 * j + u, 1)].rearrange("o p n -> p (o n)"))\
                        .then_inc(hw_loaded[u], 16)

        @block.tensor
        def _(pe):
            ident = g.con("ident")
            with pe.Fori(0, NP) as j:
                pe.wait_ge(s["o_ready"], j * UN + 1)
                for u in range(2):
                    pe.wait_ge(hw_loaded[u], j * 16 + 16)
                for k in range(2):
                    for b in range(2):
                        mm = nc.tensor.matmul(ps[:, 4 + b, :], hw[k][:, 3 * P:4 * P], lat[:, LAT_KV + k, b * HALF:(b + 1) * HALF],
                                              start=k == 0, stop=k == 1)
                mm.then_inc(s["k_made"], 1)
                for u in range(2):
                    for k in range(3):
                        for b in range(2):
                            mm = nc.tensor.matmul(ps[:, 6 * u + b, :], hw[u][:, k * P:(k + 1) * P], lat[:, LAT_Q + k, b * HALF:(b + 1) * HALF],
                                                  start=k == 0, stop=k == 2)
                    mm.then_inc(s["q_made"], 1)

                def scores(m):
                    u, c = unit[m]
                    if m % NC == 0:
                        pe.wait_ge(s["odd_q_turned" if u else "q_turned"], j + 2)
                        pe.wait_ge(s["k_ready"], j * 2 + 3)
                        pe.wait_ge(s["q_ready"], j * 2 + u + 2)
                    if m == 1:
                        pe.wait_ge(s["q_ready"], j * 2 + 3)
                    if m >= 2:
                        pe.wait_ge(s["exped"], j * UN + m)
                    n = (c + 1) * CH
                    for b in range((n + HALF - 1) // HALF):
                        w = min(HALF, n - b * HALF)
                        mm = nc.tensor.matmul(ps[:, 4 + 2 * (m % 2) + b, 0:w], q[u][HEAD_ROWS[u], c * CH:(c + 1) * CH],
                                              kr[u][HEAD_ROWS[u], b * HALF:b * HALF + w], start=True, stop=True)
                    mm.then_inc(s["s_made"], 1)

                def turn(m):
                    c = unit[m][1]
                    pe.wait_ge(s["exped"], j * UN + m + 2)
                    if m == 0:
                        pe.wait_ge(s["y_ready"], j * 2 + 1)
                    for n in range(groups[m]):
                        last = max((k for k in range(m) if groups[k] > n), default=None)
                        if last is not None:
                            pe.wait_ge(s["t_ready"], j * GT + sum(groups[:last]) + n + 2)
                        for blk in range(4 * n, min(4 * n + 4, c + 1)):
                            mm = nc.tensor.transpose(ps[:, 2 + n, (blk % 4) * CH:(blk % 4 + 1) * CH],
                                                     prob[:, m % 2, blk * CH:(blk + 1) * CH], ident)
                        mm.then_inc(s["t_made"], 1)

                def values(m):
                    u, c = unit[m]
                    pe.wait_ge(s["t_ready"], j * GT + sum(groups[:m + 1]) + 1)
                    if m >= 2:
                        pe.wait_ge(s["o_ready"], j * UN + m)
                    for blk in range(c + 1):
                        mm = nc.tensor.matmul(ps[:, m % 2, 0:HD], pt[:, m % 2, blk, :], v[:, blk, bass.ds(j * P + u * HD, HD)],
                                              start=blk == 0, stop=blk == c)
                    mm.then_inc(s["o_made"], 1)

                scores(0)
                for m in range(UN):
                    if m + 1 < UN:
                        scores(m + 1)
                    turn(m)
                    if m:
                        values(m - 1)
                values(UN - 1)
                pe.wait_ge(s["o_ready"], j * UN + UN + 1)
                for n in range(2):
                    for c in range(4 * n, 4 * n + 4):
                        mm = nc.tensor.transpose(ps[:, 2 + n, (c % 4) * CH:(c % 4 + 1) * CH], otok[:, c, :], ident)
                    mm.then_inc(s["y_made"], 1)

        def two(b0, rows):
            return ps[rows, b0:b0 + 2, :].rearrange("p b n -> p (b n)")

        @block.scalar
        def _(act):
            with act.Fori(0, NP) as j:
                act.wait_ge(s["k_made"], j + 2)
                for u in range(2):
                    nc.scalar.activation(kr[u][NOPE_ROWS[u], :], two(4, NOPE_ROWS[u]), ACT.Copy).then_inc(s["k_ready"], 1)
                act.wait_ge(s["q_made"], j * 2 + 2)
                nc.scalar.activation(q[0][NOPE_ROWS[0], :], two(0, NOPE_ROWS[0]), ACT.Copy).then_inc(s["q_ready"], 1)
                act.wait_ge(s["q_made"], j * 2 + 3)
                nc.scalar.activation(q[1][:, :], two(6, HEAD_ROWS[1]), ACT.Copy).then_inc(s["q_ready"], 1)
                for m in range(UN):
                    u, c = unit[m]
                    n = (c + 1) * CH
                    act.wait_ge(s["negated"], j * UN + m + 2)
                    if m >= 2:
                        act.wait_ge(s["t_made"], j * GT + sum(groups[:m - 1]) + 1)
                    nc.scalar.activation(prob[:, m % 2, 0:n], ps[:, 4 + 2 * (m % 2):6 + 2 * (m % 2), :].rearrange("p b n -> p (b n)")[:, 0:n],
                                         ACT.Exp, scale=SCALE, bias=nm[:, u, c:c + 1], accum_out=den[:, u, c:c + 1]).then_inc(s["exped"], 1)
                act.wait_ge(s["y_made"], j * 2 + 3)
                for n in range(2):
                    nc.scalar.activation(g.y[:, bass.ds(j + 8, 1), n * HALF:(n + 1) * HALF].rearrange("p o t -> p (o t)"), ps[:, 2 + n, :],
                                         ACT.Copy).then_inc(s["y_ready"], 1)

        @block.gpsimd
        def _(pool):
            one, other = ROPE_ROWS[1]
            odd_turned = g.x_rstd
            with pool.Fori(0, NP) as j:
                pool.wait_ge(s["q_ready"], j * 2 + 3)
                nc.gpsimd.tensor_tensor(odd_turned[one, :], q[1][other, :], g.rope[other, :], ALU.mult).then_inc(s["odd_turn"], 1)
                pool.wait_ge(s["odd_turn"], j * 2 + 2)
                nc.gpsimd.tensor_tensor(q[1][one, :], q[1][one, :], g.rope[one, :], ALU.mult).then_inc(s["odd_turn"], 1)
                pool.wait_ge(s["odd_turn"], j * 2 + 3)
                nc.gpsimd.tensor_tensor(q[1][one, :], q[1][one, :], odd_turned[one, :], ALU.add).then_inc(s["odd_q_turned"], 1)

        @block.vector
        def _(dve):
            nc.vector.memset(kr[1][32:64, :], 0.0).then_inc(zeroed, 1)
            dve.wait_ge(zeroed, 1)
            one, other = ROPE_ROWS[0]
            with dve.Fori(0, NP) as j:
                dve.wait_ge(s["q_made"], j * 2 + 2)
                nc.vector.tensor_tensor(q[0][one, :], two(0, one), g.rope[one, :], ALU.mult).then_inc(s["turn"], 1)
                nc.vector.tensor_tensor(turned[one, :], two(0, other), g.rope[other, :], ALU.mult).then_inc(s["turn"], 1)
                dve.wait_ge(s["turn"], j * 2 + 3)
                nc.vector.tensor_tensor(q[0][one, :], q[0][one, :], turned[one, :], ALU.add).then_inc(s["q_turned"], 1)

                def rowmax(m):
                    u, c = unit[m]
                    both = ps[:, 4 + 2 * (m % 2):6 + 2 * (m % 2), :].rearrange("p b n -> p (b n)")
                    diag = both[:, c * CH:(c + 1) * CH]
                    dve.wait_ge(s["s_made"], j * UN + m + 2)
                    nc.vector.tensor_tensor(diag, diag, g.con("causal"), ALU.add).then_inc(s["masked"], 1)
                    dve.wait_ge(s["masked"], j * UN + m + 2)
                    nc.vector.reduce_max(mx[:, u, c:c + 1], both[:, 0:(c + 1) * CH], AX.X).then_inc(s["maxed"], 1)
                    dve.wait_ge(s["maxed"], j * UN + m + 2)
                    nc.vector.tensor_scalar(nm[:, u, c:c + 1], mx[:, u, c:c + 1], -SCALE, None, ALU.mult).then_inc(s["negated"], 1)

                def turned_blocks(m):
                    c = unit[m][1]
                    for n in range(groups[m]):
                        dve.wait_ge(s["t_made"], j * GT + sum(groups[:m]) + n + 2)
                        w = min(4, c + 1 - 4 * n)
                        if m >= 2 and n == 0:
                            dve.wait_ge(s["o_made"], j * UN + m)
                        nc.vector.tensor_copy(pt[:, m % 2, 4 * n:4 * n + w, :].rearrange("p b t -> p (b t)"), ps[:, 2 + n, 0:w * CH])\
                            .then_inc(s["t_ready"], 1)

                def normalise(m):
                    u, c = unit[m]
                    nc.vector.reciprocal(rden[:, u, c:c + 1], den[:, u, c:c + 1]).then_inc(s["recip"], 1)
                    dve.wait_ge(s["recip"], j * UN + m + 2)
                    dve.wait_ge(s["o_made"], j * UN + m + 2)
                    nc.vector.tensor_scalar(otok[:, c, u * HD:(u + 1) * HD], ps[:, m % 2, 0:HD], rden[:, u, c:c + 1], None, ALU.mult)\
                        .then_inc(s["o_ready"], 1)

                rowmax(0)
                for m in range(UN):
                    if m + 1 < UN:
                        rowmax(m + 1)
                    turned_blocks(m)
                    if m:
                        normalise(m - 1)
                normalise(UN - 1)


def gate_phase(nc, g, l, h, slots):
    with ExitStack() as ctx:
        w = Stream(nc, g, "ga", slots, l * N_WT + T_GATE, N_GATE, leads=True)
        sig = ctx.enter_context(nc.sbuf_tensor("gate_sig", [P, 2, T], F32))
        t = ctx.enter_context(nc.sbuf_tensor("gate_silu", [P, 2, T], F32))
        y_parts = ctx.enter_context(nc.sbuf_tensor("gated_parts", [P, 2, 2, T], F32R))
        free, sig_ready, gated, y_rounded, y_split = ([g.loop_sems(f"ga_{n}{u}")[0] for u in range(2)]
                                                      for n in ("free", "sig", "gated", "y_rounded", "y_split"))
        g.start()
        block = ctx.enter_context(nc.Block())

        @block.sync
        def _(sp):
            def store(i, u):
                sp.wait_ge(y_split[u], i + 2)
                sp.dma_start(g.d_y[bass.ds(i * 2 + u, 1)].rearrange("o p a t -> p (o a) t"), y_parts[:, u].bitcast(F32)).then_inc(g.y_stored[u], 16)

            w.loads(sp, between=lambda i: [store(i - 1, u) for u in range(2)])

        @block.gpsimd
        def _(pool):
            w.first_splits(pool)
            w.more_splits(pool)

        @block.tensor
        def _(pe):
            w.project(pe, h, (0, 2), free)

        @block.scalar
        def _(act):
            w.first_rounds(act)
            with act.Fori(0, w.stop - 1) as i:
                for u in range(2):
                    act.wait_ge(w.done[u], i + 1)
                    act.wait_ge(free[u], i + 1)
                    nc.scalar.activation(sig[:, u, :], two(g.ps, 2 * u), ACT.Sigmoid).then_inc(sig_ready[u], 1)
                    w.round(act, i + 1, u)
                    act.wait_ge(gated[u], i + 2)
                    act.wait_ge(g.y_stored[u], (l * (N_GATE // 2) + i) * 16 + 16)
                    nc.scalar.activation(y_parts[:, u, 0, :], row(g.y, i * 2 + u), ACT.Copy).then_inc(y_rounded[u], 1)

        @block.vector
        def _(dve):
            with dve.Fori(0, N_GATE // 2) as i:
                for u in range(2):
                    y = row(g.y, i * 2 + u)
                    dve.wait_ge(sig_ready[u], i + 2)
                    nc.vector.tensor_tensor(t[:, u, :], two(g.ps, 2 * u), sig[:, u, :], ALU.mult).then_inc(free[u], 1)
                    dve.wait_ge(free[u], i + 2)
                    nc.vector.tensor_tensor(y, y, t[:, u, :], ALU.mult).then_inc(gated[u], 1)
                    dve.wait_ge(y_rounded[u], i + 2)
                    nc.vector.tensor_tensor(y_parts[:, u, 1, :], y, y_parts[:, u, 0, :].bitcast(F32), ALU.subtract).then_inc(y_split[u], 1)


def merge_phase(nc, g, l, h, slots, mixed):
    with ExitStack() as ctx:
        raw, parts = slots
        y = ctx.enter_context(nc.sbuf_tensor("branch_parts", [P, 2, NP, T], F32R))
        sig = ctx.enter_context(nc.sbuf_tensor("merge_sig", [P, 2, T], F32))
        t = ctx.enter_context(nc.sbuf_tensor("merge_term", [P, 2, T], F32))
        b_raw = ctx.enter_context(nc.sbuf_tensor("branch_weights_raw", [P, 2, NP, P], F32))
        b_parts = ctx.enter_context(nc.sbuf_tensor("branch_weights_parts", [P, 2, 2, NP, P], F32R))
        loaded, b_loaded = ([g.sem(f"me_{n}{u}") for u in range(2)] for n in ("w", "b"))
        y_loaded = [g.sem(f"me_y{part}") for part in range(2)]
        names = ("rounded", "gate_made", "made", "sig", "added", "b_rounded", "b_split")
        s = dict(zip(names, g.loop_sems(*["me_" + n for n in names])))
        split = g.started_at("me_split", 2)
        term = g.started_at("me_term", 2)
        g.start()
        block = ctx.enter_context(nc.Block())

        def units(engine, unit, before=lambda n: None):
            for n in range(NBR):
                before(n)
                with engine.Fori(0, KD // 2 - (n == NBR - 1)) as i:
                    for u in range(2):
                        unit(n, n * KD + i * 2 + u, u, i + n * KD // 2, i * 2 + u, True)
            for u in range(2):
                unit(NBR - 1, NBR * KD - 2 + u, u, NBR * KD // 2 - 1, KD - 2 + u, False)

        @block.sync
        def _(sp):
            def load_branch_weights(m, u):
                sp.dma_start(b_raw[:, u], g.d_wb[bass.ds(l * (NBR * KD) + m, 1)].rearrange("o p k m -> p (o k) m")).then_inc(b_loaded[u], 16)

            def load_y(n):
                if n:
                    sp.wait_ge(s["made"], n * KD + 1)
                for part in range(2):
                    sp.dma_start(y[:, part].bitcast(F32), g.d_y[NP * n:NP * (n + 1), :, part, :].rearrange("j p t -> p j t")).then_inc(y_loaded[part], 16)

            def unit(n, m, u, pair, d, more):
                sp.wait_ge(split, m + 1)
                sp.dma_start(raw[:, u], g.d_wt[bass.ds(l * N_WT + T_MERGE + 2 + m, 1)].rearrange("o p k m -> p (o k) m")).then_inc(loaded[u], 16)
                if more:
                    sp.wait_ge(s["b_split"], m + 2)
                    load_branch_weights(m + 2, u)

            for u in range(2):
                load_branch_weights(u, u)
            for u in range(2):
                sp.wait_ge(g.y_stored[u], (l + 1) * (16 * (N_GATE // 2)) + 16)
            load_y(0)
            units(sp, unit, before=lambda n: load_y(n) if n else None)

        def split_branch_weights(pool, m, u):
            pool.wait_ge(s["b_rounded"], m + 2)
            nc.gpsimd.tensor_tensor(b_parts[:, u, 1], b_raw[:, u], b_parts[:, u, 0].bitcast(F32), ALU.subtract).then_inc(s["b_split"], 1)

        @block.gpsimd
        def _(pool):
            def unit(n, m, u, pair, d, more):
                pool.wait_ge(s["rounded"], m + 2)
                nc.gpsimd.tensor_tensor(parts[:, u, 1], raw[:, u], parts[:, u, 0].bitcast(F32), ALU.subtract).then_inc(split, 1)
                if more:
                    split_branch_weights(pool, m + 2, u)

            for u in range(2):
                split_branch_weights(pool, u, u)
            units(pool, unit)

        @block.tensor
        def _(pe):
            def unit(n, m, u, pair, d, more):
                pe.wait_ge(split, m + 1)
                pe.wait_ge(term, m + 1)
                for k in range(KD):
                    mm = products_of_parts(nc, k, lambda b: g.ps[:, 4 * u + b, :], lambda part: parts[:, u, part, k, :], h)
                mm.then_inc(s["gate_made"], 1)
                pe.wait_ge(s["b_split"], m + 2)
                for w, x in ((0, 0), (1, 0), (0, 1)):
                    if w == 0:
                        pe.wait_ge(y_loaded[x], 16 * (n + 1))
                    for k in range(NP):
                        for b in range(2):
                            mm = nc.tensor.matmul(g.ps[:, 4 * u + 2 + b, :], b_parts[:, u, w, k, :], y[:, x, k, b * HALF:(b + 1) * HALF],
                                                  start=(w, x, k) == (0, 0, 0), stop=(x, k) == (1, NP - 1))
                mm.then_inc(s["made"], 1)

            units(pe, unit)

        def round_branch_weights(act, pair, u):
            act.wait_ge(b_loaded[u], pair * 16 + 16)
            nc.scalar.activation(b_parts[:, u, 0], b_raw[:, u], ACT.Copy).then_inc(s["b_rounded"], 1)

        @block.scalar
        def _(act):
            def unit(n, m, u, pair, d, more):
                act.wait_ge(s["gate_made"], m + 2)
                act.wait_ge(loaded[u], pair * 16 + 16)
                nc.scalar.activation(parts[:, u, 0], raw[:, u], ACT.Copy).then_inc(s["rounded"], 1)
                act.wait_ge(term, m + 1)
                nc.scalar.activation(sig[:, u, :], two(g.ps, 4 * u), ACT.Sigmoid).then_inc(s["sig"], 1)
                if more:
                    act.wait_ge(s["made"], m + 2)
                    round_branch_weights(act, pair + 1, u)

            for u in range(2):
                round_branch_weights(act, 0, u)
            for u in range(2):
                act.wait_ge(g.y_stored[u], (l + 1) * (16 * (N_GATE // 2)) + 16)
            units(act, unit)

        @block.vector
        def _(dve):
            def unit(n, m, u, pair, d, more):
                dve.wait_ge(s["sig"], m + 2)
                dve.wait_ge(s["made"], m + 2)
                out = row(mixed, d)
                if n == 0:
                    nc.vector.tensor_tensor(out, two(g.ps, 4 * u + 2), sig[:, u, :], ALU.mult).then_inc(term, 1)
                else:
                    nc.vector.tensor_tensor(t[:, u, :], two(g.ps, 4 * u + 2), sig[:, u, :], ALU.mult).then_inc(term, 1)
                    dve.wait_ge(term, m + 3)
                    nc.vector.tensor_tensor(out, out, t[:, u, :], ALU.add).then_inc(s["added"], 1)

            units(dve, unit)


def out_phase(nc, g, l, h, slots, mixed):
    with ExitStack() as ctx:
        w = Stream(nc, g, "ou", slots, l * N_WT + T_OUT, KD, follows=True)
        acc, rstd = (ctx.enter_context(nc.sbuf_tensor(n, [P, T], F32)) for n in ("o_acc", "o_rstd"))
        sq = ctx.enter_context(nc.sbuf_tensor("o_sq", [P, 2, T], F32))
        x = ctx.enter_context(nc.sbuf_tensor("x", [P, KD, T], F32))
        o = mixed
        free = [g.loop_sems(f"ou_free{u}")[0] for u in range(2)]
        x_loaded, summed, logged, rooted, scaled, updated, stored, m_rounded, m_split, x_squared, x_summed = g.sems(
            "ou_x_loaded ou_summed ou_logged ou_rooted ou_scaled ou_updated ou_stored ou_m_rounded ou_m_split x_squared x_summed")
        squared, added = g.loop_sems("ou_squared", "ou_added")
        late_updated = g.sem("ou_late_updated")
        g.start()
        block = ctx.enter_context(nc.Block())
        on_pool = (0, 2, 4, 6)
        by_readiness = (1, 0, 3, 2, 5, 4, 7, 6)
        update = {}
        for k in range(KD):
            sem = late_updated if k in on_pool else updated
            update[k] = (sem, sum(1 for n in range(k + 1) if (n in on_pool) == (k in on_pool)))

        @block.sync
        def _(sp):
            w.loads(sp, between=lambda i: sp.dma_start(x[:, bass.ds(2 * i, 2), :], g.d_out[:, bass.ds(2 * i, 2), :]).then_inc(x_loaded, 16))
            sp.dma_start(x[:, 0:2, :], g.d_out[:, 0:2, :]).then_inc(x_loaded, 16)
            sp.wait_ge(x_loaded, 64)
            for k in by_readiness:
                sp.wait_ge(*update[k])
                sp.dma_start(g.d_out[:, k, :], x[:, k, :]).then_inc(stored, 16)
            sp.wait_ge(stored, 16 * KD)

        @block.gpsimd
        def _(pool):
            w.first_splits(pool)
            w.more_splits(pool)
            pool.wait_ge(x_loaded, 64)
            for k in on_pool:
                pool.wait_ge(scaled, k + 2)
                nc.gpsimd.tensor_tensor(x[:, k, :], x[:, k, :], o[:, k, :], ALU.add).then_inc(late_updated, 1)

        @block.tensor
        def _(pe):
            for u in range(2):
                pe.wait_ge(w.split_done[u], 1)
            for k in range(KD):
                pe.wait_ge(m_split, k + 1)
                for u in range(2):
                    mm = w.products(k, u, h, (0, 2))
                    if k == KD - 1:
                        mm.then_inc(w.done[u], 1)
            w.project(pe, h, (0, 2), free, 1)
            pe.wait_ge(added, KD + 1)
            for b in range(2):
                mm = nc.tensor.matmul(g.ps[:, 4 + b, :], g.ones[:, :], acc[:, b * HALF:(b + 1) * HALF], start=True, stop=True)
            mm.then_inc(summed, 1)
            sum_of_squares(nc, g, pe, sq, x_squared, x_summed)

        @block.scalar
        def _(act):
            for k in range(KD):
                nc.scalar.activation(h[:, 0, k, :], mixed[:, k, :], ACT.Copy).then_inc(m_rounded, 1)
            act.wait_ge(m_split, KD)

            def empty(i, u):
                act.wait_ge(added, i * 2 + (u + 1))
                nc.scalar.activation(sq[:, 0, :], two(g.ps, 2 * u), ACT.Square).then_inc(squared, 1)
                nc.scalar.activation(row(o, i * 2 + u), two(g.ps, 2 * u), ACT.Copy, scale=g.par[:, bass.ds(i * 2 + (u + PAR["post"]), 1)])\
                    .then_inc(free[u], 1)

            w.more_rounds(act, empty)
            act.wait_ge(summed, 1)
            nc.scalar.activation(rstd[:, :], two(g.ps, 4), ACT.Ln, scale=1.0 / D, bias=g.eps(NORM_EPS)).then_inc(logged, 1)
            act.wait_ge(logged, 1)
            nc.scalar.activation(rstd[:, :], rstd[:, :], ACT.Exp, scale=-0.5).then_inc(rooted, 1)
            for n, k in enumerate(by_readiness):
                act.wait_ge(*update[k])
                square(nc, g, act, sq, x, k, n, x_squared, x_summed)

        @block.vector
        def _(dve):
            nc.vector.memset(acc[:, :], 0.0).then_inc(scaled, 1)
            for k in range(KD):
                dve.wait_ge(m_rounded, k + 1)
                nc.vector.tensor_tensor(h[:, 1, k, :], mixed[:, k, :], h[:, 0, k, :].bitcast(F32), ALU.subtract).then_inc(m_split, 1)
            dve.wait_ge(scaled, 1)
            with dve.Fori(0, KD) as i:
                dve.wait_ge(squared, i + 2)
                dve.wait_ge(added, i + 1)
                nc.vector.tensor_tensor(acc[:, :], acc[:, :], sq[:, 0, :], ALU.add).then_inc(added, 1)
            dve.wait_ge(rooted, 1)
            dve.wait_ge(x_loaded, 64)
            for k in range(KD):
                nc.vector.tensor_tensor(o[:, k, :], o[:, k, :], rstd[:, :], ALU.mult).then_inc(scaled, 1)
                if k not in on_pool:
                    dve.wait_ge(scaled, k + 2)
                    nc.vector.tensor_tensor(x[:, k, :], x[:, k, :], o[:, k, :], ALU.add).then_inc(updated, 1)


def square(nc, g, act, sq, x, k, n, squared, summed):
    if n >= 2:
        act.wait_ge(summed, n - 1)
    nc.scalar.activation(sq[:, n % 2, :], x[:, k, :], ACT.Square).then_inc(squared, 1)


def sum_of_squares(nc, g, pe, sq, squared, summed):
    for k in range(KD):
        pe.wait_ge(squared, k + 1)
        for b in range(2):
            mm = nc.tensor.matmul(g.ps[:, 6 + b, :], g.ones[:, :], sq[:, k % 2, b * HALF:(b + 1) * HALF], start=k == 0, stop=k == KD - 1)
        mm.then_inc(summed, 1)


def setup_phase(nc, g):
    C1 = 6.28125
    C2 = 0.0019350051879882812
    C3 = 2 * math.pi - C1 - C2
    MAGIC = 1.5 * 2 ** 23
    with ExitStack() as ctx:
        pos = ctx.enter_context(nc.sbuf_tensor("pos", [P, T], I32))
        ang, turns, rest = (ctx.enter_context(nc.sbuf_tensor(n, [P, T], F32)) for n in ("ang", "turns", "rest"))
        sq = ctx.enter_context(nc.sbuf_tensor("x_sq", [P, 2, T], F32))
        x = ctx.enter_context(nc.sbuf_tensor("first_x", [P, KD, T], F32))
        con_loaded, pos_loaded, filled, step, zeroed, folded, roped, squared, summed = g.sems(
            "con pos filled step zeroed folded roped squared summed")
        x_loaded = [g.sem(f"x_loaded{q}") for q in range(4)]
        zeros = ctx.enter_context(nc.sbuf_tensor("zeros", [P, NP, T], F32))
        g.start()
        block = ctx.enter_context(nc.Block())
        @block.sync
        def _(sp):
            for q in range(4):
                sp.dma_start(x[:, 2 * q:2 * q + 2, :], g.d_x[:, 2 * q:2 * q + 2, :]).then_inc(x_loaded[q], 16)
            sp.dma_start(pos[:, :], g.d_pos.partition_broadcast(P)).then_inc(pos_loaded, 16)
            sp.dma_start(g.consts[:, :], g.d_con).then_inc(con_loaded, 16)
            sp.wait_ge(zeroed, 1)
            sp.dma_start(g.d_v, zeros[:, :, :]).then_inc(g.v_stored, 16)
            sp.dma_start(g.d_out, g.d_x).then_inc(g.x_copied, 16)
            sp.wait_ge(con_loaded, 16)
            sp.wait_ge(g.v_stored, 16)

        @block.tensor
        def _(pe):
            pe.wait_ge(filled, len(g.small_values) + 1)
            sum_of_squares(nc, g, pe, sq, squared, summed)

        @block.vector
        def _(dve):
            nc.vector.memset(g.ones[:, :], 1.0).then_inc(filled, 1)
            nc.vector.memset(zeros[:, :, :], 0.0).then_inc(zeroed, 1)
            for n, value in enumerate(g.small_values):
                nc.vector.memset(g.small[:, n:n + 1], value).then_inc(filled, 1)
            dve.wait_ge(con_loaded, 16)
            dve.wait_ge(pos_loaded, 16)
            n = [0]

            def chained(ins):
                n[0] += 1
                ins.then_inc(step, 1)
                dve.wait_ge(step, n[0])

            chained(nc.vector.tensor_copy(ang[:, :], pos[:, :]))
            chained(nc.vector.tensor_scalar(ang[:, :], ang[:, :], g.con("freq")[:, :], None, ALU.mult))
            chained(nc.vector.tensor_scalar(turns[:, :], ang[:, :], 1.0 / (2 * math.pi), MAGIC, ALU.mult, ALU.add))
            chained(nc.vector.tensor_scalar(turns[:, :], turns[:, :], MAGIC, None, ALU.subtract))
            for part in (C1, C2, C3):
                chained(nc.vector.scalar_tensor_tensor(ang[:, :], turns[:, :], -part, ang[:, :], ALU.mult, ALU.add))
            chained(nc.vector.tensor_scalar(rest[:, :], ang[:, :], 3.1415925, -3.1415925, ALU.min, ALU.max))
            for cosines in (slice(0, 32), slice(64, 96)):
                chained(nc.vector.scalar_tensor_tensor(ang[cosines, :], rest[cosines, :], -1.0, rest[cosines, :], ALU.mult, ALU.min))
                nc.vector.tensor_scalar(rest[cosines, :], ang[cosines, :], math.pi / 2, None, ALU.add).then_inc(folded, 1)

        @block.scalar
        def _(act):
            for k in range(KD):
                act.wait_ge(x_loaded[k // 2], 16)
                square(nc, g, act, sq, x, k, k, squared, summed)
            act.wait_ge(folded, 2)
            nc.scalar.activation(g.rope[:, :], rest[:, :], ACT.Sin).then_inc(roped, 1)


def build(nc, d_x, d_pos, d_con, d_par, d_wt, d_up, d_wgv, d_gln, d_ws, d_bs, d_whead, d_wv, d_wb, d_out):
    g = Core()
    g.d_x, g.d_pos, g.d_con, g.d_par, g.d_wt, g.d_up, g.d_wgv, g.d_gln = d_x, d_pos, d_con, d_par, d_wt, d_up, d_wgv, d_gln
    g.d_ws, g.d_bs, g.d_whead, g.d_wv, g.d_wb, g.d_out = d_ws, d_bs, d_whead, d_wv, d_wb, d_out
    g.d_h = nc.dram_tensor("h_parts", (P, 2, KD, T), F32).ap()
    g.d_y = nc.dram_tensor("y_parts", (NBR * NP, P, 2, T), F32).ap()
    g.d_v = nc.dram_tensor("v_first", (P, NP, T), F32).ap()
    g.small_values = [NORM_EPS, GN_EPS, LN_EPS, 0.5 * KK_SHIFT * math.log(2.0)]
    with ExitStack() as ctx:
        def sb(name, *shape):
            return ctx.enter_context(nc.sbuf_tensor(name, [P, *shape], F32))

        g.consts, g.ones, g.rope, g.par = sb("consts", N_CON), sb("ones", P), sb("rope", T), sb("par", N_PAR)
        g.x_rstd = sb("x_rstd", T)
        g.small = sb("small", len(g.small_values))
        g.ps = ctx.enter_context(nc.psum_tensor("ps", [P, 8, HALF], F32))
        g.con = lambda name: g.consts[:, CON[name][0]:CON[name][0] + CON[name][1]]
        g.pcol = lambda name, k: g.par[:, PAR[name] + k:PAR[name] + k + 1]
        g.eps = lambda value: g.small[:, g.small_values.index(value):g.small_values.index(value) + 1]

        pool = [ctx.enter_context(nc.semaphore(f"s{i}")) for i in range(40)]
        g.v_stored, g.x_copied = (ctx.enter_context(nc.semaphore(n)) for n in ("v_stored", "x_copied"))
        g.y_stored = [ctx.enter_context(nc.semaphore(f"y_stored{u}")) for u in range(2)]
        for u in range(2):
            nc.sync.sem_inc(g.y_stored[u], 16)
        used, started = [], []

        def sem(name):
            used.append(pool[len(used)])
            return used[-1]

        g.sem = sem
        g.sems = lambda names: [sem(n) for n in names.split()]

        def loop_sems(*names):
            return [started_at(n, 1) for n in names]

        def started_at(name, value):
            started.append((sem(name), value))
            return started[-1][0]

        def start():
            values = {id(x): value for x, value in started}
            for n, x in enumerate(used):
                engine = (nc.sync, nc.gpsimd, nc.tensor, nc.scalar, nc.vector)[n % 5]
                engine.sem_clear(x)
                if id(x) in values:
                    engine.sem_inc(x, values[id(x)])
            nc.all_engine_barrier()
            used.clear()
            started.clear()

        g.loop_sems, g.started_at, g.start = loop_sems, started_at, start
        setup_phase(nc, g)
        with nc.Fori(0, L) as l:
            ys, hs = ExitStack(), ExitStack()
            g.y = ys.enter_context(nc.sbuf_tensor("y", [P, NBR * NP, T], F32))
            with ExitStack() as rw:
                mix = rw.enter_context(nc.sbuf_tensor("mix", [P, N_RW, T], F32))
                ar = g.y[:, NP:NBR * NP, :].rearrange("p j t -> p (j t)").rearrange("p (j c x t) -> p j c x t", j=NP, c=NC, x=2)
                with nc.sbuf_tensor("h_first", [P, 2, KD, T], F32R, side="right") as h:
                    rwkv_project_phase(nc, g, l, h, mix)
                with ExitStack() as ch:
                    decay = ch.enter_context(nc.sbuf_tensor("decay", [P, NP, NC], F32))
                    v = ch.enter_context(nc.sbuf_tensor("v", [P, NP, T], F32))
                    rwkv_prepare_phase(nc, g, l, mix, ar, decay, v)
                    rwkv_chunk_phase(nc, g, l, mix, ar, decay, v)
                h = hs.enter_context(nc.sbuf_tensor("h_again", [P, 2, KD, T], F32R, side="right"))
                rwkv_finish_phase(nc, g, l, mix, h)
            with hs:
                def weight_slots(ctx, name):
                    return (ctx.enter_context(nc.sbuf_tensor(f"{name}_raw", [P, 2, KD, P], F32, side="right")),
                            ctx.enter_context(nc.sbuf_tensor(f"{name}_parts", [P, 2, 2, KD, P], F32R, side="right")))

                with ExitStack() as at:
                    with ExitStack() as ws:
                        slots = weight_slots(ws, "early_weights")
                        gmlp_phase(nc, g, l, h, slots)
                        lat = at.enter_context(nc.sbuf_tensor("latents", [P, N_LAT, T], F32))
                        kr = [at.enter_context(nc.sbuf_tensor(f"k_head{u}", [P, T], F32)) for u in range(2)]
                        v = at.enter_context(nc.sbuf_tensor("v_all", [P, NC, BW], F32))
                        latent_phase(nc, g, l, h, slots, lat, kr, v)
                    attention_phase(nc, g, l, lat, kr, v)
                slots = weight_slots(hs, "late_weights")
                gate_phase(nc, g, l, h, slots)
                ys.close()
                mixed = hs.enter_context(nc.sbuf_tensor("mixed", [P, KD, T], F32))
                merge_phase(nc, g, l, h, slots, mixed)
                out_phase(nc, g, l, h, slots, mixed)


def constants():
    con = np.zeros((P, N_CON), np.float32)

    def put(name, value):
        con[:, CON[name][0]:CON[name][0] + CON[name][1]] = value

    i, j = np.arange(P)[:, None], np.arange(P)[None, :]
    put("ident", i == j)
    put("blocks", i // HD == j // HD)
    put("amask", np.concatenate([i < j, i <= j, i < j, i <= j], 1))
    put("unit", (i % 2 == 0) & (j == i + 1))
    level = []
    for lev in range(1, 7):
        n = 1 << lev
        cols = np.arange(P).reshape(-1, 2, n)[:, 1, :].reshape(1, -1)
        level.append(i // n == cols // n - 1)
    put("level", np.concatenate(level, 1))
    put("causal", np.where(j <= i, 0.0, MASKED))
    put("restart", np.tile(np.arange(CH + 1) > 0, NC)[None, :])
    freq = (np.float32(1.0) / (np.float32(10000.0) ** (np.arange(0, ROPE, 2, dtype=np.float32) / np.float32(ROPE)))).astype(np.float32)
    column = np.zeros(P, np.float32)
    for first in (0, 64):
        column[first:first + 32] = np.tile(freq, 2)
        column[first + 32:first + 64] = np.concatenate([-freq, freq])
    put("freq", column[:, None])
    return con


def tiles(w):
    k, m = w.shape
    return w.reshape(k // P, P, m // P, P).transpose(2, 1, 0, 3)


def columns(v):
    return v.reshape(-1, P).T


def lay_out(x, positions, w_in, pre_norm, post_norm, rwkv_mu, rwkv_w0, rwkv_w_up, rwkv_a0, rwkv_a_up, rwkv_k_k, rwkv_k_a, rwkv_r_k,
            rwkv_ln_w, rwkv_ln_b, rwkv_v0, rwkv_v_down, rwkv_v_up, gmlp_ln_w, gmlp_ln_b, gmlp_w_s, gmlp_b_s, mla_q_norm, mla_w_uq,
            mla_kv_norm, mla_w_ukv, w_branch, w_out):
    z = lambda *shape: np.zeros(shape, np.float32)
    par, wt, up, wgv, gln, ws, bs, whead, wv, wb = ([] for _ in range(10))
    for l in range(L):
        v0 = rwkv_v0[l - 1] if l else z(BW)
        v_down = rwkv_v_down[l - 1] if l else z(D, V_LORA)
        v_up = rwkv_v_up[l - 1] if l else z(V_LORA, BW)
        par.append(np.concatenate([columns(a) for a in (
            pre_norm[l], post_norm[l], np.concatenate([rwkv_mu[l], z(P)]), rwkv_w0[l], rwkv_a0[l], rwkv_k_k[l], rwkv_k_a[l],
            rwkv_r_k[l].reshape(-1), rwkv_ln_w[l], rwkv_ln_b[l], v0, mla_q_norm[l], mla_kv_norm[l],
            np.full(P, 1.0 if l else 0.0, np.float32))], 1))
        w = w_in[l]
        kr = w[:, O_KR:O_KR + ROPE]
        half = ROPE // 2
        swap = lambda a: np.concatenate([a[:, half:], a[:, :half]], 1)
        wide = np.concatenate([w[:, :O_RWG], v_down, z(D, P - V_LORA), w[:, O_GU:O_GV], w[:, O_CKV:O_KR], kr, swap(kr), kr, swap(kr), w[:, O_CQ:O_CKV],
                               w[:, O_RWG:O_GU], w[:, O_GG:O_CQ], w[:, O_MG:O_MERGE]], 1)
        wt.append(tiles(wide))
        u = z(NP, P, 3, P)
        for j in range(NP):
            cols = slice(j * P, (j + 1) * P)
            u[j, :64, 0], u[j, 64:, 1], u[j, :V_LORA, 2] = rwkv_w_up[l][:, cols], rwkv_a_up[l][:, cols], v_up[:, cols]
        up.append(u)
        wgv.append(w[:, O_GV:O_GG].reshape(KD, P, BW).transpose(1, 0, 2))
        gln.append(np.broadcast_to(np.stack([gmlp_ln_w[l], gmlp_ln_b[l]])[None], (P, 2, BW)))
        ws.append(gmlp_w_s[l].transpose(2, 0, 1))
        bs.append(np.repeat(gmlp_b_s[l], HD, axis=0).reshape(NP, P, CH).transpose(1, 0, 2))
        uq = mla_w_uq[l].reshape(Q_LORA, NH, QK)
        ukv = mla_w_ukv[l].reshape(KV_LORA, NH, NOPE + HD)
        for h in range(NH):
            parts = [uq[:, h, :NOPE], uq[:, h, NOPE:], swap(uq[:, h, NOPE:])]
            one = np.concatenate(parts[1:] + parts[:1] if h % 2 else parts, 1)
            pair = np.concatenate([ukv[:, 2 * (h // 2) + n, :NOPE] for n in range(2)], 1)
            whead.append(np.concatenate([one.reshape(3, P, P).transpose(1, 0, 2).reshape(P, -1), pair.reshape(2, P, P)[h % 2]], 1))
        wv.append(ukv[:, :, NOPE:].reshape(KV_LORA, BW).reshape(2, P, BW).transpose(1, 0, 2))
        wt += [tiles(w[:, O_MERGE:]), tiles(w_out[l])]
        wb += [tiles(w_branch[l, n]) for n in range(NBR)]
    cat = lambda a: np.ascontiguousarray(np.concatenate(a, 0))
    stack = lambda a: np.ascontiguousarray(np.stack(a, 0))
    return {
        "x": np.ascontiguousarray(x[0].T.reshape(KD, P, T).transpose(1, 0, 2)), "pos": np.ascontiguousarray(positions.reshape(1, T)),
        "con": constants(), "par": stack(par), "wt": cat(wt), "up": cat(up), "wgv": stack(wgv), "gln": stack(gln), "ws": stack(ws),
        "bs": stack(bs), "whead": stack(whead), "wv": stack(wv), "wb": cat(wb),
    }


def kernel(**inputs):
    import concourse.bacc as _bacc
    from concourse.bass_utils import run_bass_kernel_spmd as _run

    arrays = lay_out(**{k: np.asarray(v) for k, v in inputs.items()})
    nc = _bacc.Bacc("TRN2", target_bir_lowering=False, num_devices=1)
    args = {f"d_{k}": nc.dram_tensor(f"in_{k}", a.shape, mybir.dt.from_np(a.dtype), kind="ExternalInput").ap() for k, a in arrays.items()}
    out = nc.dram_tensor("out_x", (P, KD, T), F32, kind="ExternalOutput").ap()
    build(nc, d_out=out, **args)
    r = _run(nc, [{f"in_{k}": a for k, a in arrays.items()}], core_ids=[0])
    got = r.results[0]["out_x"]
    return np.ascontiguousarray(got.transpose(1, 0, 2).reshape(D, T).T)[None]
```
